# Optimizing a Trainium2 kernel written in Bass

```python
import jax, jax.numpy as jnp
from jax import lax
import numpy as np

D_MODEL = 1024
BATCH = 1
SEQ = 256
DEPTH = 2
DEC_BATCH = 1
DEC_SEQ = 32
PAST_LEN = 512

CHUNK = 64

N_A_LAYERS = DEPTH // 2
N_B_LAYERS = DEPTH - N_A_LAYERS
N_DENSE = (DEPTH + 1) // 2
N_MOE = DEPTH // 2

POOL_WINDOWS = (2, 4, 8, 16)
N_POOL_GROUPS = len(POOL_WINDOWS)
POOL_GROUP = D_MODEL // N_POOL_GROUPS
POOL_HIST = max(POOL_WINDOWS) - 1

N_HEADS = 16
HEAD_DIM = D_MODEL // N_HEADS
KV_WIDTH = N_HEADS * HEAD_DIM
Q_BLOCK = 128

D_FF = ((8 * D_MODEL // 3 + 127) // 128) * 128
N_EXPERTS = 8
TOP_K = 2
EPS = 1e-6

kernel_name = "yoco_pool_fox_moe_stream_step"

def rms_norm(x, g):
    xf = x.astype(jnp.float32)
    y = xf * lax.rsqrt(jnp.mean(xf * xf, axis=-1, keepdims=True) + EPS)
    return (y * g.astype(jnp.float32)).astype(x.dtype)

def pool_mixer(u, hist, start_pos, w_pool, pool_scale):
    b, n, d = u.shape
    full = jnp.concatenate([hist.astype(u.dtype), u], axis=1)
    full_f = full.astype(jnp.float32)
    csum = jnp.concatenate([jnp.zeros((b, 1, d), jnp.float32), jnp.cumsum(full_f, axis=1)], axis=1)
    end = csum[:, POOL_HIST + 1:]
    n_avail = start_pos + jnp.arange(n, dtype=jnp.int32) + 1
    groups = []
    for g, w in enumerate(POOL_WINDOWS):
        lo, hi = g * POOL_GROUP, (g + 1) * POOL_GROUP
        s0 = POOL_HIST + 1 - w
        win_sum = end[:, :, lo:hi] - csum[:, s0:s0 + n, lo:hi]
        cnt = jnp.minimum(n_avail, w).astype(jnp.float32)[None, :, None]
        groups.append(win_sum / cnt)
    pooled = jnp.stack(groups, axis=2)
    diff = pooled - full_f[:, POOL_HIST:].reshape(b, n, N_POOL_GROUPS, POOL_GROUP)
    y = jnp.einsum('bngc,gce->bnge', diff.astype(u.dtype), w_pool).reshape(b, n, d)
    return y * pool_scale, full[:, -POOL_HIST:]

def swiglu(x, w_gu, w_down):
    gate, up = jnp.split(x @ w_gu, 2, axis=-1)
    return (jax.nn.silu(gate) * up) @ w_down

def moe_swiglu(x, w_router, w_gu, w_down):
    logits = (x @ w_router).astype(jnp.float32)
    top_v, top_i = lax.top_k(logits, TOP_K)
    top_w = jax.nn.softmax(top_v, axis=-1)
    gates = jnp.sum(jax.nn.one_hot(top_i, N_EXPERTS, dtype=jnp.float32) * top_w[..., None], axis=-2)
    out = jnp.zeros(x.shape, jnp.float32)
    for e in range(N_EXPERTS):
        out = out + gates[..., e:e + 1] * swiglu(x, w_gu[e], w_down[e]).astype(jnp.float32)
    return out.astype(x.dtype)

def shared_kv(h, g_kv, w_kvf, b_f, g_k):
    b, n, _ = h.shape
    proj = rms_norm(h, g_kv) @ w_kvf
    k = rms_norm(proj[..., :KV_WIDTH].reshape(b, n, N_HEADS, HEAD_DIM), g_k)
    v = proj[..., KV_WIDTH:2 * KV_WIDTH].reshape(b, n, N_HEADS, HEAD_DIM)
    logf = jax.nn.log_sigmoid((proj[..., 2 * KV_WIDTH:] + b_f).astype(jnp.float32))
    return k, v, logf

def fox_attend(q, c_q, q_pos, k, v, c_k, k_pos):
    s = jnp.einsum('bqhd,bkhd->bhqk', q, k).astype(jnp.float32) * (HEAD_DIM ** -0.5)
    s = s + jnp.transpose(c_q, (0, 2, 1))[:, :, :, None] - jnp.transpose(c_k, (0, 2, 1))[:, :, None, :]
    s = jnp.where((k_pos[None, :] <= q_pos[:, None])[None, None], s, -jnp.inf)
    p = jax.nn.softmax(s, axis=-1).astype(v.dtype)
    return jnp.einsum('bhqk,bkhd->bqhd', p, v)

def fox_prompt(q, k, v, logf):
    b, s = q.shape[:2]
    c = jnp.cumsum(logf.astype(jnp.float32), axis=1)
    nb = s // Q_BLOCK
    pos = jnp.arange(s, dtype=jnp.int32)
    qb = jnp.moveaxis(q.reshape(b, nb, Q_BLOCK, N_HEADS, HEAD_DIM), 1, 0)
    cb = jnp.moveaxis(c.reshape(b, nb, Q_BLOCK, N_HEADS), 1, 0)
    pb = pos.reshape(nb, Q_BLOCK)
    out = lax.map(lambda a: fox_attend(a[0], a[1], a[2], k, v, c, pos), (qb, cb, pb))
    return jnp.moveaxis(out, 0, 1).reshape(b, s, KV_WIDTH)

def fox_sample(q, k_new, v_new, logf_new, cache_k, cache_v, cache_logf):
    b, n = q.shape[:2]
    p_len = cache_k.shape[1]
    k = jnp.concatenate([cache_k.astype(k_new.dtype), k_new], axis=1)
    v = jnp.concatenate([cache_v.astype(v_new.dtype), v_new], axis=1)
    c = jnp.cumsum(jnp.concatenate([cache_logf.astype(jnp.float32), logf_new], axis=1), axis=1)
    k_pos = jnp.arange(p_len + n, dtype=jnp.int32)
    q_pos = p_len + jnp.arange(n, dtype=jnp.int32)
    return fox_attend(q, c[:, p_len:], q_pos, k, v, c, k_pos).reshape(b, n, KV_WIDTH)

def run_trunk(x, pool_hist, kv_cache, params):
    (g_pool_norm, w_pool, pool_scale, g_kv_norm, w_kvf, b_f, g_k, g_attn_norm, w_q, g_q, w_o,
     g_ffn_norm, w_ffn_gu, w_ffn_down, w_router, w_moe_gu, w_moe_down) = params
    b, n, _ = x.shape
    start_pos = 0 if kv_cache is None else kv_cache[0].shape[1]
    h = x
    pool_states = []
    k = v = logf = None
    for layer in range(DEPTH):
        if layer < N_A_LAYERS:
            hist = jnp.zeros((b, POOL_HIST, D_MODEL), x.dtype) if pool_hist is None else pool_hist[layer]
            y, st = pool_mixer(rms_norm(h, g_pool_norm[layer]), hist, start_pos, w_pool[layer], pool_scale[layer])
            pool_states.append(st)
            h = h + y
        else:
            if layer == N_A_LAYERS:
                k, v, logf = shared_kv(h, g_kv_norm, w_kvf, b_f, g_k)
            i = layer - N_A_LAYERS
            q = rms_norm((rms_norm(h, g_attn_norm[i]) @ w_q[i]).reshape(b, n, N_HEADS, HEAD_DIM), g_q[i])
            if kv_cache is None:
                o = fox_prompt(q, k, v, logf)
            else:
                o = fox_sample(q, k, v, logf, *kv_cache)
            h = h + o @ w_o[i]
        u = rms_norm(h, g_ffn_norm[layer])
        if layer % 2 == 0:
            h = h + swiglu(u, w_ffn_gu[layer // 2], w_ffn_down[layer // 2])
        else:
            h = h + moe_swiglu(u, w_router[layer // 2], w_moe_gu[layer // 2], w_moe_down[layer // 2])
    return h, jnp.stack(pool_states, axis=0), k, v, logf

def setup_inputs(seed: int = 0) -> dict:
    key = jax.random.key(seed)
    ks = jax.random.split(key, 24)

    def nrm(i, shape, scale):
        return jax.random.normal(ks[i], shape, jnp.float32) * scale

    def gain(i, shape):
        return 1.0 + 0.05 * jax.random.normal(ks[i], shape, jnp.float32)

    d, f = D_MODEL, D_FF
    return {
        "x_prompt": nrm(0, (BATCH, SEQ, d), 1.0),
        "x_sample": nrm(1, (DEC_BATCH, DEC_SEQ, d), 1.0),
        "state_pool": nrm(2, (N_A_LAYERS, DEC_BATCH, POOL_HIST, d), 1.0),
        "cache_k": nrm(3, (DEC_BATCH, PAST_LEN, N_HEADS, HEAD_DIM), 1.0),
        "cache_v": nrm(4, (DEC_BATCH, PAST_LEN, N_HEADS, HEAD_DIM), 1.0),
        "cache_logf": jax.nn.log_sigmoid(3.5 + 1.5 * jax.random.normal(ks[5], (DEC_BATCH, PAST_LEN, N_HEADS), jnp.float32)),
        "g_pool_norm": gain(6, (N_A_LAYERS, d)),
        "w_pool": nrm(7, (N_A_LAYERS, N_POOL_GROUPS, POOL_GROUP, POOL_GROUP), POOL_GROUP ** -0.5),
        "pool_scale": gain(8, (N_A_LAYERS, d)),
        "g_kv_norm": gain(9, (d,)),
        "w_kvf": nrm(10, (d, 2 * KV_WIDTH + N_HEADS), d ** -0.5),
        "b_f": jax.random.uniform(ks[11], (N_HEADS,), dtype=jnp.float32, minval=1.0, maxval=6.0),
        "g_k": gain(12, (HEAD_DIM,)),
        "g_attn_norm": gain(13, (N_B_LAYERS, d)),
        "w_q": nrm(14, (N_B_LAYERS, d, KV_WIDTH), d ** -0.5),
        "g_q": gain(15, (N_B_LAYERS, HEAD_DIM)),
        "w_o": nrm(16, (N_B_LAYERS, KV_WIDTH, d), KV_WIDTH ** -0.5),
        "g_ffn_norm": gain(17, (DEPTH, d)),
        "w_ffn_gu": nrm(18, (N_DENSE, d, 2 * f), d ** -0.5),
        "w_ffn_down": nrm(19, (N_DENSE, f, d), f ** -0.5),
        "w_router": nrm(20, (N_MOE, d, N_EXPERTS), d ** -0.5),
        "w_moe_gu": nrm(21, (N_MOE, N_EXPERTS, d, 2 * f), d ** -0.5),
        "w_moe_down": nrm(22, (N_MOE, N_EXPERTS, f, d), f ** -0.5),
    }

def reference(x_prompt, x_sample, state_pool, cache_k, cache_v, cache_logf,
              g_pool_norm, w_pool, pool_scale, g_kv_norm, w_kvf, b_f, g_k,
              g_attn_norm, w_q, g_q, w_o, g_ffn_norm, w_ffn_gu, w_ffn_down,
              w_router, w_moe_gu, w_moe_down):
    params = (g_pool_norm, w_pool, pool_scale, g_kv_norm, w_kvf, b_f, g_k, g_attn_norm, w_q, g_q, w_o,
              g_ffn_norm, w_ffn_gu, w_ffn_down, w_router, w_moe_gu, w_moe_down)
    y_prompt, pool_prompt, k_prompt, v_prompt, logf_prompt = run_trunk(x_prompt, None, None, params)
    y_sample, pool_sample, k_sample, v_sample, logf_sample = run_trunk(
        x_sample, state_pool, (cache_k, cache_v, cache_logf), params)
    return (y_prompt, y_sample, pool_prompt, k_prompt, v_prompt, logf_prompt,
            pool_sample, k_sample, v_sample, logf_sample)


_drawn_inputs = setup_inputs


def setup_inputs(seed=0):
    import zlib

    import numpy as np

    out = dict(_drawn_inputs(seed))
    spreads = {}
    factors = {'g_attn_norm': 3.05, 'g_q': 3.452}
    for name, (base, spread) in spreads.items():
        noise = np.random.default_rng([zlib.crc32(name.encode()), seed]).standard_normal(out[name].shape)
        drawn = base * np.exp(spread * noise) if base else spread * noise
        out[name] = __import__('jax').numpy.asarray(drawn.astype(out[name].dtype))
    for name, factor in factors.items():
        out[name] = (out[name] * factor).astype(out[name].dtype)
    return out
```

```python
import concourse.bass as bass
from concourse import mybir
from contextlib import ExitStack

D = 1024
FF = 2816
NP, NS = 256, 32
TOK = NP + NS
PAST = 512
HIST = 15
H, HD = 16, 64
NE = 8
CAP = 96
PASSES = -(-TOK // CAP)
KC = D // 128
FC = FF // 128
BLK = FC // 2
EPS = 1e-6
NEG = -1.0e30

SLOTS = 6
SLOT = 6144
U_POOL = 0
U_GU = 1
U_DN = U_GU + BLK
U_Q = U_DN + 4
U_KV = U_Q + 2
U_KC = U_KV + 4
U_VC = U_KC + 1
U_O = U_VC + 1
U_MOE = U_O + 2
EXP_SLOT = [(U_MOE + u) % SLOTS for u in range(BLK)]


def earlier_user(u):
    same = [v for v in range(-BLK, u) if EXP_SLOT[v % BLK] == EXP_SLOT[u]]
    return same[-1]


def build_program(nc, ins, outs):
    F32, I32 = mybir.dt.float32, mybir.dt.int32
    ALU, ACT, AX = mybir.AluOpType, mybir.ActivationFunctionType, mybir.AxisListType
    ctx = ExitStack()
    with ctx:
        def sb(name, shape, dt=F32):
            return ctx.enter_context(nc.sbuf_tensor(name, shape, dt))

        sems = {}

        def S(name):
            if name not in sems:
                sems[name] = ctx.enter_context(nc.semaphore(name))
            return sems[name]

        ring = sb("ring", [128, SLOTS, SLOT])
        hT = sb("hT", [128, KC, TOK])
        regB = sb("regB", [128, KC * TOK])
        regC = sb("regC", [128, KC * TOK])
        regD = sb("regD", [128, 3 * D])
        regE = sb("regE", [128, H * TOK])
        ident = sb("ident", [128, 128])
        ones = sb("ones", [128, 128])
        headones = sb("headones", [128, 128])
        causal = sb("causal", [128, 128])
        causal_s = sb("causal_s", [128, NS])
        before = sb("before", [128, 128])
        slots_iota = sb("slots_iota", [128, CAP])
        sels = sb("sels", [128, H, NS])
        g_pool = sb("g_pool", [128, KC]); p_scale = sb("p_scale", [128, KC]); g_kv = sb("g_kv", [128, KC])
        g_attn = sb("g_attn", [128, KC]); g_ffn = sb("g_ffn", [128, 2, KC])
        gk = sb("gk", [128, 1]); gq = sb("gq", [128, 1]); gq8 = sb("gq8", [128, 1]); bf = sb("bf", [H, 1])
        eps = sb("eps", [128, 1]); one = sb("one", [128, 1])
        counts = sb("counts", [128, 16]); inv_cnt = sb("inv_cnt", [128, 16])
        wf = sb("wf", [128, KC, H]); wr = sb("wr", [128, KC, NE])
        rms = sb("rms", [128, 2, TOK]); rstd = sb("rstd", [128, 2, TOK])
        QS = sb("QS", [128, KC, 128])
        negs = sb("negs", [128, PAST + NS]); negp = sb("negp", [128, NP])
        stat = sb("stat", [128, 64])
        lt = sb("lt", [128, 4, H])
        lo = sb("lo", [128, 3, H])

        DE = lambda off, n: (regD[:, off:off + n] if off + n <= 3 * D else regE[:, off - 3 * D:off - 3 * D + n])
        xtok = regD[:, :].rearrange("p (t n) -> p t n", t=3)
        UW = NP + NS + 2 * HIST
        U = regE[:, 0:KC * UW].rearrange("p (c n) -> p c n", c=KC)
        winA = regD[:, 0:KC * UW].rearrange("p (c n) -> p c n", c=KC)
        winB = regC[:, 0:6 * UW].rearrange("p (c n) -> p c n", c=6)
        diff = regB[:, :].rearrange("p (c n) -> p c n", c=KC)
        u = regB[:, :].rearrange("p (c n) -> p c n", c=KC)
        sq = regC[:, :].rearrange("p (c n) -> p c n", c=KC)
        hmA = regD[:, 0:10 * TOK].rearrange("p (c n) -> p c n", c=10)
        hmB = regE[:, 0:12 * TOK].rearrange("p (c n) -> p c n", c=12)
        uq = regD[:, 0:KC * TOK].rearrange("p (c n) -> p c n", c=KC)
        kT = regC[:, :].rearrange("p (c n) -> p c n", c=KC)
        vtok = regD[:, :].rearrange("p (t n) -> p t n", t=3)
        qz = regE[:, :].rearrange("p (h n) -> p h n", h=H)
        oT = regB[:, :].rearrange("p (c n) -> p c n", c=KC)
        htok = regD[:, :].rearrange("p (t n) -> p t n", t=3)
        acc = regE[:, 0:3 * D].rearrange("p (t n) -> p t n", t=3)
        kout = [regB[:, 0:D], regB[:, D:2 * D], regE[:, 3 * D:4 * D]]
        tail4, tail5 = ring[:, 4, 4096:SLOT], ring[:, 5, 4096:SLOT]
        st_out = tail4[0:HIST, 0:2 * D].rearrange("p (s n) -> p s n", s=2)
        Pp = tail4[:, 0:3 * NP].rearrange("p (i n) -> p i n", i=3)
        PTp = tail4[:, 3 * NP:5 * NP].rearrange("p (i n) -> p i n", i=2)
        sg = tail5[:, 0:2 * TOK].rearrange("p (i n) -> p i n", i=2)
        raw = tail5[:, 0:2 * TOK].rearrange("p (i n) -> p i n", i=2)
        sqh = tail5[:, 2 * TOK:4 * TOK].rearrange("p (i n) -> p i n", i=2)
        zf, lf = tail5[0:H, 4 * TOK:5 * TOK], tail5[0:H, 5 * TOK:6 * TOK]
        af = tail5[0:H, 6 * TOK:7 * TOK]
        cat = tail4[0:H, 5 * NP:5 * NP + PAST + NS]
        Ps = [tail5[:, 0:640], tail5[:, 640:1280]]
        PTs = tail5[:, 1280:1920].rearrange("p (t n) -> p t n", t=5)
        kc = ring[:, U_KC % SLOTS, 0:4096].rearrange("p (t n) -> p t n", t=4)
        vc = ring[:, U_VC % SLOTS, 0:4096].rearrange("p (t n) -> p t n", t=4)
        xg = regB[:, 0:KC * CAP].rearrange("p (c n) -> p c n", c=KC)
        yT = regB[:, KC * CAP:2 * KC * CAP].rearrange("p (c n) -> p c n", c=KC)
        hm = regC[:, 0:6 * CAP].rearrange("p (i c n) -> p i c n", i=3, c=2)
        sl = regC[:, 6 * CAP:12 * CAP].rearrange("p (i c n) -> p i c n", i=3, c=2)
        ytok = regC[0:CAP, 12 * CAP:12 * CAP + D]
        hflat = hT[:, :, :].rearrange("p c n -> p (c n)")
        Dx = hflat[:, 0:3 * CAP].rearrange("p (t n) -> p t n", t=3)
        Dg = hflat[:, 3 * CAP:6 * CAP].rearrange("p (t n) -> p t n", t=3)
        DgT = hflat[0:CAP, 6 * CAP:6 * CAP + 3 * 128]
        qflat = QS[:, :, :].rearrange("p c n -> p (c n)")
        lg, m1, m2, key, l2 = (qflat[:, 24 * i:24 * i + 24].rearrange("p (t e) -> p t e", t=3) for i in range(5))
        tv = qflat[:, 120:144].rearrange("p (i t) -> p i t", i=8)
        rank = qflat[:, 144:171].rearrange("p (e t) -> p e t", t=3)
        gate = qflat[:, 171:198].rearrange("p (e t) -> p e t", t=3)
        cur = qflat[:, 198:204]
        wrg = qflat[:, 204:268].rearrange("p (k e) -> p k e", k=KC)
        desc = sb("desc", [128, 3, NE]); rs_tok = sb("rs_tok", [128, 3]); valid = sb("valid", [128, 3])
        most = sb("most", [128, 1]); most_i = sb("most_i", [128, 1], I32)

        P = [ctx.enter_context(nc.psum_tensor(f"P{i}", [128, 512], F32)) for i in range(8)]

        def slot(n):
            return ring[:, n % SLOTS, :]

        def through(n):
            return sum(32 if U_GU <= x < U_DN else 16 for x in range(n % SLOTS, n + 1, SLOTS))

        def arrived(eng, n):
            eng.wait_ge(S(f"arrived{n % SLOTS}"), through(n))

        def exp_arrived(eng, e, uu):
            s = EXP_SLOT[uu]
            base = through(max(n for n in range(U_MOE) if n % SLOTS == s))
            per = [v for v in range(BLK) if EXP_SLOT[v] == s]
            eng.wait_ge(S(f"arrived{s}"), e * (48 * len(per)) + (base + 48 * (per.index(uu) + 1)))

        def used(eng, n):
            if n == U_POOL:
                eng.wait_ge(S("pool_mm"), KC)
            elif n < U_DN:
                eng.wait_ge(S("ffn_gu"), 2 * (n - U_GU + 1))
            elif n < U_Q:
                eng.wait_ge(S("ffn_dn"), 2 * (n - U_DN + 1))
            elif n < U_KC:
                eng.wait_ge(S("proj_mm"), 4 * (n - U_Q + 1))
            elif n < U_O:
                eng.wait_ge(S("pvs_mm"), 4)
            else:
                eng.wait_ge(S("wo_mm"), 4 * (n - U_O + 1))

        exp_gu = [ring[:, s, 0:4096].rearrange("p (h k n) -> p h k n", h=2, k=KC) for s in range(SLOTS)]
        exp_dn = [ring[:, s, 4096:6144].rearrange("p (c n) -> p c n", c=2) for s in range(SLOTS)]

        E_GU, E_SILU, E_HM, E_D, E_AUXP, E_AUXA, E_AUXV, E_YT, E_DN = 1, 1, 3, 1, 1, 1, 3, 1, 3

        CONSTS = 26

        block = ctx.enter_context(nc.Block())

        @block.sync
        def _(sp):
            def load(n, dst, src, **kw):
                if n >= SLOTS:
                    used(sp, n - SLOTS)
                sp.dma_start(dst, src, **kw).then_inc(S(f"arrived{n % SLOTS}"), 16)

            sp.dma_start(xtok[:, 0:2, :], ins["x_prompt"][0].rearrange("(t p) n -> p t n", p=128))\
              .then_inc(S("x_in"), 16)
            sp.wait_ge(S("xtok_zero"), 1)
            sp.dma_start(xtok[0:NS, 2, :], ins["x_sample"][0]).then_inc(S("x_in"), 16)
            sp.dma_start(xtok[NS:NS + HIST, 2, :], ins["state_pool"][0, 0]).then_inc(S("x_in"), 16)
            load(U_POOL, slot(U_POOL)[:, 0:2048].rearrange("p (g k n) -> p (g k) n", g=4, k=2),
                 ins["w_pool"][0].rearrange("g (k p) n -> p (g k) n", p=128))
            for b in range(BLK):
                n = U_GU + b
                if n >= SLOTS:
                    used(sp, n - SLOTS)
                gu = ins["w_ffn_gu"][0].rearrange("(k p) (h n) -> h p k n", p=128, h=2)
                dst = slot(n)[:, 0:4096].rearrange("p (h k n) -> p h k n", h=2, k=KC)
                for half in range(2):
                    sp.dma_start(dst[:, half], gu[half, :, :, 256 * b:256 * b + 256])\
                      .then_inc(S(f"arrived{n % SLOTS}"), 16)
            for b in range(4):
                load(U_DN + b, slot(U_DN + b)[:, 0:FC * 256].rearrange("p (k n) -> p k n", k=FC),
                     ins["w_ffn_down"][0].rearrange("(k p) n -> p k n", p=128)[:, :, 256 * b:256 * b + 256])
            for n0, cnt, w in ((U_Q, 2, ins["w_q"][0]), (U_KV, 4, ins["w_kvf"]), (U_KC, 1, None), (U_VC, 1, None),
                               (U_O, 2, ins["w_o"][0])):
                for b in range(cnt):
                    n = n0 + b
                    if w is None:
                        c = ins["cache_k" if n == U_KC else "cache_v"][0].rearrange("(t p) h d -> p t (h d)", p=128)
                        load(n, slot(n)[:, 0:4096].rearrange("p (t n) -> p t n", t=4), c)
                    else:
                        load(n, slot(n)[:, 0:4096].rearrange("p (k n) -> p k n", k=KC),
                             w.rearrange("(k p) n -> p k n", p=128)[:, :, 512 * b:512 * b + 512])

            def load_expert(e, it):
                for uu in range(BLK):
                    if isinstance(it, int) and earlier_user(uu) < 0:
                        used(sp, U_MOE + uu - SLOTS)
                    else:
                        sp.wait_ge(S("e_dn"), it * BLK + (E_DN + earlier_user(uu) + 1))
                    s = EXP_SLOT[uu]
                    wgu = ins["w_moe_gu"][0, bass.ds(e, 1)].rearrange("e (k p) n -> p (e k) n", p=128)
                    wdn = ins["w_moe_down"][0, bass.ds(e, 1)].rearrange("e (k p) n -> p (e k) n", p=128)
                    sp.dma_start(exp_gu[s][:, 0], wgu[:, :, 256 * uu:256 * uu + 256]).then_inc(S(f"arrived{s}"), 16)
                    sp.dma_start(exp_gu[s][:, 1], wgu[:, :, FF + 256 * uu:FF + 256 * uu + 256])\
                      .then_inc(S(f"arrived{s}"), 16)
                    sp.dma_start(exp_dn[s], wdn[:, 2 * uu:2 * uu + 2, :]).then_inc(S(f"arrived{s}"), 16)

            load_expert(0, 0)
            with sp.Fori(1, NE) as e:
                load_expert(e, e)
            sp.wait_ge(S("most_ready"), 1)
            n = sp.value_load(most_i[0:1, 0:1], min_val=0, max_val=TOK)
            for p in range(1, PASSES):
                with sp.If(n > p * CAP):
                    with sp.Fori(0, NE) as e:
                        load_expert(e, e + p * NE)

        @block.gpsimd
        def _(pool):
            pool.memset(xtok[:, 2, :], 0.0).then_inc(S("xtok_zero"), 1)
            for dst, src in ((g_pool, ins["g_pool_norm"][0]), (p_scale, ins["pool_scale"][0]), (g_kv, ins["g_kv_norm"]),
                             (g_attn, ins["g_attn_norm"][0]), (g_ffn[:, 0], ins["g_ffn_norm"][0]),
                             (g_ffn[:, 1], ins["g_ffn_norm"][1])):
                with nc.allow_non_contiguous_dma(reason="a gain for each feature, 4 KB"):
                    pool.dma_start(dst[:, :], src.rearrange("(c p) -> p c", p=128)).then_inc(S("gains_in"), 16)
            for half in range(2):
                pool.dma_start(gk[64 * half:64 * half + 64, :], ins["g_k"].rearrange("(d a) -> d a", a=1))\
                    .then_inc(S("gains_in"), 16)
                pool.dma_start(gq[64 * half:64 * half + 64, :], ins["g_q"][0].rearrange("(d a) -> d a", a=1))\
                    .then_inc(S("gains_in"), 16)
            pool.dma_start(bf[:, :], ins["b_f"].rearrange("(d a) -> d a", a=1)).then_inc(S("gains_in"), 16)
            pool.dma_start(wf[:, :, :], ins["w_kvf"].rearrange("(k p) n -> p k n", p=128)[:, :, 2 * D:2 * D + H])\
                .then_inc(S("gains_in"), 16)
            pool.dma_start(wr[:, :, :], ins["w_router"][0].rearrange("(k p) n -> p k n", p=128))\
                .then_inc(S("gains_in"), 16)
            pool.dma_start(lt[:, :, :], ins["cache_logf"][0].rearrange("(t p) h -> p t h", p=128))\
                .then_inc(S("gains_in"), 16)
            made = 0

            def const(ins):
                nonlocal made
                made += 1
                ins.then_inc(S("const"), 1)
                pool.wait_ge(S("const"), made)

            const(pool.memset(ident[:, :], 0.0))
            const(pool.memset(causal[:, :], 0.0))
            const(pool.memset(causal_s[:, :], 0.0))
            const(pool.memset(before[:, :], 0.0))
            const(pool.memset(ones[:, :], 1.0))
            const(pool.memset(headones[:, :], 0.0))
            const(pool.iota(slots_iota[:, :], [[1, CAP]], base=0, channel_multiplier=0,
                            allow_small_or_imprecise_dtypes=True))
            const(pool.iota(counts[:, :], [[1, 16]], base=1, channel_multiplier=0,
                            allow_small_or_imprecise_dtypes=True))
            const(pool.iota(desc[:, :, :], [[0, 3], [-1, NE]], base=NE, channel_multiplier=0,
                            allow_small_or_imprecise_dtypes=True))
            const(pool.memset(eps[:, :], EPS))
            const(pool.memset(one[:, :], 1.0))
            const(pool.memset(valid[:, :], 1.0))
            const(pool.affine_select(out=ident[:, :], in_=ident[:, :], compare_op=ALU.not_equal, fill=1.0, base=0,
                                     pattern=[[-1, 128]], channel_multiplier=1))
            const(pool.affine_select(out=causal[:, :], in_=causal[:, :], compare_op=ALU.is_ge, fill=NEG, base=0,
                                     pattern=[[-1, 128]], channel_multiplier=1))
            const(pool.affine_select(out=before[:, :], in_=before[:, :], compare_op=ALU.is_ge, fill=1.0, base=0,
                                     pattern=[[-1, 128]], channel_multiplier=1))
            for q in range(4):
                const(pool.affine_select(out=causal_s[32 * q:32 * q + 32, :], in_=causal_s[32 * q:32 * q + 32, :],
                                         compare_op=ALU.is_ge, fill=NEG, base=0, pattern=[[-1, NS]],
                                         channel_multiplier=1))
            for q in range(2):
                const(pool.memset(headones[64 * q:64 * q + 64, 64 * q:64 * q + 64], 1.0))
            const(pool.memset(valid[32:64, 2:3], 0.0))
            const(pool.memset(valid[64:128, 2:3], 0.0))
            const(pool.memset(QS[:, :, :], 0.0))
            const(pool.memset(negs[:, :], 0.0))
            const(pool.memset(negp[:, :], 0.0))
            assert made == CONSTS
            pool.wait_ge(S("ffn_out"), KC)
            pool.memset(qz[0:64, 1:H:2, :], 0.0).then_inc(S("qz_zero"), 1)
            pool.memset(qz[64:128, 0:H:2, :], 0.0).then_inc(S("qz_zero"), 1)
            pool.wait_ge(S("state_out"), 4)
            pool.dma_start(outs["state_prompt"][0, 0], st_out[:, 0, :]).then_inc(S("stored"), 16)
            pool.dma_start(outs["state_sample"][0, 0], st_out[:, 1, :]).then_inc(S("stored"), 16)
            pool.wait_ge(S("stored"), 32)
            pool.wait_ge(S("proj_mm"), KC)
            pool.memset(vtok[:, 2, :], 0.0).then_inc(S("v_zero"), 1)
            pool.wait_ge(S("logf_tok"), 3)
            pool.dma_start(outs["logf_prompt"][0].rearrange("(t p) h -> p t h", p=128), lo[:, 0:2, :])\
                .then_inc(S("stored"), 16)
            pool.dma_start(outs["logf_sample"][0], lo[0:NS, 2, :]).then_inc(S("stored"), 16)
            pool.wait_ge(S("v_tok"), KC)
            pool.dma_start(outs["v_prompt"][0].rearrange("(t p) h d -> p t (h d)", p=128), vtok[:, 0:2, :])\
                .then_inc(S("v_stored"), 16)
            pool.dma_start(outs["v_sample"][0].rearrange("p h d -> p (h d)"), vtok[0:NS, 2, :])\
                .then_inc(S("v_stored"), 16)
            pool.wait_ge(S("v_stored"), 32)
            pool.wait_ge(S("wo_mm"), KC)
            pool.memset(htok[:, 2, :], 0.0).then_inc(S("htok_zero"), 1)
            pool.wait_ge(S("k_tok"), 6)
            for t in range(2):
                pool.dma_start(outs["k_prompt"][0, 128 * t:128 * t + 128].rearrange("p h d -> p (h d)"), kout[t])\
                    .then_inc(S("k_stored"), 16)
            pool.dma_start(outs["k_sample"][0].rearrange("p h d -> p (h d)"), kout[2][0:NS, :])\
                .then_inc(S("k_stored"), 16)
            pool.wait_ge(S("acc_done"), 1)
            pool.dma_start(outs["y_prompt"][0].rearrange("(t p) n -> p t n", p=128), acc[:, 0:2, :])\
                .then_inc(S("stored"), 16)
            pool.dma_start(outs["y_sample"][0], acc[0:NS, 2, :]).then_inc(S("stored"), 16)
            pool.wait_ge(S("stored"), 96)
            pool.wait_ge(S("k_stored"), 48)

        @block.tensor
        def _(pe):
            def mm(out, lhsT, rhs, start, stop, **kw):
                return pe.matmul(out, lhsT, rhs, start=start, stop=stop, **kw)

            pe.wait_ge(S("const"), CONSTS)
            pe.wait_ge(S("x_in"), 48)
            for c in range(KC):
                if c >= 4:
                    pe.wait_ge(S("xT"), c - 3)
                for t in range(3):
                    m = pe.transpose(P[c % 4][:, 128 * t:128 * t + 128], xtok[:, t, 128 * c:128 * c + 128], ident[:, :])
                m.then_inc(S("xT_mm"), 1)

            def sum_squares(bank, stage, c):
                pe.wait_ge(S(stage + "_sq"), c + 1)
                m = mm(P[bank][:, 0:TOK], ones[:, :], sq[:, c, :], c == 0, c == KC - 1)
                if c == KC - 1:
                    m.then_inc(S(stage + "_ss"), 1)

            for c in range(KC):
                sum_squares(4, "n0", c)

            arrived(pe, U_POOL)
            wp = slot(U_POOL)[:, 0:2048].rearrange("p (g k n) -> p (g k) n", g=4, k=2)
            for c in range(KC):
                g = c // 2
                pe.wait_ge(S("diff"), g + 1)
                if c >= 4:
                    pe.wait_ge(S("pooled"), c - 3)
                for k in range(2):
                    m = mm(P[c % 4][:, 0:TOK], wp[:, 2 * g + k, 128 * (c % 2):128 * (c % 2) + 128],
                           diff[:, 2 * g + k, :], k == 0, k == 1)
                m.then_inc(S("pool_mm"), 1)
            for s, at in ((0, HIST + NP - HIST), (1, HIST + NP + HIST + NS - HIST)):
                for half in range(2):
                    bank = [5, 6, 7, 4][2 * s + half]
                    for c in range(4):
                        m = pe.transpose(P[bank][0:HIST, 128 * c:128 * c + 128],
                                         U[:, 4 * half + c, at:at + HIST], ident[:, :])
                    m.then_inc(S("state_mm"), 1)

            for c in range(KC):
                if c == 0:
                    pe.wait_ge(S("pooled"), 5)
                sum_squares(0, "n1", c)

            pe.wait_ge(S("state_out"), 4)
            for b in range(BLK):
                n = U_GU + b
                arrived(pe, n)
                w = slot(n)[:, 0:4096].rearrange("p (h k n) -> p h k n", h=2, k=KC)
                for j in range(2):
                    f = 2 * b + j
                    if f >= 3:
                        pe.wait_ge(S("ffn_hm"), f - 2)
                    for half in range(2):
                        for k in range(KC):
                            if f == 0 and half == 0:
                                pe.wait_ge(S("u_ffn"), k + 1)
                            m = mm(P[1 + 2 * (f % 3) + half][:, 0:TOK], w[:, half, k, 128 * j:128 * j + 128],
                                   u[:, k, :], k == 0, k == KC - 1)
                    m.then_inc(S("ffn_gu"), 1)
            for b in range(4):
                n = U_DN + b
                arrived(pe, n)
                w = slot(n)[:, 0:FC * 256].rearrange("p (k n) -> p k n", k=FC)
                for j in range(2):
                    d = 2 * b + j
                    if d >= 2:
                        pe.wait_ge(S("ffn_out"), d - 1)
                    for f in range(FC):
                        if d == 0:
                            pe.wait_ge(S("ffn_hm"), f + 1)
                        src = hmA[:, f, :] if f < 10 else hmB[:, f - 10, :]
                        m = mm(P[7 if d % 2 == 0 else 0][:, 0:TOK], w[:, f, 128 * j:128 * j + 128], src,
                               f == 0, f == FC - 1)
                    m.then_inc(S("ffn_dn"), 1)
                    if d >= 1:
                        sum_squares(1, "n2", d - 1)
            sum_squares(1, "n2", KC - 1)

            def proj(i, w, col, act, first_wait):
                if i >= 2:
                    pe.wait_ge(S("raw"), i - 1)
                for k in range(KC):
                    if first_wait is not None:
                        pe.wait_ge(S(first_wait), k + 1)
                    m = mm(P[2 + i % 2][:, 0:TOK], w[:, k, col:col + 128], act[:, k, :], k == 0, k == KC - 1)
                m.then_inc(S("proj_mm"), 1)
                return m

            def head_sums(i):
                pe.wait_ge(S("head_sq"), i + 1)
                if i >= 2:
                    pe.wait_ge(S("head_rms"), i - 1)
                mm(P[4 + i % 2][:, 0:TOK], headones[:, :], sqh[:, i % 2, :], True, True).then_inc(S("head_ss"), 1)

            pe.wait_ge(S("gains_in"), 224)
            for t in range(4):
                m = pe.transpose(P[6][0:H, 128 * t:128 * t + 128], lt[:, t, :], ident[:, :])
            m.then_inc(S("cache_f"), 1)
            for i in range(2 * KC):
                n = (U_Q if i < KC else U_KV) + (i % KC) // 4
                if i % 4 == 0:
                    arrived(pe, n)
                w = slot(n)[:, 0:4096].rearrange("p (k n) -> p k n", k=KC)
                m = proj(i, w, 128 * (i % 4), uq if i < KC else u,
                         "u_q" if i == 0 else "u_kv" if i == KC else None)
                if i == KC:
                    for k in range(KC):
                        m = mm(P[7][0:H, 0:TOK], wf[:, k, :], u[:, k, :], k == 0, k == KC - 1)
                    m.then_inc(S("f_mm"), 1)
                if i >= 1:
                    head_sums(i - 1)

            def v_transposes(c):
                i = 2 * KC + c
                pe.wait_ge(S("raw"), i + 1)
                if c >= 2:
                    pe.wait_ge(S("v_tok"), c - 1)
                if c == 0:
                    pe.wait_ge(S("cat_ready"), 1)
                if c == 1:
                    pe.wait_ge(S("z_ready"), 1)
                for t in range(3):
                    r = 128 if t < 2 else NS
                    m = pe.transpose(P[6 + c % 2][0:r, 128 * t:128 * t + 128], raw[:, i % 2, 128 * t:128 * t + r], ident[:, :])
                m.then_inc(S("vt_mm"), 1)

            for c in range(KC):
                i = 2 * KC + c
                n = U_KV + 2 + c // 4
                if c % 4 == 0:
                    arrived(pe, n)
                w = slot(n)[:, 0:4096].rearrange("p (k n) -> p k n", k=KC)
                m = proj(i, w, 128 * (c % 4), u, None)
                if c == 0:
                    head_sums(2 * KC - 1)
                if c == 2:
                    pe.wait_ge(S("lf_ready"), 1)
                    for t in range(3):
                        r = 128 if t < 2 else NS
                        m = pe.transpose(P[1][0:r, H * t:H * t + H], lf[:, 128 * t:128 * t + r], ident[0:H, 0:H])
                    m.then_inc(S("lf_mm"), 1)
                if c >= 1:
                    v_transposes(c - 1)
            v_transposes(KC - 1)

            arrived(pe, U_KC)
            for j in range(8):
                if j >= 2:
                    pe.wait_ge(S("kc_out"), j - 1)
                if j == 1:
                    pe.wait_ge(S("logf_tok"), 3)
                for c in range(4):
                    m = pe.transpose(P[j % 2][:, 128 * c:128 * c + 128],
                                     kc[:, j // 2, 512 * (j % 2) + 128 * c:512 * (j % 2) + 128 * c + 128], ident[:, :])
                m.then_inc(S("kc_mm"), 1)

            def scores(n):
                h, qt = n // 2, n % 2
                nk = 128 * (qt + 1)
                if n == 0:
                    pe.wait_ge(S("k_ready"), KC)
                    pe.wait_ge(S("q_ready"), KC)
                    pe.wait_ge(S("neg_ready"), 2)
                    pe.wait_ge(S("kc_out"), 8)
                if n >= 3:
                    pe.wait_ge(S("p_exp"), n - 2)
                b = P[n % 3]
                mm(b[:, 0:nk], qz[:, h, 128 * qt:128 * qt + 128], kT[:, h // 2, 0:nk], True, False)
                mm(b[:, 0:nk], ident[:, h:h + 1].to_broadcast([128, 128]), negp[:, 0:nk], False, False)
                mm(b[:, nk - 128:nk], ident[:, :], causal[:, :], False, True).then_inc(S("s_mm"), 1)

            def probs_T(n):
                pe.wait_ge(S("p_norm"), n + 1)
                if n >= 2:
                    pe.wait_ge(S("pt_out"), n - 1)
                for t in range(n % 2 + 1):
                    m = pe.transpose(P[3 + n % 2][:, 128 * t:128 * t + 128], Pp[:, n % 3, 128 * t:128 * t + 128], ident[:, :])
                m.then_inc(S("pt_mm"), 1)

            def values(n):
                h, qt = n // 2, n % 2
                c = h // 2
                pe.wait_ge(S("pt_out"), n + 1)
                if n % 4 == 0 and c >= 2:
                    pe.wait_ge(S("o_out"), c - 1)
                at = NP * (h % 2) + 128 * qt
                for t in range(qt + 1):
                    m = mm(P[5 + c % 2][:, at:at + 128], vtok[:, t, 128 * c:128 * c + 128],
                           PTp[:, n % 2, 128 * t:128 * t + 128], t == 0, t == qt)
                m.then_inc(S("pv_mm"), 1)

            NA = 2 * H
            pe.wait_ge(S("v_tok"), KC)
            for n in range(NA + 3):
                if n < NA:
                    scores(n)
                if 2 <= n < NA + 2:
                    probs_T(n - 2)
                if n >= 3:
                    values(n - 3)

            arrived(pe, U_VC)
            SB = [(0, 1), (2, 7)]

            def s_scores(j):
                if j >= 2:
                    pe.wait_ge(S("ps_exp"), j - 1)
                if j == 0:
                    pe.wait_ge(S("p_exp"), NA)
                b0, b1 = P[SB[j % 2][0]], P[SB[j % 2][1]]
                for a in range(2):
                    c = 2 * j + a
                    mm(b0[:, :].rearrange("p (t n) -> p t n", t=4), QS[:, c, :], kc[:, :, 128 * c:128 * c + 128], a == 0, False)
                    mm(b1[:, 0:NS], QS[:, c, :], kT[:, c, NP:TOK], a == 0, False)
                sel = sels[:, 4 * j:4 * j + 4, :].rearrange("p h n -> p (h n)")
                mm(b0[:, :], sel, negs[:, 0:PAST], False, True)
                mm(b1[:, 0:NS], sel, negs[:, PAST:PAST + NS], False, False)
                mm(b1[:, 0:NS], ident[:, :], causal_s[:, :], False, True).then_inc(S("ss_mm"), 1)

            def s_values(j):
                pe.wait_ge(S("ps_norm"), j + 1)
                if j >= 1:
                    pe.wait_ge(S("pts_out"), j)
                for t in range(5):
                    m = pe.transpose(P[3 + t // 4][:, 128 * (t % 4):128 * (t % 4) + 128], Ps[j % 2][:, 128 * t:128 * t + 128], ident[:, :])
                m.then_inc(S("pts_mm"), 1)
                pe.wait_ge(S("pts_out"), j + 1)
                if j == 0:
                    pe.wait_ge(S("o_out"), KC)
                if j >= 1:
                    pe.wait_ge(S("os_out"), j)
                for a in range(2):
                    c = 2 * j + a
                    for t in range(5):
                        v = vc[:, t, 128 * c:128 * c + 128] if t < 4 else vtok[:, 2, 128 * c:128 * c + 128]
                        m = mm(P[5][:, 64 * a:64 * a + 64], v, PTs[:, t, 64 * a:64 * a + 64], t == 0, t == 4)
                m.then_inc(S("pvs_mm"), 1)
                return m

            for j in range(5):
                if j < 4:
                    s_scores(j)
                if j >= 1:
                    m = s_values(j - 1)

            for d in range(KC):
                n = U_O + d // 4
                if d % 4 == 0:
                    arrived(pe, n)
                w = slot(n)[:, 0:4096].rearrange("p (k n) -> p k n", k=KC)
                if d == 0:
                    pe.wait_ge(S("os_out"), 4)
                if d >= 2:
                    pe.wait_ge(S("h2"), d - 1)
                for k in range(KC):
                    m = mm(P[d % 2][:, 0:TOK], w[:, k, 128 * (d % 4):128 * (d % 4) + 128], oT[:, k, :], k == 0, k == KC - 1)
                m.then_inc(S("wo_mm"), 1)
            for j in range(6):
                t, half = j // 2, j % 2
                r = 128 if t < 2 else NS
                pe.wait_ge(S("h2"), KC)
                if j >= 2:
                    pe.wait_ge(S("h_tok"), j - 1)
                for c in range(4):
                    m = pe.transpose(P[2 + j % 2][0:r, 128 * c:128 * c + 128], hT[:, 4 * half + c, 128 * t:128 * t + r], ident[:, :])
                m.then_inc(S("ht_mm"), 1)
            pe.wait_ge(S("wrg_ready"), 1)
            for t in range(3):
                r = 128 if t < 2 else NS
                for k in range(KC):
                    m = mm(P[4][0:r, NE * t:NE * t + NE], hT[:, k, 128 * t:128 * t + r], wrg[:, k, :], k == 0, k == KC - 1)
            m.then_inc(S("lg_mm"), 1)
            for j in range(6):
                t, half = j // 2, j % 2
                r = 128 if t < 2 else NS
                if j >= 2:
                    pe.wait_ge(S("k_tok"), j - 1)
                for c in range(4):
                    m = pe.transpose(P[5 + j % 2][0:r, 128 * c:128 * c + 128], kT[:, 4 * half + c, 128 * t:128 * t + r], ident[:, :])
                m.then_inc(S("kt_mm"), 1)
            pe.wait_ge(S("mask_ready"), 1)
            for t in range(3):
                for s in range(t + 1):
                    mm(P[7][:, NE * t:NE * t + NE], before[:, :] if s == t else ones[:, :], key[:, s, :], s == 0, s == t)
            for s in range(3):
                m = mm(P[7][:, 32:32 + NE], ones[:, :], key[:, s, :], s == 0, s == 2)
            m.then_inc(S("rank_mm"), 1)

            def expert(it, p):

                def fill(i):
                    evac = {0: ("V", -2), 1: ("V", -1), 2: ("V", 0), 3: ("A", 1), 4: ("A", 2), 5: ("A", 3), 6: ("V", 1),
                            7: ("A", 4), 8: ("A", 5), 9: ("V", 2), 10: ("V", 3), 11: ("V", 4)}[i]
                    if evac[0] == "V":
                        pe.wait_ge(S("aux_dve"), it * 7 + (E_AUXV + evac[1]))
                    else:
                        pe.wait_ge(S("aux_act"), it * 5 + (E_AUXA + evac[1]))
                    return P[5 + i % 3]

                pe.wait_ge(S("dispatch"), it + (E_D + 1 + p))
                for i, cs in enumerate((range(0, 3), range(3, 6), range(6, 8))):
                    b = fill(i)
                    for j, c in enumerate(cs):
                        for t in range(3):
                            m = mm(b[:, CAP * j:CAP * j + CAP], htok[:, t, 128 * c:128 * c + 128], Dx[:, t, :], t == 0, t == 2)
                    m.then_inc(S("aux_pe"), 1)
                b = fill(3)
                for t in range(3):
                    m = pe.transpose(b[0:CAP, 128 * t:128 * t + 128], Dg[:, t, :], ident[:, :])
                m.then_inc(S("aux_pe"), 1)

                def down(uu):
                    pe.wait_ge(S("e_hm"), it * BLK + (E_HM + uu + 1))
                    if uu == 0:
                        pe.wait_ge(S("e_yT"), it * 2 + E_YT)
                    w = exp_dn[EXP_SLOT[uu]]
                    for f in range(2):
                        for d in range(KC):
                            last = uu == BLK - 1 and f == 1
                            m = mm(P[3 + d // 4][:, CAP * (d % 4):CAP * (d % 4) + CAP], w[:, f, 128 * d:128 * d + 128],
                                   hm[:, uu % 3, f, :], uu == 0 and f == 0 and d % 4 == 0, last and d % 4 == 3,
                                   skip_group_check=True)
                    m.then_inc(S("e_dn"), 1)

                for uu in range(BLK):
                    exp_arrived(pe, it, uu)
                    w = exp_gu[EXP_SLOT[uu]]
                    prev = uu - 3 if uu >= 3 else [9, 10, 8][uu] - BLK
                    pe.wait_ge(S("e_hm"), it * BLK + (E_HM + prev + 1))
                    for half in range(2):
                        for j in range(2):
                            for k in range(KC):
                                if uu == 0 and half == 0 and j == 0 and k in (0, 3, 6):
                                    pe.wait_ge(S("aux_act"), it * 5 + (E_AUXA + k // 3 + 1))
                                m = mm(P[uu % 3][:, CAP * (2 * half + j):CAP * (2 * half + j) + CAP],
                                       w[:, half, k, 128 * j:128 * j + 128], xg[:, k, :], k == 0, k == KC - 1)
                    m.then_inc(S("e_gu"), 1)
                    if uu >= 1:
                        down(uu - 1)
                down(BLK - 1)
                for i in (4, 5):
                    b = fill(i)
                    pe.wait_ge(S("e_yT"), it * 2 + (E_YT + i - 3))
                    for c in range(4):
                        m = pe.transpose(b[0:CAP, 128 * c:128 * c + 128], yT[:, 4 * (i - 4) + c, :], ident[:, :])
                    m.then_inc(S("aux_pe"), 1)
                for i in range(6, 12):
                    half, t = (i - 6) // 3, (i - 6) % 3
                    b = fill(i)
                    pe.wait_ge(S("aux_dve"), it * 7 + (E_AUXV + 1))
                    pe.wait_ge(S("aux_act"), it * 5 + (E_AUXA + 4 + half))
                    mm(b[:, :], DgT[:, 128 * t:128 * t + 128], ytok[:, 512 * half:512 * half + 512], True, True)\
                        .then_inc(S("aux_pe"), 1)

            with pe.Fori(0, NE) as e:
                expert(e, 0)
            pe.wait_ge(S("most_ready"), 1)
            n = pe.value_load(most_i[0:1, 0:1], min_val=0, max_val=TOK)
            for p in range(1, PASSES):
                with pe.If(n > p * CAP):
                    with pe.Fori(0, NE) as e:
                        expert(e + p * NE, p)

        @block.scalar
        def _(act):
            def squares(stage, src_sem):
                for c in range(KC):
                    act.wait_ge(S(src_sem), c + 1)
                    act.activation(sq[:, c, :], hT[:, c, :], ACT.Square).then_inc(S(stage + "_sq"), 1)

            def root(stage, bank, i):
                act.wait_ge(S(stage + "_ss"), 1)
                act.activation(rms[:, i, :], P[bank][:, 0:TOK], ACT.Sqrt, bias=eps[:, :], scale=1.0 / D)\
                    .then_inc(S(stage + "_rms"), 1)

            act.wait_ge(S("const"), CONSTS)
            squares("n0", "xT")
            root("n0", 4, 0)
            for s in range(2):
                for half in range(2):
                    act.wait_ge(S("state_mm"), 2 * s + half + 1)
                    act.activation(st_out[:, s, 512 * half:512 * half + 512], P[[5, 6, 7, 4][2 * s + half]][0:HIST, :],
                                   ACT.Copy).then_inc(S("state_out"), 1)
            squares("n1", "pooled")
            root("n1", 0, 1)
            for f in range(FC):
                act.wait_ge(S("ffn_gu"), f + 1)
                if f >= 2:
                    act.wait_ge(S("ffn_hm"), f - 1)
                act.activation(sg[:, f % 2, :], P[1 + 2 * (f % 3)][:, 0:TOK], ACT.Silu).then_inc(S("ffn_sg"), 1)
            squares("n2", "ffn_out")
            root("n2", 1, 0)
            act.wait_ge(S("cache_f"), 1)
            act.wait_ge(S("stored"), 32)
            act.activation(cat[:, 0:PAST], P[6][0:H, :], ACT.Copy).then_inc(S("cat_ready"), 1)

            def head_root(i):
                act.wait_ge(S("head_ss"), i + 1)
                if i >= 2:
                    act.wait_ge(S("head_rstd"), i - 1)
                act.activation(rms[:, i % 2, :], P[4 + i % 2][:, 0:TOK], ACT.Sqrt, bias=eps[:, :], scale=1.0 / HD)\
                    .then_inc(S("head_rms"), 1)

            act.wait_ge(S("n2_rstd"), 1)
            for i in range(2 * KC):
                act.wait_ge(S("raw"), i + 1)
                if i >= 2:
                    act.wait_ge(S("head_ss"), i - 1)
                act.activation(sqh[:, i % 2, :], raw[:, i % 2, :], ACT.Square).then_inc(S("head_sq"), 1)
                if i >= 1:
                    head_root(i - 1)
            head_root(2 * KC - 1)
            act.wait_ge(S("z_ready"), 2)
            act.activation(af, af, ACT.Exp, scale=-1.0).then_inc(S("f_exp"), 1)
            act.wait_ge(S("f_exp"), 1)
            act.activation(af, af, ACT.Ln, bias=one[0:H, :]).then_inc(S("f_ln"), 1)
            for j in range(8):
                act.wait_ge(S("kc_mm"), j + 1)
                act.activation(kc[:, j // 2, 512 * (j % 2):512 * (j % 2) + 512], P[j % 2][:, :], ACT.Copy)\
                    .then_inc(S("kc_out"), 1)
            for n in range(2 * H):
                act.wait_ge(S("p_max"), n + 1)
                if n >= 3:
                    act.wait_ge(S("pt_mm"), n - 2)
                nk = 128 * (n % 2 + 1)
                act.activation(Pp[:, n % 3, 0:nk], P[n % 3][:, 0:nk], ACT.Exp, bias=stat[:, n % 3:n % 3 + 1],
                               accum_out=stat[:, 4 + n % 3:5 + n % 3]).then_inc(S("p_exp"), 1)
            for j in range(4):
                act.wait_ge(S("ps_max"), j + 1)
                if j >= 2:
                    act.wait_ge(S("pts_mm"), j - 1)
                b0, b1 = [(0, 1), (2, 7)][j % 2]
                nm = stat[:, 16 + 8 * (j % 2):17 + 8 * (j % 2)]
                act.activation(Ps[j % 2][:, 0:PAST], P[b0][:, :], ACT.Exp, bias=nm,
                               accum_out=stat[:, 17 + 8 * (j % 2):18 + 8 * (j % 2)]).then_inc(S("ps_exp_a"), 1)
                act.activation(Ps[j % 2][:, PAST:PAST + NS], P[b1][:, 0:NS], ACT.Exp, bias=nm,
                               accum_out=stat[:, 18 + 8 * (j % 2):19 + 8 * (j % 2)]).then_inc(S("ps_exp"), 1)
            act.wait_ge(S("htok_zero"), 1)
            for j in range(6):
                t, half = j // 2, j % 2
                r = 128 if t < 2 else NS
                act.wait_ge(S("ht_mm"), j + 1)
                act.activation(htok[0:r, t, 512 * half:512 * half + 512], P[2 + j % 2][0:r, :], ACT.Copy)\
                    .then_inc(S("h_tok"), 1)
            act.wait_ge(S("h_tok"), 6)
            for t in range(3):
                act.activation(acc[:, t, :], htok[:, t, :], ACT.Square, accum_out=tv[:, 0, t:t + 1])\
                    .then_inc(S("row_ss"), 1)
            act.wait_ge(S("row_ss"), 3)
            act.activation(tv[:, 1, :], tv[:, 0, :], ACT.Sqrt, bias=eps[:, :], scale=1.0 / D).then_inc(S("row_rms"), 1)
            for t in range(3):
                act.activation(acc[:, t, :], htok[:, t, :], ACT.Copy).then_inc(S("acc_init"), 1)
            for j in range(6):
                t, half = j // 2, j % 2
                r = 128 if t < 2 else NS
                act.wait_ge(S("kt_mm"), j + 1)
                act.activation(kout[t][0:r, 512 * half:512 * half + 512], P[5 + j % 2][0:r, :], ACT.Copy)\
                    .then_inc(S("k_tok"), 1)
            act.wait_ge(S("top2"), 1)
            act.activation(tv[:, 4, :], tv[:, 3, :], ACT.Exp).then_inc(S("e2_ready"), 1)
            act.wait_ge(S("k_stored"), 48)

            def expert(it):
                for i, cs in enumerate((range(0, 3), range(3, 6), range(6, 8))):
                    act.wait_ge(S("aux_pe"), it * 12 + (E_AUXP + i + 1))
                    for j, c in enumerate(cs):
                        m = act.activation(xg[:, c, :], P[5 + i][:, CAP * j:CAP * j + CAP], ACT.Copy, scale=g_ffn[:, 1, c:c + 1])
                    m.then_inc(S("aux_act"), 1)
                for uu in range(BLK):
                    act.wait_ge(S("e_gu"), it * BLK + (E_GU + uu + 1))
                    if uu >= 3:
                        act.wait_ge(S("e_hm"), it * BLK + (E_HM + uu - 2))
                    else:
                        act.wait_ge(S("e_hm"), it * BLK + (E_HM + [-1, 0, -2][uu]))
                    act.activation(sl[:, uu % 3].rearrange("p c n -> p (c n)"), P[uu % 3][:, 0:2 * CAP], ACT.Silu)\
                        .then_inc(S("e_silu"), 1)
                act.wait_ge(S("e_dn"), it * BLK + (E_DN + BLK))
                for i in range(2):
                    act.activation(yT[:, 4 * i:4 * i + 4, :].rearrange("p c n -> p (c n)"), P[3 + i][:, 0:4 * CAP], ACT.Copy)\
                        .then_inc(S("e_yT"), 1)
                for i in range(2):
                    act.wait_ge(S("aux_pe"), it * 12 + (E_AUXP + 5 + i))
                    act.activation(ytok[:, 512 * i:512 * i + 512], P[5 + (4 + i) % 3][0:CAP, :], ACT.Copy)\
                        .then_inc(S("aux_act"), 1)

            with act.Fori(0, NE) as e:
                expert(e)
            act.wait_ge(S("most_ready"), 1)
            n = act.value_load(most_i[0:1, 0:1], min_val=0, max_val=TOK)
            for p in range(1, PASSES):
                with act.If(n > p * CAP):
                    with act.Fori(0, NE) as e:
                        expert(e + p * NE)

        @block.vector
        def _(dve):
            def then(ins, name):
                chain[name] = chain.get(name, 0) + 1
                ins.then_inc(S(name), 1)
                dve.wait_ge(S(name), chain[name])

            chain = {}
            dve.wait_ge(S("const"), CONSTS)
            then(dve.reciprocal(inv_cnt[:, :], counts[:, :]), "dve_setup")
            then(dve.tensor_copy(sels[:, :, :], ident[:, 0:H].unsqueeze(2).to_broadcast([128, H, NS])), "dve_setup")
            for name, v in (("e_gu", E_GU), ("e_silu", E_SILU), ("e_hm", E_HM), ("dispatch", E_D), ("aux_pe", E_AUXP),
                            ("aux_act", E_AUXA), ("aux_dve", E_AUXV), ("e_yT", E_YT), ("e_dn", E_DN)):
                dve.sem_inc(S(name), v)
            for c in range(KC):
                dve.wait_ge(S("xT_mm"), c + 1)
                dve.tensor_copy(hT[:, c, :], P[c % 4][:, 0:TOK]).then_inc(S("xT_a"), 1)
                dve.tensor_copy(U[:, c, HIST + NP:2 * HIST + NP], P[c % 4][:, TOK:TOK + HIST]).then_inc(S("xT"), 1)
            then(dve.memset(U[:, :, 0:HIST], 0.0), "dve_setup")

            def inverse(stage, i):
                dve.wait_ge(S(stage + "_rms"), 1)
                dve.reciprocal(rstd[:, i, :], rms[:, i, :]).then_inc(S(stage + "_rstd"), 1)
                dve.wait_ge(S(stage + "_rstd"), 1)

            dve.wait_ge(S("gains_in"), 224)
            then(dve.tensor_scalar(gq8[:, :], gq[:, :], HD ** -0.5, None, ALU.mult), "dve_setup")
            inverse("n0", 0)
            for c in range(KC):
                dve.scalar_tensor_tensor(U[:, c, HIST:HIST + NP], hT[:, c, 0:NP], g_pool[:, c:c + 1],
                                         rstd[:, 0, 0:NP], ALU.mult, ALU.mult).then_inc(S("U"), 1)
                dve.scalar_tensor_tensor(U[:, c, 2 * HIST + NP:UW], hT[:, c, NP:TOK], g_pool[:, c:c + 1],
                                         rstd[:, 0, NP:TOK], ALU.mult, ALU.mult).then_inc(S("U"), 1)
            dve.wait_ge(S("U"), 2 * KC)

            def differences(g, win, w):
                cs = slice(2 * g, 2 * g + 2)
                dve.scalar_tensor_tensor(diff[:, cs, 0:NP], win[:, :, HIST:HIST + NP], 1.0 / w, U[:, cs, HIST:HIST + NP],
                                         ALU.mult, ALU.subtract).then_inc(S("diff_a"), 1)
                dve.scalar_tensor_tensor(diff[:, cs, NP:TOK], win[:, :, 2 * HIST + NP:UW], 1.0 / w,
                                         U[:, cs, 2 * HIST + NP:UW], ALU.mult, ALU.subtract).then_inc(S("diff_a"), 1)
                dve.wait_ge(S("diff_a"), 3 * g + 2)
                dve.tensor_tensor(diff[:, cs, 0:w - 1], win[:, :, HIST:HIST + w - 1],
                                  inv_cnt[:, 0:w - 1].unsqueeze(1).to_broadcast([128, 2, w - 1]), ALU.mult)\
                    .then_inc(S("diff_a"), 1)
                dve.wait_ge(S("diff_a"), 3 * g + 3)
                dve.tensor_tensor(diff[:, cs, 0:w - 1], diff[:, cs, 0:w - 1], U[:, cs, HIST:HIST + w - 1],
                                  ALU.subtract).then_inc(S("diff"), 1)

            then(dve.tensor_tensor(winA[:, :, 1:UW], U[:, :, 1:UW], U[:, :, 0:UW - 1], ALU.add), "win")
            differences(0, winA[:, 0:2], 2)
            then(dve.tensor_tensor(winB[:, :, 3:UW], winA[:, 2:8, 3:UW], winA[:, 2:8, 1:UW - 2], ALU.add), "win")
            differences(1, winB[:, 0:2], 4)
            then(dve.tensor_tensor(winA[:, 4:8, 7:UW], winB[:, 2:6, 7:UW], winB[:, 2:6, 3:UW - 4], ALU.add), "win")
            differences(2, winA[:, 4:6], 8)
            then(dve.tensor_tensor(winB[:, 4:6, 15:UW], winA[:, 6:8, 15:UW], winA[:, 6:8, 7:UW - 8], ALU.add), "win")
            differences(3, winB[:, 4:6], 16)
            for c in range(KC):
                dve.wait_ge(S("pool_mm"), c + 1)
                dve.scalar_tensor_tensor(hT[:, c, :], P[c % 4][:, 0:TOK], p_scale[:, c:c + 1], hT[:, c, :],
                                         ALU.mult, ALU.add).then_inc(S("pooled"), 1)
            dve.wait_ge(S("pooled"), KC)

            def normed(dst, g, i, name):
                for c in range(KC):
                    dve.scalar_tensor_tensor(dst[:, c, :], hT[:, c, :], g[:, c:c + 1], rstd[:, i, :],
                                             ALU.mult, ALU.mult).then_inc(S(name), 1)

            inverse("n1", 1)
            normed(u, g_ffn[:, 0], 1, "u_ffn")
            dve.wait_ge(S("state_mm"), 4)
            for f in range(FC):
                dve.wait_ge(S("ffn_sg"), f + 1)
                dst = hmA[:, f, :] if f < 10 else hmB[:, f - 10, :]
                dve.tensor_tensor(dst, sg[:, f % 2, :], P[2 + 2 * (f % 3)][:, 0:TOK], ALU.mult).then_inc(S("ffn_hm"), 1)
            for d in range(KC):
                dve.wait_ge(S("ffn_dn"), d + 1)
                dve.tensor_tensor(hT[:, d, :], hT[:, d, :], P[7 if d % 2 == 0 else 0][:, 0:TOK], ALU.add)\
                    .then_inc(S("ffn_out"), 1)
            dve.wait_ge(S("ffn_out"), KC)
            inverse("n2", 0)
            normed(uq, g_attn, 0, "u_q")
            normed(u, g_kv, 0, "u_kv")
            dve.wait_ge(S("u_kv"), KC)
            dve.wait_ge(S("qz_zero"), 2)

            def head_norm(i):
                c = i % KC
                dve.wait_ge(S("head_rms"), i + 1)
                dve.reciprocal(rstd[:, i % 2, :], rms[:, i % 2, :]).then_inc(S("head_rstd"), 1)
                dve.wait_ge(S("head_rstd"), i + 1)
                r = raw[:, i % 2, :]
                if i < KC:
                    for a in range(2):
                        ps = slice(64 * a, 64 * a + 64)
                        q4 = 32 * (2 * (c % 2) + a)
                        dve.scalar_tensor_tensor(qz[ps, 2 * c + a, :], r[ps, :], gq8[ps, :], rstd[ps, i % 2, :],
                                                 ALU.mult, ALU.mult).then_inc(S("q_a"), 1)
                        m = dve.scalar_tensor_tensor(QS[ps, c, q4:q4 + NS], r[ps, NP:TOK], gq8[ps, :],
                                                     rstd[ps, i % 2, NP:TOK], ALU.mult, ALU.mult)
                    m.then_inc(S("q_ready"), 1)
                    dve.wait_ge(S("q_ready"), c + 1)
                else:
                    dve.scalar_tensor_tensor(kT[:, c, :], r, gk[:, :], rstd[:, i % 2, :], ALU.mult, ALU.mult)\
                        .then_inc(S("k_ready"), 1)
                    dve.wait_ge(S("k_ready"), c + 1)

            def v_rows(c):
                dve.wait_ge(S("vt_mm"), c + 1)
                b = P[6 + c % 2]
                dve.tensor_copy(vtok[:, 0:2, 128 * c:128 * c + 128], b[:, 0:256].rearrange("p (t n) -> p t n", t=2))
                dve.tensor_copy(vtok[0:NS, 2, 128 * c:128 * c + 128], b[0:NS, 256:384]).then_inc(S("v_tok"), 1)

            for i in range(3 * KC):
                dve.wait_ge(S("proj_mm"), i + 1)
                if i >= 2 * KC + 2:
                    dve.wait_ge(S("vt_mm"), i - 2 * KC - 1)
                elif i >= 2:
                    dve.wait_ge(S("head_sq"), i - 1)
                dve.tensor_copy(raw[:, i % 2, :], P[2 + i % 2][:, 0:TOK]).then_inc(S("raw"), 1)
                if 1 <= i <= 2 * KC:
                    dve.wait_ge(S("raw"), i)
                    head_norm(i - 1)
                if i == KC:
                    dve.wait_ge(S("f_mm"), 1)
                    dve.tensor_scalar(zf, P[7][0:H, 0:TOK], bf[:, :], None, ALU.add).then_inc(S("z_ready"), 1)
                    dve.wait_ge(S("z_ready"), 1)
                    dve.scalar_tensor_tensor(af, zf, -1.0, zf, ALU.mult, ALU.max).then_inc(S("z_ready"), 1)
                if i == 2 * KC + 1:
                    dve.wait_ge(S("f_ln"), 1)
                    dve.scalar_tensor_tensor(lf, zf, 0.0, af, ALU.min, ALU.subtract).then_inc(S("lf_ready"), 1)
                    dve.wait_ge(S("lf_ready"), 1)
                    dve.wait_ge(S("cat_ready"), 1)
                    then(dve.tensor_copy(cat[:, PAST:PAST + NS], lf[:, NP:TOK]), "cum")
                    zero = lambda n: ones[0:H, 0:1].to_broadcast([H, n])
                    then(dve.tensor_tensor_scan(negp[0:H, :], zero(NP), lf[:, 0:NP], 0.0, ALU.mult, ALU.add), "cum")
                    then(dve.tensor_tensor_scan(negs[0:H, :], zero(PAST + NS), cat, 0.0, ALU.mult, ALU.add), "cum")
                    dve.tensor_scalar(negp[0:H, :], negp[0:H, :], -1.0, None, ALU.mult).then_inc(S("neg_ready"), 1)
                    dve.tensor_scalar(negs[0:H, :], negs[0:H, :], -1.0, None, ALU.mult).then_inc(S("neg_ready"), 1)
                if i == 2 * KC + 3:
                    dve.wait_ge(S("lf_mm"), 1)
                    for t in range(3):
                        r = 128 if t < 2 else NS
                        dve.tensor_copy(lo[0:r, t, :], P[1][0:r, H * t:H * t + H]).then_inc(S("logf_tok"), 1)
                if i == 2 * KC + 1:
                    dve.wait_ge(S("v_zero"), 1)
                if i >= 2 * KC + 1:
                    v_rows(i - 2 * KC - 1)
            v_rows(KC - 1)

            def negmax(n):
                nk = 128 * (n % 2 + 1)
                dve.wait_ge(S("s_mm"), n + 1)
                if n >= 3:
                    dve.wait_ge(S("p_exp"), n - 2)
                then(dve.reduce_max(stat[:, 8 + n % 3:9 + n % 3], P[n % 3][:, 0:nk], AX.X), "max_a")
                dve.tensor_scalar(stat[:, n % 3:n % 3 + 1], stat[:, 8 + n % 3:9 + n % 3], -1.0, None, ALU.mult)\
                    .then_inc(S("p_max"), 1)

            def norm_p(n):
                nk = 128 * (n % 2 + 1)
                dve.wait_ge(S("p_exp"), n + 1)
                then(dve.reciprocal(stat[:, 12 + n % 3:13 + n % 3], stat[:, 4 + n % 3:5 + n % 3]), "max_a")
                dve.tensor_scalar(Pp[:, n % 3, 0:nk], Pp[:, n % 3, 0:nk], stat[:, 12 + n % 3:13 + n % 3], None, ALU.mult)\
                    .then_inc(S("p_norm"), 1)

            def copy_pt(n):
                nk = 128 * (n % 2 + 1)
                dve.wait_ge(S("pt_mm"), n + 1)
                if n >= 2:
                    dve.wait_ge(S("pv_mm"), n - 1)
                dve.tensor_copy(PTp[:, n % 2, 0:nk], P[3 + n % 2][:, 0:nk]).then_inc(S("pt_out"), 1)

            def copy_o(c):
                dve.wait_ge(S("pv_mm"), 4 * c + 4)
                for a in range(2):
                    m = dve.tensor_copy(oT[64 * a:64 * a + 64, c, 0:NP], P[5 + c % 2][64 * a:64 * a + 64, NP * a:NP * a + NP])
                m.then_inc(S("o_out"), 1)

            NA = 2 * H
            for n in range(NA + 3):
                if n < NA:
                    negmax(n)
                if 1 <= n <= NA:
                    norm_p(n - 1)
                if 2 <= n < NA + 2:
                    copy_pt(n - 2)
                if n >= 3 and (n - 3) % 4 == 3:
                    copy_o((n - 3) // 4)
            for i in range(2):
                then(dve.memset(Ps[i][:, PAST + NS:640], 0.0), "max_a")

            def s_negmax(j):
                st = 16 + 8 * (j % 2)
                b0, b1 = [(0, 1), (2, 7)][j % 2]
                dve.wait_ge(S("ss_mm"), j + 1)
                if j >= 2:
                    dve.wait_ge(S("ps_exp"), j - 1)
                then(dve.reduce_max(stat[:, st + 3:st + 4], P[b0][:, :], AX.X), "max_a")
                then(dve.reduce_max(stat[:, st + 4:st + 5], P[b1][:, 0:NS], AX.X), "max_a")
                then(dve.tensor_tensor(stat[:, st + 5:st + 6], stat[:, st + 3:st + 4], stat[:, st + 4:st + 5], ALU.max), "max_a")
                dve.tensor_scalar(stat[:, st:st + 1], stat[:, st + 5:st + 6], -1.0, None, ALU.mult).then_inc(S("ps_max"), 1)

            def s_norm(j):
                st = 16 + 8 * (j % 2)
                dve.wait_ge(S("ps_exp"), j + 1)
                then(dve.tensor_tensor(stat[:, st + 6:st + 7], stat[:, st + 1:st + 2], stat[:, st + 2:st + 3], ALU.add), "max_a")
                then(dve.reciprocal(stat[:, st + 7:st + 8], stat[:, st + 6:st + 7]), "max_a")
                dve.tensor_scalar(Ps[j % 2][:, 0:PAST + NS], Ps[j % 2][:, 0:PAST + NS], stat[:, st + 7:st + 8], None, ALU.mult)\
                    .then_inc(S("ps_norm"), 1)

            def s_copy(j):
                dve.wait_ge(S("pts_mm"), j + 1)
                if j >= 1:
                    dve.wait_ge(S("pvs_mm"), j)
                dve.tensor_copy(PTs[:, 0:4, :].rearrange("p t n -> p (t n)"), P[3][:, :])
                dve.tensor_copy(PTs[:, 4, :], P[4][:, 0:128]).then_inc(S("pts_out"), 1)
                dve.wait_ge(S("pvs_mm"), j + 1)
                for a in range(2):
                    c = 2 * j + a
                    for b in range(2):
                        m = dve.tensor_copy(oT[64 * b:64 * b + 64, c, NP:TOK],
                                            P[5][64 * b:64 * b + 64, 64 * a + 32 * b:64 * a + 32 * b + 32])
                m.then_inc(S("os_out"), 1)

            for j in range(5):
                if j < 4:
                    s_negmax(j)
                if j >= 1:
                    s_copy(j - 1)
                if j < 4:
                    s_norm(j)
            for k in range(KC):
                m = dve.tensor_scalar(wrg[:, k, :], wr[:, k, :], g_ffn[:, 1, k:k + 1], None, ALU.mult)
            m.then_inc(S("wrg_ready"), 1)
            for d in range(KC):
                dve.wait_ge(S("wo_mm"), d + 1)
                dve.tensor_tensor(hT[:, d, :], hT[:, d, :], P[d % 2][:, 0:TOK], ALU.add).then_inc(S("h2"), 1)

            R = "route"
            then(dve.memset(lg[:, :, :], 0.0), R)
            dve.wait_ge(S("row_rms"), 1)
            then(dve.reciprocal(rs_tok[:, :], tv[:, 1, :]), R)
            dve.wait_ge(S("lg_mm"), 1)
            for t in range(3):
                r = 128 if t < 2 else NS
                then(dve.tensor_scalar(lg[0:r, t, :], P[4][0:r, NE * t:NE * t + NE], rs_tok[0:r, t:t + 1], None, ALU.mult), R)
            bc = lambda a: a.unsqueeze(2).to_broadcast([128, 3, NE])

            def largest(src, mask, i):
                then(dve.tensor_reduce(tv[:, i, :], src, AX.X, ALU.max), R)
                then(dve.tensor_tensor(key[:, :, :], src, bc(tv[:, i, :]), ALU.is_equal), R)
                then(dve.tensor_tensor(key[:, :, :], key[:, :, :], desc[:, :, :], ALU.mult), R)
                then(dve.tensor_reduce(tv[:, 7, :], key[:, :, :], AX.X, ALU.max), R)
                then(dve.tensor_tensor(mask, key[:, :, :], bc(tv[:, 7, :]), ALU.is_equal), R)

            largest(lg[:, :, :], m1[:, :, :], 5)
            then(dve.scalar_tensor_tensor(l2[:, :, :], m1[:, :, :], NEG, lg[:, :, :], ALU.mult, ALU.add), R)
            largest(l2[:, :, :], m2[:, :, :], 6)
            then(dve.tensor_tensor(tv[:, 3, :], tv[:, 6, :], tv[:, 5, :], ALU.subtract), R)
            dve.sem_inc(S("top2"), 1)
            bv = bc(valid[:, :])
            then(dve.tensor_tensor(m1[:, :, :], m1[:, :, :], bv, ALU.mult), R)
            then(dve.tensor_tensor(m2[:, :, :], m2[:, :, :], bv, ALU.mult), R)
            dve.tensor_tensor(key[:, :, :], m1[:, :, :], m2[:, :, :], ALU.add).then_inc(S("mask_ready"), 1)
            dve.wait_ge(S("mask_ready"), 1)
            dve.wait_ge(S("e2_ready"), 1)
            then(dve.tensor_scalar(tv[:, 2, :], tv[:, 4, :], 1.0, None, ALU.add), R)
            then(dve.reciprocal(tv[:, 5, :], tv[:, 2, :]), R)
            then(dve.tensor_tensor(tv[:, 6, :], tv[:, 4, :], tv[:, 5, :], ALU.mult), R)
            then(dve.tensor_tensor(m1[:, :, :], m1[:, :, :], bc(tv[:, 5, :]), ALU.mult), R)
            then(dve.tensor_tensor(m2[:, :, :], m2[:, :, :], bc(tv[:, 6, :]), ALU.mult), R)
            ge = gate[:, 0:NE, :].rearrange("p e t -> p t e")
            rk = rank[:, 0:NE, :].rearrange("p e t -> p t e")
            then(dve.memset(rank[:, NE, :], -1.0), R)
            then(dve.memset(gate[:, NE, :], 0.0), R)
            then(dve.tensor_tensor(ge, m1[:, :, :], m2[:, :, :], ALU.add), R)
            dve.wait_ge(S("rank_mm"), 1)
            then(dve.scalar_tensor_tensor(l2[:, :, :], P[7][:, 0:3 * NE].rearrange("p (t e) -> p t e", t=3), 1.0,
                                          key[:, :, :], ALU.add, ALU.mult), R)
            then(dve.tensor_scalar(rk, l2[:, :, :], -1.0, None, ALU.add), R)
            then(dve.reduce_max(most[:, :], P[7][:, 32:32 + NE], AX.X), R)
            dve.tensor_copy(most_i[:, :], most[:, :]).then_inc(S("most_ready"), 1)

            def expert(e, it, p):
                dve.wait_ge(S("aux_pe"), it * 12 + (E_AUXP + 4))
                dve.tensor_copy(DgT[:, :], P[5][0:CAP, 0:384]).then_inc(S("aux_dve"), 1)
                for uu in range(BLK):
                    dve.wait_ge(S("e_silu"), it * BLK + (E_SILU + uu + 1))
                    dve.wait_ge(S("e_dn"), it * BLK + (E_DN + (uu - 2 if uu >= 3 else [-1, 0, -2][uu])))
                    dve.tensor_tensor(hm[:, uu % 3].rearrange("p c n -> p (c n)"),
                                      sl[:, uu % 3].rearrange("p c n -> p (c n)"), P[uu % 3][:, 2 * CAP:4 * CAP],
                                      ALU.mult).then_inc(S("e_hm"), 1)
                    if uu == 5:
                        dispatch_next(e, it, p)
                for i in range(6, 12):
                    half, t = (i - 6) // 3, (i - 6) % 3
                    r = 128 if t < 2 else NS
                    dve.wait_ge(S("aux_pe"), it * 12 + (E_AUXP + i + 1))
                    a = acc[0:r, t, 512 * half:512 * half + 512]
                    dve.tensor_tensor(a, a, P[5 + i % 3][0:r, :], ALU.add).then_inc(S("aux_dve"), 1)

            def make(e, want_aux, want_cur, wait_read):
                dve.wait_ge(S("aux_pe"), want_aux)
                dve.wait_ge(S("dispatch"), wait_read)
                dve.tensor_copy(cur[:, 0:3], rank[:, bass.ds(e, 1), :].rearrange("p a t -> p (a t)")).then_inc(S("cur"), 1)
                dve.tensor_copy(cur[:, 3:6], gate[:, bass.ds(e, 1), :].rearrange("p a t -> p (a t)")).then_inc(S("cur"), 1)
                dve.wait_ge(S("cur"), want_cur)
                for t in range(3):
                    dve.tensor_scalar(Dg[:, t, :], slots_iota[:, :], cur[:, t:t + 1], cur[:, 3 + t:4 + t],
                                      ALU.is_equal, ALU.mult)
                for t in range(3):
                    m = dve.tensor_scalar(Dx[:, t, :], slots_iota[:, :], cur[:, t:t + 1], rs_tok[:, t:t + 1],
                                          ALU.is_equal, ALU.mult)
                m.then_inc(S("dispatch"), 1)

            def dispatch_next(e, it, p):
                make(e + 1, it * 12 + (E_AUXP + 4), it * 2 + (4 + 2 * p), it + (E_D + 1 + p))

            make(0, E_AUXP, 2, E_D)
            with dve.Fori(0, NE) as e:
                expert(e, e, 0)
            n = dve.value_load(most_i[0:1, 0:1], min_val=0, max_val=TOK)
            for p in range(1, PASSES):
                with dve.If(n > p * CAP):
                    dve.wait_ge(S("cur"), 18 * p)
                    dve.tensor_scalar(rank[:, :, :], rank[:, :, :], -float(CAP), None, ALU.add).then_inc(S("pass"), 1)
                    dve.wait_ge(S("pass"), p)
                    make(0, NE * p * 12 + E_AUXP, 18 * p + 2, NE * p + (E_D + p))
                    with dve.Fori(0, NE) as e:
                        expert(e, e + p * NE, p)
            dve.drain().then_inc(S("acc_done"), 1)

        assert len(sems) < 200, len(sems)


_INS = ["x_prompt", "x_sample", "state_pool", "cache_k", "cache_v", "cache_logf", "g_pool_norm", "w_pool",
        "pool_scale", "g_kv_norm", "w_kvf", "b_f", "g_k", "g_attn_norm", "w_q", "g_q", "w_o", "g_ffn_norm",
        "w_ffn_gu", "w_ffn_down", "w_router", "w_moe_gu", "w_moe_down"]
_OUTS = [("y_prompt", (1, 256, 1024)), ("y_sample", (1, 32, 1024)), ("state_prompt", (1, 1, 15, 1024)),
         ("k_prompt", (1, 256, 16, 64)), ("v_prompt", (1, 256, 16, 64)), ("logf_prompt", (1, 256, 16)),
         ("state_sample", (1, 1, 15, 1024)), ("k_sample", (1, 32, 16, 64)), ("v_sample", (1, 32, 16, 64)),
         ("logf_sample", (1, 32, 16))]


def kernel(**inputs):
    import numpy as _np
    import concourse.bacc as _bacc
    from concourse import mybir as _mybir
    from concourse.bass_utils import run_bass_kernel_spmd as _run

    nc = _bacc.Bacc("TRN2", target_bir_lowering=False, num_devices=1, dynamic_dma_scratch_size=4096)
    arrays, ins, outs = {}, {}, {}
    for name in _INS:
        a = _np.ascontiguousarray(inputs[name])
        arrays[f"in_{name}"] = a
        ins[name] = nc.dram_tensor(f"in_{name}", a.shape, _mybir.dt.from_np(a.dtype), kind="ExternalInput").ap()
    for name, shape in _OUTS:
        outs[name] = nc.dram_tensor(f"out_{name}", shape, _mybir.dt.float32, kind="ExternalOutput").ap()
    build_program(nc, ins, outs)
    r = _run(nc, [arrays], core_ids=[0])
    return tuple(r.results[0][f"out_{name}"] for name, _ in _OUTS)
```

```python
import concourse.bass as bass
from concourse import mybir
from contextlib import ExitStack

D = 1024
FF = 2816
NP, NS = 256, 32
TOK = NP + NS
PAST = 512
HIST = 15
H, HD = 16, 64
NE = 8
CAP = 128
PASSES = -(-TOK // CAP)
KC = D // 128
FC = FF // 128
BLK = FC // 2
SPLITS = 3 * BLK - 2
EPS = 1e-6
NEG = -1.0e30

SLOTS = 4
SLOT = 6144
U_POOL = 0
U_GU = 1
U_DN = U_GU + BLK
U_Q = U_DN + 4
U_KV = U_Q + 2
U_KC = U_KV + 4
U_VC = U_KC + 1
U_O = U_VC + 1
U_MOE = U_O + 2
EXP_SLOT = [(U_MOE + u) % SLOTS for u in range(BLK)]


def earlier_user(u):
    same = [v for v in range(-BLK, u) if EXP_SLOT[v % BLK] == EXP_SLOT[u]]
    return same[-1]


def split_no(q, u):
    if q < 2:
        assert u
        return 3 * u + q - 2
    return min(3 * u + 3, SPLITS)


def build_program(nc, ins, outs):
    F32, F32R, I32 = mybir.dt.float32, mybir.dt.float32r, mybir.dt.int32
    ALU, ACT, AX = mybir.AluOpType, mybir.ActivationFunctionType, mybir.AxisListType
    ctx = ExitStack()
    with ctx:
        def sb(name, shape, dt=F32):
            return ctx.enter_context(nc.sbuf_tensor(name, shape, dt))

        sems = {}

        def S(name):
            if name not in sems:
                sems[name] = ctx.enter_context(nc.semaphore(name))
            return sems[name]

        ring = sb("ring", [128, SLOTS, SLOT])
        w_hi = sb("w_hi", [128, 3, 2048], F32R)
        w_lo = sb("w_lo", [128, 3, 2048], F32R)
        hT = sb("hT", [128, KC, TOK])
        atB = -(-nc.sbuf_base // 32) * 32
        regB = sb("regB", [128, KC * TOK])
        atC = -(-nc.sbuf_base // 32) * 32
        regC = sb("regC", [128, KC * TOK])
        uh = nc.alloc_sbuf_tensor_at("uh", [128, KC, TOK], F32R, offset=atB)
        ul = nc.alloc_sbuf_tensor_at("ul", [128, KC, TOK], F32R, offset=atC)
        xh = nc.alloc_sbuf_tensor_at("xh", [128, KC, CAP], F32R, offset=atB)
        xl = nc.alloc_sbuf_tensor_at("xl", [128, KC, CAP], F32R, offset=atB + 4 * KC * CAP)
        hTh = nc.alloc_sbuf_tensor_at("hTh", [128, 2, 2, CAP], F32R, offset=atC)
        hTl = nc.alloc_sbuf_tensor_at("hTl", [128, 2, 2, CAP], F32R, offset=atC + 16 * CAP)
        regD = sb("regD", [128, 3 * D])
        regE = sb("regE", [128, H * TOK])
        ident = sb("ident", [128, 128])
        ones = sb("ones", [128, 128])
        headones = sb("headones", [128, 128])
        causal = sb("causal", [128, 128])
        causal_s = sb("causal_s", [128, NS])
        before = sb("before", [128, 128])
        slots_iota = sb("slots_iota", [128, CAP])
        sels = sb("sels", [128, H, NS])
        g_pool = sb("g_pool", [128, KC]); p_scale = sb("p_scale", [128, KC]); g_kv = sb("g_kv", [128, KC])
        g_attn = sb("g_attn", [128, KC]); g_ffn = sb("g_ffn", [128, 2, KC])
        gk = sb("gk", [128, 1]); gq = sb("gq", [128, 1]); gq8 = sb("gq8", [128, 1]); bf = sb("bf", [H, 1])
        eps = sb("eps", [128, 1]); one = sb("one", [128, 1])
        stat = sb("stat", [128, 64])
        silu_scratch = stat[:, 40:41]
        counts = stat[:, 48:64]; inv_cnt = sb("inv_cnt", [128, 16])
        wf = sb("wf", [128, KC, H]); wr = sb("wr", [128, KC, NE])
        rms = sb("rms", [128, 2, TOK]); rstd = sb("rstd", [128, 2, TOK])
        QS = sb("QS", [128, KC, 128])
        negs = sb("negs", [128, PAST + NS]); negp = sb("negp", [128, NP])
        lt = sb("lt", [128, 4, H])
        lo = sb("lo", [128, 3, H])

        DE = lambda off, n: (regD[:, off:off + n] if off + n <= 3 * D else regE[:, off - 3 * D:off - 3 * D + n])
        xtok = regD[:, :].rearrange("p (t n) -> p t n", t=3)
        UW = NP + NS + 2 * HIST
        U = regE[:, 0:KC * UW].rearrange("p (c n) -> p c n", c=KC)
        winA = regD[:, 0:KC * UW].rearrange("p (c n) -> p c n", c=KC)
        winB = regC[:, 0:6 * UW].rearrange("p (c n) -> p c n", c=6)
        diff = regB[:, :].rearrange("p (c n) -> p c n", c=KC)
        u32 = regD[:, 0:KC * TOK].rearrange("p (c n) -> p c n", c=KC)
        u = regB[:, :].rearrange("p (c n) -> p c n", c=KC)
        sq = regC[:, :].rearrange("p (c n) -> p c n", c=KC)
        hmA = regD[:, 0:10 * TOK].rearrange("p (c n) -> p c n", c=10)
        hmB = regE[:, 0:12 * TOK].rearrange("p (c n) -> p c n", c=12)
        uq = regD[:, 0:KC * TOK].rearrange("p (c n) -> p c n", c=KC)
        kT = regC[:, :].rearrange("p (c n) -> p c n", c=KC)
        vtok = regD[:, :].rearrange("p (t n) -> p t n", t=3)
        qz = regE[:, :].rearrange("p (h n) -> p h n", h=H)
        oT = regB[:, :].rearrange("p (c n) -> p c n", c=KC)
        htok = regD[:, :].rearrange("p (t n) -> p t n", t=3)
        acc = regE[:, 0:3 * D].rearrange("p (t n) -> p t n", t=3)
        kout = [regB[:, 0:D], regB[:, D:2 * D], regE[:, 3 * D:4 * D]]
        tail4, tail5 = ring[:, 2, 4096:SLOT], ring[:, 3, 4096:SLOT]
        st_out = tail4[0:HIST, 0:2 * D].rearrange("p (s n) -> p s n", s=2)
        Pp = tail4[:, 0:3 * NP].rearrange("p (i n) -> p i n", i=3)
        PTp = tail4[:, 3 * NP:5 * NP].rearrange("p (i n) -> p i n", i=2)
        sg = regE[:, 14 * TOK:16 * TOK].rearrange("p (i n) -> p i n", i=2)
        raw = tail5[:, 0:2 * TOK].rearrange("p (i n) -> p i n", i=2)
        sqh = tail5[:, 2 * TOK:4 * TOK].rearrange("p (i n) -> p i n", i=2)
        zf, lf = tail5[0:H, 4 * TOK:5 * TOK], tail5[0:H, 5 * TOK:6 * TOK]
        af = tail5[0:H, 6 * TOK:7 * TOK]
        cat = tail4[0:H, 5 * NP:5 * NP + PAST + NS]
        Ps = [tail5[:, 0:640], tail5[:, 640:1280]]
        PTs = tail5[:, 1280:1920].rearrange("p (t n) -> p t n", t=5)
        kc = ring[:, U_KC % SLOTS, 0:4096].rearrange("p (t n) -> p t n", t=4)
        vc = ring[:, U_VC % SLOTS, 0:4096].rearrange("p (t n) -> p t n", t=4)
        ytok = regC[0:CAP, 8 * CAP:8 * CAP + D]
        hflat = hT[:, :, :].rearrange("p c n -> p (c n)")
        Dx = hflat[:, 0:3 * CAP].rearrange("p (t n) -> p t n", t=3)
        Dg = hflat[:, 3 * CAP:6 * CAP].rearrange("p (t n) -> p t n", t=3)
        DgT = hflat[0:CAP, 6 * CAP:6 * CAP + 3 * 128]
        sl = hflat[:, 1152:1664].rearrange("p (i n) -> p i n", i=2)
        hm = hflat[:, 1664:2176].rearrange("p (i n) -> p i n", i=2)
        qflat = QS[:, :, :].rearrange("p c n -> p (c n)")
        lg, m1, m2, key, l2 = (qflat[:, 24 * i:24 * i + 24].rearrange("p (t e) -> p t e", t=3) for i in range(5))
        tv = qflat[:, 120:144].rearrange("p (i t) -> p i t", i=8)
        rank = qflat[:, 144:171].rearrange("p (e t) -> p e t", t=3)
        cur = qflat[:, 198:204]
        gate = qflat[:, 171:198].rearrange("p (e t) -> p e t", t=3)
        wrg = qflat[:, 204:268].rearrange("p (k e) -> p k e", k=KC)
        desc = sb("desc", [128, 3, NE]); rs_tok = sb("rs_tok", [128, 3]); valid = sb("valid", [128, 3])
        most = sb("most", [128, 1]); most_i = sb("most_i", [128, 1], I32)

        P = [ctx.enter_context(nc.psum_tensor(f"P{i}", [128, 512], F32)) for i in range(8)]

        def slot(n):
            return ring[:, n % SLOTS, :]

        def through(n):
            return sum(32 if U_GU <= x < U_DN else 16 for x in range(n % SLOTS, n + 1, SLOTS))

        def arrived(eng, n):
            eng.wait_ge(S(f"arrived{n % SLOTS}"), through(n))

        def exp_arrived(eng, e, uu):
            s = EXP_SLOT[uu]
            base = through(max(n for n in range(U_MOE) if n % SLOTS == s))
            per = [v for v in range(BLK) if EXP_SLOT[v] == s]
            eng.wait_ge(S(f"arrived{s}"), e * (48 * len(per)) + (base + 48 * (per.index(uu) + 1)))

        def used(eng, n):
            if n == U_POOL:
                eng.wait_ge(S("pool_mm"), KC)
            elif n < U_DN:
                eng.wait_ge(S("ffn_wl"), 2 * (n - U_GU + 1))
            elif n < U_Q:
                eng.wait_ge(S("ffn_dn"), 2 * (n - U_DN + 1))
            elif n < U_KC:
                eng.wait_ge(S("proj_mm"), 4 * (n - U_Q + 1))
            elif n < U_O:
                eng.wait_ge(S("pvs_mm"), 4)
            else:
                eng.wait_ge(S("wo_mm"), 4 * (n - U_O + 1))

        exp_gu = [ring[:, s, 0:4096].rearrange("p (k h n) -> p k h n", k=KC, h=2) for s in range(SLOTS)]
        exp_dn = [ring[:, s, 4096:6144].rearrange("p (c n) -> p c n", c=2) for s in range(SLOTS)]

        E_GA, E_GB, E_T, E_DN, E_SILU, E_HM, E_HTH, E_HTL = 1, 1, 2, 1, 1, 2, 1, 2
        E_HI, E_LO, E_XH, E_Y, E_D, E_AUXP, E_AUXV = 1, 8, 1, 2, 1, 1, 1
        ITS = 9

        def down_buf(uu):
            return 2 if uu < BLK - 1 else 1

        def ffn_raw(f):
            w = slot(U_GU + f // 2)[:, 0:4096].rearrange("p (h n) -> p h n", h=2 * KC)
            return w[:, :, 128 * (f % 2):128 * (f % 2) + 128]

        def ffn_part(part, f):
            return part[:, f % 3, :].rearrange("p (h n) -> p h n", h=2 * KC)

        CONSTS = 23

        block = ctx.enter_context(nc.Block())

        @block.sync
        def _(sp):
            def load(n, dst, src, **kw):
                if n >= SLOTS:
                    used(sp, n - SLOTS)
                sp.dma_start(dst, src, **kw).then_inc(S(f"arrived{n % SLOTS}"), 16)

            sp.dma_start(xtok[:, 0:2, :], ins["x_prompt"][0].rearrange("(t p) n -> p t n", p=128))\
              .then_inc(S("x_in"), 16)
            sp.wait_ge(S("xtok_zero"), 1)
            sp.dma_start(xtok[0:NS, 2, :], ins["x_sample"][0]).then_inc(S("x_in"), 16)
            sp.dma_start(xtok[NS:NS + HIST, 2, :], ins["state_pool"][0, 0]).then_inc(S("x_in"), 16)
            load(U_POOL, slot(U_POOL)[:, 0:2048].rearrange("p (g k n) -> p (g k) n", g=4, k=2),
                 ins["w_pool"][0].rearrange("g (k p) n -> p (g k) n", p=128))
            for b in range(BLK):
                n = U_GU + b
                if n >= SLOTS:
                    used(sp, n - SLOTS)
                gu = ins["w_ffn_gu"][0].rearrange("(k p) (h n) -> h p k n", p=128, h=2)
                dst = slot(n)[:, 0:4096].rearrange("p (h k n) -> p h k n", h=2, k=KC)
                for half in range(2):
                    sp.dma_start(dst[:, half], gu[half, :, :, 256 * b:256 * b + 256])\
                      .then_inc(S(f"arrived{n % SLOTS}"), 16)
            for b in range(4):
                if (U_DN + b) % SLOTS == 2:
                    sp.wait_ge(S("stored"), 32)
                load(U_DN + b, slot(U_DN + b)[:, 0:FC * 256].rearrange("p (k n) -> p k n", k=FC),
                     ins["w_ffn_down"][0].rearrange("(k p) n -> p k n", p=128)[:, :, 256 * b:256 * b + 256])
            for n0, cnt, w in ((U_Q, 2, ins["w_q"][0]), (U_KV, 4, ins["w_kvf"]), (U_KC, 1, None), (U_VC, 1, None),
                               (U_O, 2, ins["w_o"][0])):
                for b in range(cnt):
                    n = n0 + b
                    if w is None:
                        c = ins["cache_k" if n == U_KC else "cache_v"][0].rearrange("(t p) h d -> p t (h d)", p=128)
                        load(n, slot(n)[:, 0:4096].rearrange("p (t n) -> p t n", t=4), c)
                    else:
                        load(n, slot(n)[:, 0:4096].rearrange("p (k n) -> p k n", k=KC),
                             w.rearrange("(k p) n -> p k n", p=128)[:, :, 512 * b:512 * b + 512])

            def load_expert(e, it):
                for uu in range(BLK):
                    if isinstance(it, int) and earlier_user(uu) < 0:
                        used(sp, U_MOE + uu - SLOTS)
                    else:
                        v = earlier_user(uu)
                        sp.wait_ge(S("w_lo"), it * SPLITS + (E_LO + split_no(2, v % BLK) - (SPLITS if v < 0 else 0)))
                        if v == 0:
                            sp.wait_ge(S("first_lo"), it * 2 + 2)
                    s = EXP_SLOT[uu]
                    wgu = ins["w_moe_gu"][0, bass.ds(e, 1)].rearrange("e (k p) n -> p (e k) n", p=128)
                    wdn = ins["w_moe_down"][0, bass.ds(e, 1)].rearrange("e (k p) n -> p (e k) n", p=128)
                    sp.dma_start(exp_gu[s][:, :, 0], wgu[:, :, 256 * uu:256 * uu + 256]).then_inc(S(f"arrived{s}"), 16)
                    sp.dma_start(exp_gu[s][:, :, 1], wgu[:, :, FF + 256 * uu:FF + 256 * uu + 256])\
                      .then_inc(S(f"arrived{s}"), 16)
                    sp.dma_start(exp_dn[s], wdn[:, 2 * uu:2 * uu + 2, :]).then_inc(S(f"arrived{s}"), 16)

            load_expert(0, 0)
            with sp.Fori(1, NE) as e:
                load_expert(e, e)
            sp.wait_ge(S("most_ready"), 1)
            n = sp.value_load(most_i[0:1, 0:1], min_val=0, max_val=TOK)
            for p in range(1, PASSES):
                with sp.If(n > p * CAP):
                    with sp.Fori(0, NE) as e:
                        load_expert(e, e + p * NE)

        @block.gpsimd
        def _(pool):
            pool.memset(xtok[:, 2, :], 0.0).then_inc(S("xtok_zero"), 1)
            made = 0

            def const(ins):
                nonlocal made
                made += 1
                ins.then_inc(S("const"), 1)
                pool.wait_ge(S("const"), made)

            const(pool.memset(ident[:, :], 0.0))
            const(pool.memset(causal[:, :], 0.0))
            const(pool.memset(causal_s[:, :], 0.0))
            const(pool.memset(before[:, :], 0.0))
            const(pool.memset(ones[:, :], 1.0))
            const(pool.memset(headones[:, :], 0.0))
            const(pool.iota(slots_iota[:, :], [[1, CAP]], base=0, channel_multiplier=0,
                            allow_small_or_imprecise_dtypes=True))
            const(pool.iota(counts[:, :], [[1, 16]], base=1, channel_multiplier=0,
                            allow_small_or_imprecise_dtypes=True))
            const(pool.iota(desc[:, :, :], [[0, 3], [-1, NE]], base=NE, channel_multiplier=0,
                            allow_small_or_imprecise_dtypes=True))
            const(pool.memset(eps[:, :], EPS))
            const(pool.memset(one[:, :], 1.0))
            const(pool.memset(valid[:, :], 1.0))
            const(pool.affine_select(out=ident[:, :], in_=ident[:, :], compare_op=ALU.not_equal, fill=1.0, base=0,
                                     pattern=[[-1, 128]], channel_multiplier=1))
            const(pool.affine_select(out=causal[:, :], in_=causal[:, :], compare_op=ALU.is_ge, fill=NEG, base=0,
                                     pattern=[[-1, 128]], channel_multiplier=1))
            const(pool.affine_select(out=before[:, :], in_=before[:, :], compare_op=ALU.is_ge, fill=1.0, base=0,
                                     pattern=[[-1, 128]], channel_multiplier=1))
            for q in range(4):
                const(pool.affine_select(out=causal_s[32 * q:32 * q + 32, :], in_=causal_s[32 * q:32 * q + 32, :],
                                         compare_op=ALU.is_ge, fill=NEG, base=0, pattern=[[-1, NS]],
                                         channel_multiplier=1))
            for q in range(2):
                const(pool.memset(headones[64 * q:64 * q + 64, 64 * q:64 * q + 64], 1.0))
            const(pool.memset(valid[32:64, 2:3], 0.0))
            const(pool.memset(valid[64:128, 2:3], 0.0))
            assert made == CONSTS
            for dst, src in ((g_kv, ins["g_kv_norm"]), (g_attn, ins["g_attn_norm"][0]), (g_ffn[:, 1], ins["g_ffn_norm"][1])):
                with nc.allow_non_contiguous_dma(reason="a gain for each feature, 4 KB"):
                    pool.dma_start(dst[:, :], src.rearrange("(c p) -> p c", p=128)).then_inc(S("gains_in"), 16)
            for half in range(2):
                pool.dma_start(gk[64 * half:64 * half + 64, :], ins["g_k"].rearrange("(d a) -> d a", a=1))\
                    .then_inc(S("gains_in"), 16)
                pool.dma_start(gq[64 * half:64 * half + 64, :], ins["g_q"][0].rearrange("(d a) -> d a", a=1))\
                    .then_inc(S("gains_in"), 16)
            pool.dma_start(bf[:, :], ins["b_f"].rearrange("(d a) -> d a", a=1)).then_inc(S("gains_in"), 16)
            pool.dma_start(wf[:, :, :], ins["w_kvf"].rearrange("(k p) n -> p k n", p=128)[:, :, 2 * D:2 * D + H])\
                .then_inc(S("gains_in"), 16)
            pool.dma_start(wr[:, :, :], ins["w_router"][0].rearrange("(k p) n -> p k n", p=128))\
                .then_inc(S("gains_in"), 16)
            pool.dma_start(lt[:, :, :], ins["cache_logf"][0].rearrange("(t p) h -> p t h", p=128))\
                .then_inc(S("gains_in"), 16)
            for tile in (QS[:, :, :], negs[:, :], negp[:, :]):
                pool.memset(tile, 0.0).then_inc(S("zeros"), 1)
            pool.wait_ge(S("U"), 4)
            pool.wait_ge(S("U_hist"), 1)
            for i, (dst, src, c) in enumerate(((winA, U, 6), (winB, winA, 4), (winA, winB, 6), (winB, winA, 4))):
                w = 1 << i
                a = src[:, 6:8] if src is not winB else src[:, 4:6]
                pool.tensor_tensor(dst[:, c:c + 2, 2 * w - 1:UW], a[:, :, 2 * w - 1:UW], a[:, :, w - 1:UW - w], ALU.add)\
                    .then_inc(S("win3"), 1)
                pool.wait_ge(S("win3"), i + 1)
            pool.wait_ge(S("state_out"), 4)
            pool.dma_start(outs["state_prompt"][0, 0], st_out[:, 0, :]).then_inc(S("stored"), 16)
            pool.dma_start(outs["state_sample"][0, 0], st_out[:, 1, :]).then_inc(S("stored"), 16)
            pool.wait_ge(S("stored"), 32)
            pool.wait_ge(S("ffn_out"), KC)
            pool.memset(qz[0:64, 1:H:2, :], 0.0).then_inc(S("qz_zero"), 1)
            pool.memset(qz[64:128, 0:H:2, :], 0.0).then_inc(S("qz_zero"), 1)
            pool.wait_ge(S("proj_mm"), KC)
            pool.memset(vtok[:, 2, :], 0.0).then_inc(S("v_zero"), 1)
            pool.wait_ge(S("logf_tok"), 3)
            pool.dma_start(outs["logf_prompt"][0].rearrange("(t p) h -> p t h", p=128), lo[:, 0:2, :])\
                .then_inc(S("stored"), 16)
            pool.dma_start(outs["logf_sample"][0], lo[0:NS, 2, :]).then_inc(S("stored"), 16)
            pool.wait_ge(S("v_tok"), KC)
            pool.dma_start(outs["v_prompt"][0].rearrange("(t p) h d -> p t (h d)", p=128), vtok[:, 0:2, :])\
                .then_inc(S("v_stored"), 16)
            pool.dma_start(outs["v_sample"][0].rearrange("p h d -> p (h d)"), vtok[0:NS, 2, :])\
                .then_inc(S("v_stored"), 16)
            pool.wait_ge(S("v_stored"), 32)
            pool.wait_ge(S("wo_mm"), KC)
            pool.memset(htok[:, 2, :], 0.0).then_inc(S("htok_zero"), 1)
            pool.wait_ge(S("k_tok"), 6)
            for t in range(2):
                pool.dma_start(outs["k_prompt"][0, 128 * t:128 * t + 128].rearrange("p h d -> p (h d)"), kout[t])\
                    .then_inc(S("k_stored"), 16)
            pool.dma_start(outs["k_sample"][0].rearrange("p h d -> p (h d)"), kout[2][0:NS, :])\
                .then_inc(S("k_stored"), 16)

            def expert(it):
                s = EXP_SLOT[0]
                for q in range(2):
                    if q == 0:
                        exp_arrived(pool, it, 0)
                        pool.wait_ge(S("e_ga"), it * BLK + E_GA)
                    else:
                        pool.wait_ge(S("e_dn"), it * BLK + E_DN)
                    w = ring[:, s, 2048 * q:2048 * q + 2048]
                    pool.tensor_tensor(w_hi[:, q, :], w, ones[:, 0:1].to_broadcast([128, 2048]), ALU.mult).then_inc(S("first_hi"), 1)
                    pool.wait_ge(S("first_hi"), it * 2 + (q + 1))
                    pool.tensor_tensor(w_lo[:, q, :], w, w_hi[:, q, :].bitcast(F32), ALU.subtract)\
                        .then_inc(S("first_lo"), 1)

            with pool.Fori(0, NE) as e:
                expert(e)
            pool.wait_ge(S("most_ready"), 1)
            n = pool.value_load(most_i[0:1, 0:1], min_val=0, max_val=TOK)
            for p in range(1, PASSES):
                with pool.If(n > p * CAP):
                    with pool.Fori(0, NE) as e:
                        expert(e + p * NE)
            pool.wait_ge(S("acc_done"), 1)
            pool.dma_start(outs["y_prompt"][0].rearrange("(t p) n -> p t n", p=128), acc[:, 0:2, :])\
                .then_inc(S("stored"), 16)
            pool.dma_start(outs["y_sample"][0], acc[0:NS, 2, :]).then_inc(S("stored"), 16)
            pool.wait_ge(S("stored"), 96)
            pool.wait_ge(S("k_stored"), 48)

        @block.tensor
        def _(pe):
            def mm(out, lhsT, rhs, start, stop, **kw):
                return pe.matmul(out, lhsT, rhs, start=start, stop=stop, **kw)

            def products(bank, pairs, first, last):
                for i, (a, w) in enumerate(pairs):
                    m = mm(bank, a, w, first and i == 0, last and i == len(pairs) - 1, skip_group_check=True)
                return m

            def three(ah, al, wh, wl):
                return [(ah, wh), (ah, wl), (al, wh)]

            pe.wait_ge(S("const"), CONSTS)
            pe.wait_ge(S("x_in"), 48)
            for c in range(KC):
                if c >= 4:
                    pe.wait_ge(S("xT"), c - 3)
                for t in range(3):
                    m = pe.transpose(P[c % 4][:, 128 * t:128 * t + 128], xtok[:, t, 128 * c:128 * c + 128], ident[:, :])
                m.then_inc(S("xT_mm"), 1)

            def sum_squares(bank, stage, c):
                pe.wait_ge(S(stage + "_sq"), c + 1)
                m = mm(P[bank][:, 0:TOK], ones[:, :], sq[:, c, :], c == 0, c == KC - 1)
                if c == KC - 1:
                    m.then_inc(S(stage + "_ss"), 1)

            for c in range(KC):
                sum_squares(4, "n0", c)

            arrived(pe, U_POOL)
            wp = slot(U_POOL)[:, 0:2048].rearrange("p (g k n) -> p (g k) n", g=4, k=2)
            for c in range(KC):
                g = c // 2
                pe.wait_ge(S("diff"), g + 1)
                if c >= 4:
                    pe.wait_ge(S("pooled"), c - 3)
                for k in range(2):
                    m = mm(P[c % 4][:, 0:TOK], wp[:, 2 * g + k, 128 * (c % 2):128 * (c % 2) + 128],
                           diff[:, 2 * g + k, :], k == 0, k == 1)
                m.then_inc(S("pool_mm"), 1)
            for c in range(KC):
                if c == 0:
                    pe.wait_ge(S("pooled"), 5)
                sum_squares(0, "n1", c)
            for s, at in ((0, HIST + NP - HIST), (1, HIST + NP + HIST + NS - HIST)):
                for half in range(2):
                    bank = [5, 6, 7, 4][2 * s + half]
                    for c in range(4):
                        m = pe.transpose(P[bank][0:HIST, 128 * c:128 * c + 128],
                                         U[:, 4 * half + c, at:at + HIST], ident[:, :])
                    m.then_inc(S("state_mm"), 1)


            for f in range(FC):
                if f == 1:
                    pe.wait_ge(S("state_out"), 4)
                if f >= 3:
                    pe.wait_ge(S("ffn_hm"), f - 2)
                pe.wait_ge(S("ffn_wl"), f + 1)
                wh, wl = ffn_part(w_hi, f), ffn_part(w_lo, f)
                for half in range(2):
                    for k in range(KC):
                        if f == 0 and half == 0:
                            pe.wait_ge(S("u_ffn"), k + 1)
                        h, l = wh[:, KC * half + k, :], wl[:, KC * half + k, :]
                        m = products(P[1 + 2 * (f % 3) + half][:, 0:TOK],
                                     [(h, uh[:, k, :]), (h, ul[:, k, :]), (l, uh[:, k, :])], k == 0, k == KC - 1)
                m.then_inc(S("ffn_gu"), 1)
            for b in range(4):
                n = U_DN + b
                arrived(pe, n)
                w = slot(n)[:, 0:FC * 256].rearrange("p (k n) -> p k n", k=FC)
                for j in range(2):
                    d = 2 * b + j
                    if d >= 2:
                        pe.wait_ge(S("ffn_out"), d - 1)
                    for f in range(FC):
                        if d == 0:
                            pe.wait_ge(S("ffn_hm"), f + 1)
                        src = hmA[:, f, :] if f < 10 else hmB[:, f - 10, :]
                        m = mm(P[7 if d % 2 == 0 else 0][:, 0:TOK], w[:, f, 128 * j:128 * j + 128], src,
                               f == 0, f == FC - 1)
                    m.then_inc(S("ffn_dn"), 1)
                    if d >= 1:
                        sum_squares(1, "n2", d - 1)
            sum_squares(1, "n2", KC - 1)

            def proj(i, w, col, act, first_wait):
                if i >= 2:
                    pe.wait_ge(S("raw"), i - 1)
                for k in range(KC):
                    if first_wait is not None:
                        pe.wait_ge(S(first_wait), k + 1)
                    m = mm(P[2 + i % 2][:, 0:TOK], w[:, k, col:col + 128], act[:, k, :], k == 0, k == KC - 1)
                m.then_inc(S("proj_mm"), 1)
                return m

            def head_sums(i):
                pe.wait_ge(S("head_sq"), i + 1)
                if i >= 2:
                    pe.wait_ge(S("head_rms"), i - 1)
                mm(P[4 + i % 2][:, 0:TOK], headones[:, :], sqh[:, i % 2, :], True, True).then_inc(S("head_ss"), 1)

            pe.wait_ge(S("gains_in"), 176)
            for t in range(4):
                m = pe.transpose(P[6][0:H, 128 * t:128 * t + 128], lt[:, t, :], ident[:, :])
            m.then_inc(S("cache_f"), 1)
            for i in range(2 * KC):
                n = (U_Q if i < KC else U_KV) + (i % KC) // 4
                if i % 4 == 0:
                    arrived(pe, n)
                w = slot(n)[:, 0:4096].rearrange("p (k n) -> p k n", k=KC)
                m = proj(i, w, 128 * (i % 4), uq if i < KC else u,
                         "u_q" if i == 0 else "u_kv" if i == KC else None)
                if i == KC:
                    for k in range(KC):
                        m = mm(P[7][0:H, 0:TOK], wf[:, k, :], u[:, k, :], k == 0, k == KC - 1)
                    m.then_inc(S("f_mm"), 1)
                if i >= 1:
                    head_sums(i - 1)

            def v_transposes(c):
                i = 2 * KC + c
                pe.wait_ge(S("raw"), i + 1)
                if c >= 2:
                    pe.wait_ge(S("v_tok"), c - 1)
                if c == 0:
                    pe.wait_ge(S("cat_ready"), 1)
                if c == 1:
                    pe.wait_ge(S("z_ready"), 1)
                for t in range(3):
                    r = 128 if t < 2 else NS
                    m = pe.transpose(P[6 + c % 2][0:r, 128 * t:128 * t + 128], raw[:, i % 2, 128 * t:128 * t + r], ident[:, :])
                m.then_inc(S("vt_mm"), 1)

            for c in range(KC):
                i = 2 * KC + c
                n = U_KV + 2 + c // 4
                if c % 4 == 0:
                    arrived(pe, n)
                w = slot(n)[:, 0:4096].rearrange("p (k n) -> p k n", k=KC)
                m = proj(i, w, 128 * (c % 4), u, None)
                if c == 0:
                    head_sums(2 * KC - 1)
                if c == 2:
                    pe.wait_ge(S("lf_ready"), 1)
                    for t in range(3):
                        r = 128 if t < 2 else NS
                        m = pe.transpose(P[1][0:r, H * t:H * t + H], lf[:, 128 * t:128 * t + r], ident[0:H, 0:H])
                    m.then_inc(S("lf_mm"), 1)
                if c >= 1:
                    v_transposes(c - 1)
            v_transposes(KC - 1)

            arrived(pe, U_KC)
            for j in range(8):
                if j >= 2:
                    pe.wait_ge(S("kc_out"), j - 1)
                if j == 1:
                    pe.wait_ge(S("logf_tok"), 3)
                for c in range(4):
                    m = pe.transpose(P[j % 2][:, 128 * c:128 * c + 128],
                                     kc[:, j // 2, 512 * (j % 2) + 128 * c:512 * (j % 2) + 128 * c + 128], ident[:, :])
                m.then_inc(S("kc_mm"), 1)

            def scores(n):
                h, qt = n // 2, n % 2
                nk = 128 * (qt + 1)
                if n == 0:
                    pe.wait_ge(S("k_ready"), KC)
                    pe.wait_ge(S("q_ready"), KC)
                    pe.wait_ge(S("neg_ready"), 2)
                    pe.wait_ge(S("kc_out"), 8)
                if n >= 3:
                    pe.wait_ge(S("p_exp"), n - 2)
                b = P[n % 3]
                mm(b[:, 0:nk], qz[:, h, 128 * qt:128 * qt + 128], kT[:, h // 2, 0:nk], True, False)
                mm(b[:, 0:nk], ident[:, h:h + 1].to_broadcast([128, 128]), negp[:, 0:nk], False, False)
                mm(b[:, nk - 128:nk], ident[:, :], causal[:, :], False, True).then_inc(S("s_mm"), 1)

            def probs_T(n):
                pe.wait_ge(S("p_norm"), n + 1)
                if n >= 2:
                    pe.wait_ge(S("pt_out"), n - 1)
                for t in range(n % 2 + 1):
                    m = pe.transpose(P[3 + n % 2][:, 128 * t:128 * t + 128], Pp[:, n % 3, 128 * t:128 * t + 128], ident[:, :])
                m.then_inc(S("pt_mm"), 1)

            def values(n):
                h, qt = n // 2, n % 2
                c = h // 2
                pe.wait_ge(S("pt_out"), n + 1)
                if n % 4 == 0 and c >= 2:
                    pe.wait_ge(S("o_out"), c - 1)
                at = NP * (h % 2) + 128 * qt
                for t in range(qt + 1):
                    m = mm(P[5 + c % 2][:, at:at + 128], vtok[:, t, 128 * c:128 * c + 128],
                           PTp[:, n % 2, 128 * t:128 * t + 128], t == 0, t == qt)
                m.then_inc(S("pv_mm"), 1)

            NA = 2 * H
            pe.wait_ge(S("v_tok"), KC)
            for n in range(NA + 3):
                if n < NA:
                    scores(n)
                if 2 <= n < NA + 2:
                    probs_T(n - 2)
                if n >= 3:
                    values(n - 3)

            arrived(pe, U_VC)
            SB = [(0, 1), (2, 7)]

            def s_scores(j):
                if j >= 2:
                    pe.wait_ge(S("ps_exp"), j - 1)
                if j == 0:
                    pe.wait_ge(S("p_exp"), NA)
                b0, b1 = P[SB[j % 2][0]], P[SB[j % 2][1]]
                for a in range(2):
                    c = 2 * j + a
                    mm(b0[:, :].rearrange("p (t n) -> p t n", t=4), QS[:, c, :], kc[:, :, 128 * c:128 * c + 128], a == 0, False)
                    mm(b1[:, 0:NS], QS[:, c, :], kT[:, c, NP:TOK], a == 0, False)
                sel = sels[:, 4 * j:4 * j + 4, :].rearrange("p h n -> p (h n)")
                mm(b0[:, :], sel, negs[:, 0:PAST], False, True)
                mm(b1[:, 0:NS], sel, negs[:, PAST:PAST + NS], False, False)
                mm(b1[:, 0:NS], ident[:, :], causal_s[:, :], False, True).then_inc(S("ss_mm"), 1)

            def s_values(j):
                pe.wait_ge(S("ps_norm"), j + 1)
                if j >= 1:
                    pe.wait_ge(S("pts_out"), j)
                for t in range(5):
                    m = pe.transpose(P[3 + t // 4][:, 128 * (t % 4):128 * (t % 4) + 128], Ps[j % 2][:, 128 * t:128 * t + 128], ident[:, :])
                m.then_inc(S("pts_mm"), 1)
                pe.wait_ge(S("pts_out"), j + 1)
                if j == 0:
                    pe.wait_ge(S("o_out"), KC)
                if j >= 1:
                    pe.wait_ge(S("os_out"), j)
                for a in range(2):
                    c = 2 * j + a
                    for t in range(5):
                        v = vc[:, t, 128 * c:128 * c + 128] if t < 4 else vtok[:, 2, 128 * c:128 * c + 128]
                        m = mm(P[5][:, 64 * a:64 * a + 64], v, PTs[:, t, 64 * a:64 * a + 64], t == 0, t == 4)
                m.then_inc(S("pvs_mm"), 1)
                return m

            for j in range(5):
                if j < 4:
                    s_scores(j)
                if j >= 1:
                    m = s_values(j - 1)

            for d in range(KC):
                n = U_O + d // 4
                if d % 4 == 0:
                    arrived(pe, n)
                w = slot(n)[:, 0:4096].rearrange("p (k n) -> p k n", k=KC)
                if d == 0:
                    pe.wait_ge(S("os_out"), 4)
                if d >= 2:
                    pe.wait_ge(S("h2"), d - 1)
                for k in range(KC):
                    m = mm(P[d % 2][:, 0:TOK], w[:, k, 128 * (d % 4):128 * (d % 4) + 128], oT[:, k, :], k == 0, k == KC - 1)
                m.then_inc(S("wo_mm"), 1)
            for j in range(6):
                t, half = j // 2, j % 2
                r = 128 if t < 2 else NS
                pe.wait_ge(S("h2"), KC)
                if j >= 2:
                    pe.wait_ge(S("h_tok"), j - 1)
                for c in range(4):
                    m = pe.transpose(P[2 + j % 2][0:r, 128 * c:128 * c + 128], hT[:, 4 * half + c, 128 * t:128 * t + r], ident[:, :])
                m.then_inc(S("ht_mm"), 1)
            pe.wait_ge(S("wrg_ready"), 1)
            for t in range(3):
                r = 128 if t < 2 else NS
                for k in range(KC):
                    m = mm(P[4][0:r, NE * t:NE * t + NE], hT[:, k, 128 * t:128 * t + r], wrg[:, k, :], k == 0, k == KC - 1)
            m.then_inc(S("lg_mm"), 1)
            for j in range(6):
                t, half = j // 2, j % 2
                r = 128 if t < 2 else NS
                if j >= 2:
                    pe.wait_ge(S("k_tok"), j - 1)
                for c in range(4):
                    m = pe.transpose(P[5 + j % 2][0:r, 128 * c:128 * c + 128], kT[:, 4 * half + c, 128 * t:128 * t + r], ident[:, :])
                m.then_inc(S("kt_mm"), 1)
            pe.wait_ge(S("mask_ready"), 1)
            for t in range(3):
                for s in range(t + 1):
                    mm(P[7][:, NE * t:NE * t + NE], before[:, :] if s == t else ones[:, :], key[:, s, :], s == 0, s == t)
            for s in range(3):
                m = mm(P[7][:, 32:32 + NE], ones[:, :], key[:, s, :], s == 0, s == 2)
            m.then_inc(S("rank_mm"), 1)

            def gather(first, want_d, want_v):
                pe.wait_ge(S("dispatch"), want_d)
                pe.wait_ge(S("aux_dve"), want_v)
                b = P[5 + first // 4]
                for j in range(4):
                    c = first + j
                    for t in range(3):
                        m = mm(b[:, CAP * j:CAP * j + CAP], htok[:, t, 128 * c:128 * c + 128], Dx[:, t, :], t == 0, t == 2)
                m.then_inc(S("aux_pe"), 1)

            def expert(it, p):
                V = it * ITS + (E_AUXV + 2 * (p + 1))

                def gate_up(uu, q):
                    if uu == 0:
                        pe.wait_ge(S("first_lo"), it * 2 + (q + 1))
                    else:
                        pe.wait_ge(S("w_lo"), it * SPLITS + (E_LO + split_no(q, uu)))
                    if q == 0:
                        pe.wait_ge(S("e_hm"), it * BLK + (E_HM + uu - 1))
                    for k in range(4):
                        c = 4 * q + k
                        wh, wl = w_hi[:, q, 512 * k:512 * k + 512], w_lo[:, q, 512 * k:512 * k + 512]
                        m = products(P[uu % 2][:, :], three(xh[:, c, :], xl[:, c, :], wh, wl), c == 0, c == KC - 1)
                    m.then_inc(S("e_gb" if q else "e_ga"), 1)

                def turn(uu):
                    pe.wait_ge(S("e_hm"), it * BLK + (E_HM + uu + 1))
                    pe.wait_ge(S("e_htl"), it * BLK + (E_HTL + uu))
                    if uu == 0:
                        pe.wait_ge(S("aux_dve"), V)
                    for f in range(2):
                        m = pe.transpose(P[2][:, 128 * f:128 * f + 128], hm[:, uu % 2, 128 * f:128 * f + 128], ident[:, :])
                    m.then_inc(S("e_t"), 1)

                def down(uu):
                    pe.wait_ge(S("e_htl"), it * BLK + (E_HTL + uu + 1))
                    pe.wait_ge(S("w_lo"), it * SPLITS + (E_LO + split_no(2, uu)))
                    if uu == 0:
                        pe.wait_ge(S("e_y"), it * 2 + E_Y)
                    for f in range(2):
                        for half in range(2):
                            at = 1024 * f + 512 * half
                            wh, wl = w_hi[:, down_buf(uu), at:at + 512], w_lo[:, down_buf(uu), at:at + 512]
                            m = products(P[3 + half][:, :], three(hTh[:, uu % 2, f, :], hTl[:, uu % 2, f, :], wh, wl),
                                         uu == 0 and f == 0, uu == BLK - 1 and f == 1)
                    m.then_inc(S("e_dn"), 1)

                for uu in range(BLK):
                    if uu == 0:
                        pe.wait_ge(S("aux_dve"), V)
                    gate_up(uu, 0)
                    if uu == 0:
                        for t in range(3):
                            m = pe.transpose(P[7][0:CAP, 128 * t:128 * t + 128], Dg[:, t, :], ident[:, :])
                        m.then_inc(S("aux_pe"), 1)
                    else:
                        turn(uu - 1)
                    gate_up(uu, 1)
                    if uu >= 1:
                        down(uu - 1)
                turn(BLK - 1)
                gather(0, it + (E_D + 2 + p), V + 1)
                down(BLK - 1)
                gather(4, it + (E_D + 2 + p), V + 1)
                for i, (bank, emptied) in enumerate(((7, 1), (2, 1), (5, 2), (6, 3), (7, 4), (2, 5))):
                    half, t = i // 3, i % 3
                    r = 128 if t < 2 else NS
                    pe.wait_ge(S("aux_dve"), V + emptied)
                    pe.wait_ge(S("e_y"), it * 2 + (E_Y + 1 + half))
                    if bank == 2:
                        pe.wait_ge(S("e_htl"), it * BLK + (E_HTL + BLK))
                    mm(P[bank][0:r, :], DgT[:, 128 * t:128 * t + r], ytok[:, 512 * half:512 * half + 512], True, True)\
                        .then_inc(S("aux_pe"), 1)

            def first_gather(p):
                for first in (0, 4):
                    gather(first, NE * p + (E_D + 1 + p), NE * p * ITS + (E_AUXV + 2 * p))

            first_gather(0)
            with pe.Fori(0, NE) as e:
                expert(e, 0)
            pe.wait_ge(S("most_ready"), 1)
            n = pe.value_load(most_i[0:1, 0:1], min_val=0, max_val=TOK)
            for p in range(1, PASSES):
                with pe.If(n > p * CAP):
                    first_gather(p)
                    with pe.Fori(0, NE) as e:
                        expert(e + p * NE, p)

        @block.scalar
        def _(act):
            def squares(stage, src_sem):
                for c in range(KC):
                    act.wait_ge(S(src_sem), c + 1)
                    act.activation(sq[:, c, :], hT[:, c, :], ACT.Square).then_inc(S(stage + "_sq"), 1)

            def root(stage, bank, i):
                act.wait_ge(S(stage + "_ss"), 1)
                act.activation(rms[:, i, :], P[bank][:, 0:TOK], ACT.Sqrt, bias=eps[:, :], scale=1.0 / D)\
                    .then_inc(S(stage + "_rms"), 1)

            for dst, src in ((g_pool, ins["g_pool_norm"][0]), (p_scale, ins["pool_scale"][0]),
                             (g_ffn[:, 0], ins["g_ffn_norm"][0])):
                with nc.allow_non_contiguous_dma(reason="a gain for each feature, 4 KB"):
                    act.dma_start(dst[:, :], src.rearrange("(c p) -> p c", p=128)).then_inc(S("first_gains"), 16)
            act.wait_ge(S("const"), CONSTS)
            squares("n0", "xT")
            root("n0", 4, 0)

            def ffn_high(f):
                if f % 2 == 0:
                    arrived(act, U_GU + f // 2)
                if f >= 3:
                    act.wait_ge(S("ffn_gu"), f - 2)
                act.activation(ffn_part(w_hi, f), ffn_raw(f), ACT.Copy).then_inc(S("ffn_wh"), 1)

            for f in range(3):
                ffn_high(f)
            squares("n1", "pooled")
            root("n1", 0, 1)
            for c in range(KC):
                act.wait_ge(S("u32"), c + 1)
                act.activation(uh[:, c, :], u32[:, c, :], ACT.Copy).then_inc(S("u_high"), 1)
            for s in range(2):
                for half in range(2):
                    act.wait_ge(S("state_mm"), 2 * s + half + 1)
                    act.activation(st_out[:, s, 512 * half:512 * half + 512], P[[5, 6, 7, 4][2 * s + half]][0:HIST, :],
                                   ACT.Copy).then_inc(S("state_out"), 1)
            for f in range(FC):
                if 3 <= f + 2 < FC:
                    ffn_high(f + 2)
                act.wait_ge(S("ffn_gu"), f + 1)
                if f >= 2:
                    act.wait_ge(S("ffn_hm"), f - 1)
                act.activation(sg[:, f % 2, :], P[1 + 2 * (f % 3)][:, 0:TOK], ACT.Silu).then_inc(S("ffn_sg"), 1)
            squares("n2", "ffn_out")
            root("n2", 1, 0)
            act.wait_ge(S("cache_f"), 1)
            act.wait_ge(S("stored"), 32)
            act.activation(cat[:, 0:PAST], P[6][0:H, :], ACT.Copy).then_inc(S("cat_ready"), 1)

            def head_root(i):
                act.wait_ge(S("head_ss"), i + 1)
                if i >= 2:
                    act.wait_ge(S("head_rstd"), i - 1)
                act.activation(rms[:, i % 2, :], P[4 + i % 2][:, 0:TOK], ACT.Sqrt, bias=eps[:, :], scale=1.0 / HD)\
                    .then_inc(S("head_rms"), 1)

            act.wait_ge(S("n2_rstd"), 1)
            for i in range(2 * KC):
                act.wait_ge(S("raw"), i + 1)
                if i >= 2:
                    act.wait_ge(S("head_ss"), i - 1)
                act.activation(sqh[:, i % 2, :], raw[:, i % 2, :], ACT.Square).then_inc(S("head_sq"), 1)
                if i >= 1:
                    head_root(i - 1)
            head_root(2 * KC - 1)
            act.wait_ge(S("z_ready"), 2)
            act.activation(af, af, ACT.Exp, scale=-1.0).then_inc(S("f_exp"), 1)
            act.wait_ge(S("f_exp"), 1)
            act.activation(af, af, ACT.Ln, bias=one[0:H, :]).then_inc(S("f_ln"), 1)
            for j in range(8):
                act.wait_ge(S("kc_mm"), j + 1)
                act.activation(kc[:, j // 2, 512 * (j % 2):512 * (j % 2) + 512], P[j % 2][:, :], ACT.Copy)\
                    .then_inc(S("kc_out"), 1)
            for n in range(2 * H):
                act.wait_ge(S("p_max"), n + 1)
                if n >= 3:
                    act.wait_ge(S("pt_mm"), n - 2)
                nk = 128 * (n % 2 + 1)
                act.activation(Pp[:, n % 3, 0:nk], P[n % 3][:, 0:nk], ACT.Exp, bias=stat[:, n % 3:n % 3 + 1],
                               accum_out=stat[:, 4 + n % 3:5 + n % 3]).then_inc(S("p_exp"), 1)
            for j in range(4):
                act.wait_ge(S("ps_max"), j + 1)
                if j >= 2:
                    act.wait_ge(S("pts_mm"), j - 1)
                b0, b1 = [(0, 1), (2, 7)][j % 2]
                nm = stat[:, 16 + 8 * (j % 2):17 + 8 * (j % 2)]
                act.activation(Ps[j % 2][:, 0:PAST], P[b0][:, :], ACT.Exp, bias=nm,
                               accum_out=stat[:, 17 + 8 * (j % 2):18 + 8 * (j % 2)]).then_inc(S("ps_exp_a"), 1)
                act.activation(Ps[j % 2][:, PAST:PAST + NS], P[b1][:, 0:NS], ACT.Exp, bias=nm,
                               accum_out=stat[:, 18 + 8 * (j % 2):19 + 8 * (j % 2)]).then_inc(S("ps_exp"), 1)
            act.wait_ge(S("htok_zero"), 1)
            for j in range(6):
                t, half = j // 2, j % 2
                r = 128 if t < 2 else NS
                act.wait_ge(S("ht_mm"), j + 1)
                act.activation(htok[0:r, t, 512 * half:512 * half + 512], P[2 + j % 2][0:r, :], ACT.Copy)\
                    .then_inc(S("h_tok"), 1)
            act.wait_ge(S("h_tok"), 6)
            for t in range(3):
                act.activation(acc[:, t, :], htok[:, t, :], ACT.Square, accum_out=tv[:, 0, t:t + 1])\
                    .then_inc(S("row_ss"), 1)
            act.wait_ge(S("row_ss"), 3)
            act.activation(tv[:, 1, :], tv[:, 0, :], ACT.Sqrt, bias=eps[:, :], scale=1.0 / D).then_inc(S("row_rms"), 1)
            for t in range(3):
                act.activation(acc[:, t, :], htok[:, t, :], ACT.Copy).then_inc(S("acc_init"), 1)
            for j in range(6):
                t, half = j // 2, j % 2
                r = 128 if t < 2 else NS
                act.wait_ge(S("kt_mm"), j + 1)
                act.activation(kout[t][0:r, 512 * half:512 * half + 512], P[5 + j % 2][0:r, :], ACT.Copy)\
                    .then_inc(S("k_tok"), 1)
            act.wait_ge(S("top2"), 1)
            act.activation(tv[:, 4, :], tv[:, 3, :], ACT.Exp).then_inc(S("e2_ready"), 1)
            act.wait_ge(S("k_stored"), 48)

            def rows_high(first, want_p):
                act.wait_ge(S("aux_pe"), want_p)
                for c in range(first, first + 4):
                    m = act.activation(xh[:, c, :], P[5 + first // 4][:, CAP * (c % 4):CAP * (c % 4) + CAP], ACT.Copy,
                                       scale=g_ffn[:, 1, c:c + 1])
                m.then_inc(S("e_xh"), 1)

            def expert(it, p):
                A = it * ITS + (E_AUXP + 2 * (p + 1))

                def high(q, uu):
                    if q == 0 or (q == 2 and uu == 0):
                        exp_arrived(act, it, uu)
                    if q == 0:
                        act.wait_ge(S("e_ga"), it * BLK + (E_GA + uu))
                    elif q == 1 or uu == BLK - 1:
                        act.wait_ge(S("e_gb"), it * BLK + (E_GB + (uu if q == 1 else BLK)))
                    else:
                        act.wait_ge(S("e_dn"), it * BLK + (E_DN + uu))
                    s, w = EXP_SLOT[uu], 2048 * q
                    buf = down_buf(uu) if q == 2 else q
                    act.activation(w_hi[:, buf, :], ring[:, s, w:w + 2048], ACT.Copy).then_inc(S("w_hi"), 1)

                def hidden_high(uu):
                    act.wait_ge(S("e_t"), it * BLK + (E_T + uu + 1))
                    act.wait_ge(S("e_dn"), it * BLK + (E_DN + uu - 1 if uu >= 1 else E_DN))
                    act.activation(hTh[:, uu % 2].rearrange("p f n -> p (f n)"), P[2][:, 0:256], ACT.Copy)\
                        .then_inc(S("e_hth"), 1)

                act.activation(silu_scratch[:, :], one[:, :], ACT.Silu)
                for uu in range(BLK):
                    if uu >= 1:
                        hidden_high(uu - 1)
                    if uu < BLK - 1:
                        high(0, uu + 1)
                    act.wait_ge(S("e_gb"), it * BLK + (E_GB + uu + 1))
                    act.wait_ge(S("e_hm"), it * BLK + (E_HM + uu - 1))
                    act.activation(sl[:, uu % 2, :], P[uu % 2][:, 0:256], ACT.Silu).then_inc(S("e_silu"), 1)
                    if uu < BLK - 1:
                        high(1, uu + 1)
                    high(2, uu)
                hidden_high(BLK - 1)
                rows_high(0, A + 2)
                act.wait_ge(S("e_dn"), it * BLK + (E_DN + BLK))
                act.wait_ge(S("aux_pe"), A)
                for half in range(2):
                    act.activation(ytok[:, 512 * half:512 * half + 512], P[3 + half][:, :], ACT.Copy)\
                        .then_inc(S("e_y"), 1)
                rows_high(4, A + 3)

            def first_rows(p):
                for i in range(2):
                    rows_high(4 * i, NE * p * ITS + (E_AUXP + 2 * p + i + 1))

            first_rows(0)
            with act.Fori(0, NE) as e:
                expert(e, 0)
            act.wait_ge(S("most_ready"), 1)
            n = act.value_load(most_i[0:1, 0:1], min_val=0, max_val=TOK)
            for p in range(1, PASSES):
                with act.If(n > p * CAP):
                    first_rows(p)
                    with act.Fori(0, NE) as e:
                        expert(e + p * NE, p)

        @block.vector
        def _(dve):
            def then(ins, name):
                chain[name] = chain.get(name, 0) + 1
                ins.then_inc(S(name), 1)
                dve.wait_ge(S(name), chain[name])

            chain = {}
            dve.wait_ge(S("const"), CONSTS)
            then(dve.reciprocal(inv_cnt[:, :], counts[:, :]), "dve_setup")
            then(dve.tensor_copy(sels[:, :, :], ident[:, 0:H].unsqueeze(2).to_broadcast([128, H, NS])), "dve_setup")
            for name, v in (("e_ga", E_GA), ("e_gb", E_GB), ("e_t", E_T), ("e_dn", E_DN), ("e_silu", E_SILU), ("e_hm", E_HM),
                            ("e_hth", E_HTH), ("e_htl", E_HTL), ("w_hi", E_HI), ("w_lo", E_LO), ("e_xh", E_XH),
                            ("e_y", E_Y), ("dispatch", E_D), ("aux_pe", E_AUXP), ("aux_dve", E_AUXV)):
                dve.sem_inc(S(name), v)
            for c in range(KC):
                dve.wait_ge(S("xT_mm"), c + 1)
                dve.tensor_copy(hT[:, c, :], P[c % 4][:, 0:TOK]).then_inc(S("xT_a"), 1)
                dve.tensor_copy(U[:, c, HIST + NP:2 * HIST + NP], P[c % 4][:, TOK:TOK + HIST]).then_inc(S("xT"), 1)
            dve.memset(U[:, :, 0:HIST], 0.0).then_inc(S("U_hist"), 1)
            dve.wait_ge(S("U_hist"), 1)

            def inverse(stage, i):
                dve.wait_ge(S(stage + "_rms"), 1)
                dve.reciprocal(rstd[:, i, :], rms[:, i, :]).then_inc(S(stage + "_rstd"), 1)
                dve.wait_ge(S(stage + "_rstd"), 1)

            dve.wait_ge(S("first_gains"), 48)
            inverse("n0", 0)
            for c in (6, 7, 0, 1, 2, 3, 4, 5):
                dve.scalar_tensor_tensor(U[:, c, HIST:HIST + NP], hT[:, c, 0:NP], g_pool[:, c:c + 1],
                                         rstd[:, 0, 0:NP], ALU.mult, ALU.mult).then_inc(S("U"), 1)
                dve.scalar_tensor_tensor(U[:, c, 2 * HIST + NP:UW], hT[:, c, NP:TOK], g_pool[:, c:c + 1],
                                         rstd[:, 0, NP:TOK], ALU.mult, ALU.mult).then_inc(S("U"), 1)
            dve.wait_ge(S("U"), 2 * KC)

            def differences(g, win, w):
                cs = slice(2 * g, 2 * g + 2)
                dve.scalar_tensor_tensor(diff[:, cs, 0:NP], win[:, :, HIST:HIST + NP], 1.0 / w, U[:, cs, HIST:HIST + NP],
                                         ALU.mult, ALU.subtract).then_inc(S("diff_a"), 1)
                dve.scalar_tensor_tensor(diff[:, cs, NP:TOK], win[:, :, 2 * HIST + NP:UW], 1.0 / w,
                                         U[:, cs, 2 * HIST + NP:UW], ALU.mult, ALU.subtract).then_inc(S("diff_a"), 1)
                dve.wait_ge(S("diff_a"), 3 * g + 2)
                dve.tensor_tensor(diff[:, cs, 0:w - 1], win[:, :, HIST:HIST + w - 1],
                                  inv_cnt[:, 0:w - 1].unsqueeze(1).to_broadcast([128, 2, w - 1]), ALU.mult)\
                    .then_inc(S("diff_a"), 1)
                dve.wait_ge(S("diff_a"), 3 * g + 3)
                dve.tensor_tensor(diff[:, cs, 0:w - 1], diff[:, cs, 0:w - 1], U[:, cs, HIST:HIST + w - 1],
                                  ALU.subtract).then_inc(S("diff"), 1)

            then(dve.tensor_tensor(winA[:, 0:6, 1:UW], U[:, 0:6, 1:UW], U[:, 0:6, 0:UW - 1], ALU.add), "win")
            differences(0, winA[:, 0:2], 2)
            then(dve.tensor_tensor(winB[:, 0:4, 3:UW], winA[:, 2:6, 3:UW], winA[:, 2:6, 1:UW - 2], ALU.add), "win")
            differences(1, winB[:, 0:2], 4)
            then(dve.tensor_tensor(winA[:, 4:6, 7:UW], winB[:, 2:4, 7:UW], winB[:, 2:4, 3:UW - 4], ALU.add), "win")
            differences(2, winA[:, 4:6], 8)
            dve.wait_ge(S("win3"), 4)
            differences(3, winB[:, 4:6], 16)

            def ffn_low(f):
                dve.wait_ge(S("ffn_wh"), f + 1)
                dve.tensor_tensor(ffn_part(w_lo, f), ffn_raw(f), ffn_part(w_hi, f).bitcast(F32), ALU.subtract)\
                    .then_inc(S("ffn_wl"), 1)

            for c in range(KC):
                dve.wait_ge(S("pool_mm"), c + 1)
                dve.scalar_tensor_tensor(hT[:, c, :], P[c % 4][:, 0:TOK], p_scale[:, c:c + 1], hT[:, c, :],
                                         ALU.mult, ALU.add).then_inc(S("pooled"), 1)
                if c == 1:
                    ffn_low(0)
            dve.wait_ge(S("pooled"), KC)

            def normed(dst, g, i, name):
                for c in range(KC):
                    dve.scalar_tensor_tensor(dst[:, c, :], hT[:, c, :], g[:, c:c + 1], rstd[:, i, :],
                                             ALU.mult, ALU.mult).then_inc(S(name), 1)

            inverse("n1", 1)
            for c in range(KC + 1):
                if c < KC:
                    dve.scalar_tensor_tensor(u32[:, c, :], hT[:, c, :], g_ffn[:, 0, c:c + 1], rstd[:, 1, :],
                                             ALU.mult, ALU.mult).then_inc(S("u32"), 1)
                if c >= 1:
                    dve.wait_ge(S("u_high"), c)
                    dve.tensor_tensor(ul[:, c - 1, :], u32[:, c - 1, :], uh[:, c - 1, :].bitcast(F32), ALU.subtract)\
                        .then_inc(S("u_ffn"), 1)
            dve.wait_ge(S("u_ffn"), KC)
            ffn_low(1)
            ffn_low(2)
            dve.wait_ge(S("state_mm"), 4)
            for f in range(FC):
                if 3 <= f + 2 < FC:
                    ffn_low(f + 2)
                dve.wait_ge(S("ffn_sg"), f + 1)
                dst = hmA[:, f, :] if f < 10 else hmB[:, f - 10, :]
                dve.tensor_tensor(dst, sg[:, f % 2, :], P[2 + 2 * (f % 3)][:, 0:TOK], ALU.mult).then_inc(S("ffn_hm"), 1)
            for d in range(KC):
                dve.wait_ge(S("ffn_dn"), d + 1)
                dve.tensor_tensor(hT[:, d, :], hT[:, d, :], P[7 if d % 2 == 0 else 0][:, 0:TOK], ALU.add)\
                    .then_inc(S("ffn_out"), 1)
            dve.wait_ge(S("ffn_out"), KC)
            dve.wait_ge(S("gains_in"), 176)
            then(dve.tensor_scalar(gq8[:, :], gq[:, :], HD ** -0.5, None, ALU.mult), "dve_setup")
            inverse("n2", 0)
            normed(uq, g_attn, 0, "u_q")
            normed(u, g_kv, 0, "u_kv")
            dve.wait_ge(S("u_kv"), KC)
            dve.wait_ge(S("qz_zero"), 2)
            dve.wait_ge(S("zeros"), 3)

            def head_norm(i):
                c = i % KC
                dve.wait_ge(S("head_rms"), i + 1)
                dve.reciprocal(rstd[:, i % 2, :], rms[:, i % 2, :]).then_inc(S("head_rstd"), 1)
                dve.wait_ge(S("head_rstd"), i + 1)
                r = raw[:, i % 2, :]
                if i < KC:
                    for a in range(2):
                        ps = slice(64 * a, 64 * a + 64)
                        q4 = 32 * (2 * (c % 2) + a)
                        dve.scalar_tensor_tensor(qz[ps, 2 * c + a, :], r[ps, :], gq8[ps, :], rstd[ps, i % 2, :],
                                                 ALU.mult, ALU.mult).then_inc(S("q_a"), 1)
                        m = dve.scalar_tensor_tensor(QS[ps, c, q4:q4 + NS], r[ps, NP:TOK], gq8[ps, :],
                                                     rstd[ps, i % 2, NP:TOK], ALU.mult, ALU.mult)
                    m.then_inc(S("q_ready"), 1)
                    dve.wait_ge(S("q_ready"), c + 1)
                else:
                    dve.scalar_tensor_tensor(kT[:, c, :], r, gk[:, :], rstd[:, i % 2, :], ALU.mult, ALU.mult)\
                        .then_inc(S("k_ready"), 1)
                    dve.wait_ge(S("k_ready"), c + 1)

            def v_rows(c):
                dve.wait_ge(S("vt_mm"), c + 1)
                b = P[6 + c % 2]
                dve.tensor_copy(vtok[:, 0:2, 128 * c:128 * c + 128], b[:, 0:256].rearrange("p (t n) -> p t n", t=2))
                dve.tensor_copy(vtok[0:NS, 2, 128 * c:128 * c + 128], b[0:NS, 256:384]).then_inc(S("v_tok"), 1)

            for i in range(3 * KC):
                dve.wait_ge(S("proj_mm"), i + 1)
                if i >= 2 * KC + 2:
                    dve.wait_ge(S("vt_mm"), i - 2 * KC - 1)
                elif i >= 2:
                    dve.wait_ge(S("head_sq"), i - 1)
                dve.tensor_copy(raw[:, i % 2, :], P[2 + i % 2][:, 0:TOK]).then_inc(S("raw"), 1)
                if 1 <= i <= 2 * KC:
                    dve.wait_ge(S("raw"), i)
                    head_norm(i - 1)
                if i == KC:
                    dve.wait_ge(S("f_mm"), 1)
                    dve.tensor_scalar(zf, P[7][0:H, 0:TOK], bf[:, :], None, ALU.add).then_inc(S("z_ready"), 1)
                    dve.wait_ge(S("z_ready"), 1)
                    dve.scalar_tensor_tensor(af, zf, -1.0, zf, ALU.mult, ALU.max).then_inc(S("z_ready"), 1)
                if i == 2 * KC + 1:
                    dve.wait_ge(S("f_ln"), 1)
                    dve.scalar_tensor_tensor(lf, zf, 0.0, af, ALU.min, ALU.subtract).then_inc(S("lf_ready"), 1)
                    dve.wait_ge(S("lf_ready"), 1)
                    dve.wait_ge(S("cat_ready"), 1)
                    then(dve.tensor_copy(cat[:, PAST:PAST + NS], lf[:, NP:TOK]), "cum")
                    zero = lambda n: ones[0:H, 0:1].to_broadcast([H, n])
                    then(dve.tensor_tensor_scan(negp[0:H, :], zero(NP), lf[:, 0:NP], 0.0, ALU.mult, ALU.add), "cum")
                    then(dve.tensor_tensor_scan(negs[0:H, :], zero(PAST + NS), cat, 0.0, ALU.mult, ALU.add), "cum")
                    dve.tensor_scalar(negp[0:H, :], negp[0:H, :], -1.0, None, ALU.mult).then_inc(S("neg_ready"), 1)
                    dve.tensor_scalar(negs[0:H, :], negs[0:H, :], -1.0, None, ALU.mult).then_inc(S("neg_ready"), 1)
                if i == 2 * KC + 3:
                    dve.wait_ge(S("lf_mm"), 1)
                    for t in range(3):
                        r = 128 if t < 2 else NS
                        dve.tensor_copy(lo[0:r, t, :], P[1][0:r, H * t:H * t + H]).then_inc(S("logf_tok"), 1)
                if i == 2 * KC + 1:
                    dve.wait_ge(S("v_zero"), 1)
                if i >= 2 * KC + 1:
                    v_rows(i - 2 * KC - 1)
            v_rows(KC - 1)

            def negmax(n):
                nk = 128 * (n % 2 + 1)
                dve.wait_ge(S("s_mm"), n + 1)
                if n >= 3:
                    dve.wait_ge(S("p_exp"), n - 2)
                then(dve.reduce_max(stat[:, 8 + n % 3:9 + n % 3], P[n % 3][:, 0:nk], AX.X), "max_a")
                dve.tensor_scalar(stat[:, n % 3:n % 3 + 1], stat[:, 8 + n % 3:9 + n % 3], -1.0, None, ALU.mult)\
                    .then_inc(S("p_max"), 1)

            def norm_p(n):
                nk = 128 * (n % 2 + 1)
                dve.wait_ge(S("p_exp"), n + 1)
                then(dve.reciprocal(stat[:, 12 + n % 3:13 + n % 3], stat[:, 4 + n % 3:5 + n % 3]), "max_a")
                dve.tensor_scalar(Pp[:, n % 3, 0:nk], Pp[:, n % 3, 0:nk], stat[:, 12 + n % 3:13 + n % 3], None, ALU.mult)\
                    .then_inc(S("p_norm"), 1)

            def copy_pt(n):
                nk = 128 * (n % 2 + 1)
                dve.wait_ge(S("pt_mm"), n + 1)
                if n >= 2:
                    dve.wait_ge(S("pv_mm"), n - 1)
                dve.tensor_copy(PTp[:, n % 2, 0:nk], P[3 + n % 2][:, 0:nk]).then_inc(S("pt_out"), 1)

            def copy_o(c):
                dve.wait_ge(S("pv_mm"), 4 * c + 4)
                for a in range(2):
                    m = dve.tensor_copy(oT[64 * a:64 * a + 64, c, 0:NP], P[5 + c % 2][64 * a:64 * a + 64, NP * a:NP * a + NP])
                m.then_inc(S("o_out"), 1)

            NA = 2 * H
            for n in range(NA + 3):
                if n < NA:
                    negmax(n)
                if 1 <= n <= NA:
                    norm_p(n - 1)
                if 2 <= n < NA + 2:
                    copy_pt(n - 2)
                if n >= 3 and (n - 3) % 4 == 3:
                    copy_o((n - 3) // 4)
            for i in range(2):
                then(dve.memset(Ps[i][:, PAST + NS:640], 0.0), "max_a")

            def s_negmax(j):
                st = 16 + 8 * (j % 2)
                b0, b1 = [(0, 1), (2, 7)][j % 2]
                dve.wait_ge(S("ss_mm"), j + 1)
                if j >= 2:
                    dve.wait_ge(S("ps_exp"), j - 1)
                then(dve.reduce_max(stat[:, st + 3:st + 4], P[b0][:, :], AX.X), "max_a")
                then(dve.reduce_max(stat[:, st + 4:st + 5], P[b1][:, 0:NS], AX.X), "max_a")
                then(dve.tensor_tensor(stat[:, st + 5:st + 6], stat[:, st + 3:st + 4], stat[:, st + 4:st + 5], ALU.max), "max_a")
                dve.tensor_scalar(stat[:, st:st + 1], stat[:, st + 5:st + 6], -1.0, None, ALU.mult).then_inc(S("ps_max"), 1)

            def s_norm(j):
                st = 16 + 8 * (j % 2)
                dve.wait_ge(S("ps_exp"), j + 1)
                then(dve.tensor_tensor(stat[:, st + 6:st + 7], stat[:, st + 1:st + 2], stat[:, st + 2:st + 3], ALU.add), "max_a")
                then(dve.reciprocal(stat[:, st + 7:st + 8], stat[:, st + 6:st + 7]), "max_a")
                dve.tensor_scalar(Ps[j % 2][:, 0:PAST + NS], Ps[j % 2][:, 0:PAST + NS], stat[:, st + 7:st + 8], None, ALU.mult)\
                    .then_inc(S("ps_norm"), 1)

            def s_copy(j):
                dve.wait_ge(S("pts_mm"), j + 1)
                if j >= 1:
                    dve.wait_ge(S("pvs_mm"), j)
                dve.tensor_copy(PTs[:, 0:4, :].rearrange("p t n -> p (t n)"), P[3][:, :])
                dve.tensor_copy(PTs[:, 4, :], P[4][:, 0:128]).then_inc(S("pts_out"), 1)
                dve.wait_ge(S("pvs_mm"), j + 1)
                for a in range(2):
                    c = 2 * j + a
                    for b in range(2):
                        m = dve.tensor_copy(oT[64 * b:64 * b + 64, c, NP:TOK],
                                            P[5][64 * b:64 * b + 64, 64 * a + 32 * b:64 * a + 32 * b + 32])
                m.then_inc(S("os_out"), 1)

            for j in range(5):
                if j < 4:
                    s_negmax(j)
                if j >= 1:
                    s_copy(j - 1)
                if j < 4:
                    s_norm(j)
            for k in range(KC):
                m = dve.tensor_scalar(wrg[:, k, :], wr[:, k, :], g_ffn[:, 1, k:k + 1], None, ALU.mult)
            m.then_inc(S("wrg_ready"), 1)
            for d in range(KC):
                dve.wait_ge(S("wo_mm"), d + 1)
                dve.tensor_tensor(hT[:, d, :], hT[:, d, :], P[d % 2][:, 0:TOK], ALU.add).then_inc(S("h2"), 1)

            R = "route"
            then(dve.memset(lg[:, :, :], 0.0), R)
            dve.wait_ge(S("row_rms"), 1)
            then(dve.reciprocal(rs_tok[:, :], tv[:, 1, :]), R)
            dve.wait_ge(S("lg_mm"), 1)
            for t in range(3):
                r = 128 if t < 2 else NS
                then(dve.tensor_scalar(lg[0:r, t, :], P[4][0:r, NE * t:NE * t + NE], rs_tok[0:r, t:t + 1], None, ALU.mult), R)
            bc = lambda a: a.unsqueeze(2).to_broadcast([128, 3, NE])

            def largest(src, mask, i):
                then(dve.tensor_reduce(tv[:, i, :], src, AX.X, ALU.max), R)
                then(dve.tensor_tensor(key[:, :, :], src, bc(tv[:, i, :]), ALU.is_equal), R)
                then(dve.tensor_tensor(key[:, :, :], key[:, :, :], desc[:, :, :], ALU.mult), R)
                then(dve.tensor_reduce(tv[:, 7, :], key[:, :, :], AX.X, ALU.max), R)
                then(dve.tensor_tensor(mask, key[:, :, :], bc(tv[:, 7, :]), ALU.is_equal), R)

            largest(lg[:, :, :], m1[:, :, :], 5)
            then(dve.scalar_tensor_tensor(l2[:, :, :], m1[:, :, :], NEG, lg[:, :, :], ALU.mult, ALU.add), R)
            largest(l2[:, :, :], m2[:, :, :], 6)
            then(dve.tensor_tensor(tv[:, 3, :], tv[:, 6, :], tv[:, 5, :], ALU.subtract), R)
            dve.sem_inc(S("top2"), 1)
            bv = bc(valid[:, :])
            then(dve.tensor_tensor(m1[:, :, :], m1[:, :, :], bv, ALU.mult), R)
            then(dve.tensor_tensor(m2[:, :, :], m2[:, :, :], bv, ALU.mult), R)
            dve.tensor_tensor(key[:, :, :], m1[:, :, :], m2[:, :, :], ALU.add).then_inc(S("mask_ready"), 1)
            dve.wait_ge(S("mask_ready"), 1)
            dve.wait_ge(S("e2_ready"), 1)
            then(dve.tensor_scalar(tv[:, 2, :], tv[:, 4, :], 1.0, None, ALU.add), R)
            then(dve.reciprocal(tv[:, 5, :], tv[:, 2, :]), R)
            then(dve.tensor_tensor(tv[:, 6, :], tv[:, 4, :], tv[:, 5, :], ALU.mult), R)
            then(dve.tensor_tensor(m1[:, :, :], m1[:, :, :], bc(tv[:, 5, :]), ALU.mult), R)
            then(dve.tensor_tensor(m2[:, :, :], m2[:, :, :], bc(tv[:, 6, :]), ALU.mult), R)
            ge = gate[:, 0:NE, :].rearrange("p e t -> p t e")
            rk = rank[:, 0:NE, :].rearrange("p e t -> p t e")
            then(dve.memset(rank[:, NE, :], -1.0), R)
            then(dve.memset(gate[:, NE, :], 0.0), R)
            then(dve.tensor_tensor(ge, m1[:, :, :], m2[:, :, :], ALU.add), R)
            dve.wait_ge(S("rank_mm"), 1)
            then(dve.scalar_tensor_tensor(l2[:, :, :], P[7][:, 0:3 * NE].rearrange("p (t e) -> p t e", t=3), 1.0,
                                          key[:, :, :], ALU.add, ALU.mult), R)
            then(dve.tensor_scalar(rk, l2[:, :, :], -1.0, None, ALU.add), R)
            then(dve.reduce_max(most[:, :], P[7][:, 32:32 + NE], AX.X), R)
            dve.tensor_copy(most_i[:, :], most[:, :]).then_inc(S("most_ready"), 1)

            def rows_low(first, want_h):
                dve.wait_ge(S("e_xh"), want_h)
                for c in range(first, first + 4):
                    m = dve.scalar_tensor_tensor(xl[:, c, :], P[5 + first // 4][:, CAP * (c % 4):CAP * (c % 4) + CAP],
                                                 g_ffn[:, 1, c:c + 1], xh[:, c, :].bitcast(F32), ALU.mult, ALU.subtract)
                m.then_inc(S("aux_dve"), 1)

            def expert(e, it, p):
                A, XH = it * ITS + (E_AUXP + 2 * (p + 1)), it * 2 + (E_XH + 2 * (p + 1))

                def low(q, uu):
                    dve.wait_ge(S("w_hi"), it * SPLITS + (E_HI + split_no(q, uu)))
                    s, w = EXP_SLOT[uu], 2048 * q
                    buf = down_buf(uu) if q == 2 else q
                    dve.tensor_tensor(w_lo[:, buf, :], ring[:, s, w:w + 2048], w_hi[:, buf, :].bitcast(F32), ALU.subtract)\
                        .then_inc(S("w_lo"), 1)

                def hidden_low(uu):
                    dve.wait_ge(S("e_hth"), it * BLK + (E_HTH + uu + 1))
                    dve.tensor_tensor(hTl[:, uu % 2].rearrange("p f n -> p (f n)"), P[2][:, 0:256],
                                      hTh[:, uu % 2].rearrange("p f n -> p (f n)").bitcast(F32), ALU.subtract)\
                        .then_inc(S("e_htl"), 1)

                for uu in range(BLK):
                    if uu == BLK - 1:
                        dispatch_next(e, it, p)
                    if uu == 0:
                        dve.wait_ge(S("aux_pe"), A + 1)
                        dve.tensor_copy(DgT[:, :], P[7][0:CAP, 0:384]).then_inc(S("aux_dve"), 1)
                    else:
                        hidden_low(uu - 1)
                    if uu < BLK - 1:
                        low(0, uu + 1)
                    dve.wait_ge(S("e_silu"), it * BLK + (E_SILU + uu + 1))
                    dve.wait_ge(S("e_t"), it * BLK + (E_T + uu - 1))
                    dve.tensor_tensor(hm[:, uu % 2, :], sl[:, uu % 2, :], P[uu % 2][:, 256:512], ALU.mult)\
                        .then_inc(S("e_hm"), 1)
                    if uu < BLK - 1:
                        low(1, uu + 1)
                    low(2, uu)
                hidden_low(BLK - 1)
                for i in range(2):
                    rows_low(4 * i, XH + (i + 1))
                for i, bank in enumerate((7, 2, 5, 6, 7, 2)):
                    half, t = i // 3, i % 3
                    r = 128 if t < 2 else NS
                    dve.wait_ge(S("aux_pe"), A + (i + 4))
                    a = acc[0:r, t, 512 * half:512 * half + 512]
                    dve.tensor_tensor(a, a, P[bank][0:r, :], ALU.add).then_inc(S("aux_dve"), 1)

            def first_rows(p):
                for i in range(2):
                    rows_low(4 * i, NE * p * 2 + (E_XH + 2 * p + i + 1))

            def make(e, want_aux, want_cur, wait_read):
                dve.wait_ge(S("aux_pe"), want_aux)
                dve.wait_ge(S("dispatch"), wait_read)
                dve.tensor_copy(cur[:, 0:3], rank[:, bass.ds(e, 1), :].rearrange("p a t -> p (a t)")).then_inc(S("cur"), 1)
                dve.tensor_copy(cur[:, 3:6], gate[:, bass.ds(e, 1), :].rearrange("p a t -> p (a t)")).then_inc(S("cur"), 1)
                dve.wait_ge(S("cur"), want_cur)
                for t in range(3):
                    dve.tensor_scalar(Dg[:, t, :], slots_iota[:, :], cur[:, t:t + 1], cur[:, 3 + t:4 + t],
                                      ALU.is_equal, ALU.mult)
                for t in range(3):
                    m = dve.tensor_scalar(Dx[:, t, :], slots_iota[:, :], cur[:, t:t + 1], rs_tok[:, t:t + 1],
                                          ALU.is_equal, ALU.mult)
                m.then_inc(S("dispatch"), 1)

            def dispatch_next(e, it, p):
                make(e + 1, it * ITS + (E_AUXP + 2 * (p + 1) + 1), it * 2 + (4 + 2 * p), it + (E_D + 1 + p))

            make(0, E_AUXP, 2, E_D)
            first_rows(0)
            with dve.Fori(0, NE) as e:
                expert(e, e, 0)
            n = dve.value_load(most_i[0:1, 0:1], min_val=0, max_val=TOK)
            for p in range(1, PASSES):
                with dve.If(n > p * CAP):
                    dve.wait_ge(S("cur"), 18 * p)
                    dve.tensor_scalar(rank[:, :, :], rank[:, :, :], -float(CAP), None, ALU.add).then_inc(S("pass"), 1)
                    dve.wait_ge(S("pass"), p)
                    make(0, NE * p * ITS + (E_AUXP + 2 * p), 18 * p + 2, NE * p + (E_D + p))
                    first_rows(p)
                    with dve.Fori(0, NE) as e:
                        expert(e, e + p * NE, p)
            dve.drain().then_inc(S("acc_done"), 1)

        assert len(sems) < 200, len(sems)


_INS = ["x_prompt", "x_sample", "state_pool", "cache_k", "cache_v", "cache_logf", "g_pool_norm", "w_pool",
        "pool_scale", "g_kv_norm", "w_kvf", "b_f", "g_k", "g_attn_norm", "w_q", "g_q", "w_o", "g_ffn_norm",
        "w_ffn_gu", "w_ffn_down", "w_router", "w_moe_gu", "w_moe_down"]
_OUTS = [("y_prompt", (1, 256, 1024)), ("y_sample", (1, 32, 1024)), ("state_prompt", (1, 1, 15, 1024)),
         ("k_prompt", (1, 256, 16, 64)), ("v_prompt", (1, 256, 16, 64)), ("logf_prompt", (1, 256, 16)),
         ("state_sample", (1, 1, 15, 1024)), ("k_sample", (1, 32, 16, 64)), ("v_sample", (1, 32, 16, 64)),
         ("logf_sample", (1, 32, 16))]


def kernel(**inputs):
    import numpy as _np
    import concourse.bacc as _bacc
    from concourse import mybir as _mybir
    from concourse.bass_utils import run_bass_kernel_spmd as _run

    nc = _bacc.Bacc("TRN2", target_bir_lowering=False, num_devices=1, dynamic_dma_scratch_size=4096)
    arrays, ins, outs = {}, {}, {}
    for name in _INS:
        a = _np.ascontiguousarray(inputs[name])
        arrays[f"in_{name}"] = a
        ins[name] = nc.dram_tensor(f"in_{name}", a.shape, _mybir.dt.from_np(a.dtype), kind="ExternalInput").ap()
    for name, shape in _OUTS:
        outs[name] = nc.dram_tensor(f"out_{name}", shape, _mybir.dt.float32, kind="ExternalOutput").ap()
    build_program(nc, ins, outs)
    r = _run(nc, [arrays], core_ids=[0])
    return tuple(r.results[0][f"out_{name}"] for name, _ in _OUTS)
```

```python
import concourse.bass as bass
from concourse import mybir
from contextlib import ExitStack

D = 1024
FF = 2816
NP, NS = 256, 32
TOK = NP + NS
PAST = 512
HIST = 15
H, HD = 16, 64
NE = 8
CAP = 128
PASSES = -(-TOK // CAP)
KC = D // 128
FC = FF // 128
BLK = FC // 2
DN_PARTS = ((0, 4), (4, 8), (8, BLK))
SPLITS = 3 * BLK - 2
EPS = 1e-6
NEG = -1.0e30

SLOTS = 4
SLOT = 6144
U_POOL = 0
U_GU = 1
U_DN = U_GU + BLK
U_Q = U_DN + 4
U_KV = U_Q + 2
U_KC = U_KV + 4
U_VC = U_KC + 1
U_O = U_VC + 1
U_MOE = U_O + 2
EXP_SLOT = [(U_MOE + u) % SLOTS for u in range(BLK)]


def earlier_user(u):
    same = [v for v in range(-BLK, u) if EXP_SLOT[v % BLK] == EXP_SLOT[u]]
    return same[-1]


def split_no(q, u):
    if q < 2:
        assert u
        return 3 * u + q - 2
    return min(3 * u + 3, SPLITS)


def build_program(nc, ins, outs):
    F32, F32R, I32 = mybir.dt.float32, mybir.dt.float32r, mybir.dt.int32
    ALU, ACT, AX = mybir.AluOpType, mybir.ActivationFunctionType, mybir.AxisListType
    ctx = ExitStack()
    with ctx:
        def sb(name, shape, dt=F32):
            return ctx.enter_context(nc.sbuf_tensor(name, shape, dt))

        sems = {}

        def S(name):
            if name not in sems:
                sems[name] = ctx.enter_context(nc.semaphore(name))
            return sems[name]

        at_ring = -(-nc.sbuf_base // 32) * 32
        ring = sb("ring", [128, SLOTS, SLOT])
        w_hi = sb("w_hi", [128, 3, 2048], F32R)
        w_lo = sb("w_lo", [128, 3, 2048], F32R)
        hT = sb("hT", [128, KC, TOK])
        atB = -(-nc.sbuf_base // 32) * 32
        regB = sb("regB", [128, KC * TOK])
        atC = -(-nc.sbuf_base // 32) * 32
        regC = sb("regC", [128, KC * TOK])
        uh = nc.alloc_sbuf_tensor_at("uh", [128, KC, TOK], F32R, offset=atB)
        ul = nc.alloc_sbuf_tensor_at("ul", [128, KC, TOK], F32R, offset=atC)
        xh = nc.alloc_sbuf_tensor_at("xh", [128, KC, CAP], F32R, offset=atB)
        xl = nc.alloc_sbuf_tensor_at("xl", [128, KC, CAP], F32R, offset=atB + 4 * KC * CAP)
        hTh = nc.alloc_sbuf_tensor_at("hTh", [128, 2, 2, CAP], F32R, offset=atC)
        hTl = nc.alloc_sbuf_tensor_at("hTl", [128, 2, 2, CAP], F32R, offset=atC + 16 * CAP)
        atD = -(-nc.sbuf_base // 32) * 32
        regD = sb("regD", [128, 3 * D])
        regE = sb("regE", [128, H * TOK])
        uqh = nc.alloc_sbuf_tensor_at("uqh", [128, KC, TOK], F32R, offset=atD)
        wfh = nc.alloc_sbuf_tensor_at("wfh", [128, KC, H], F32R, offset=atD + 4 * KC * TOK)
        wfl = nc.alloc_sbuf_tensor_at("wfl", [128, KC, H], F32R, offset=atD + 4 * KC * (TOK + H))
        kvl = [nc.alloc_sbuf_tensor_at(f"kvl{i}", [128, 4, TOK], F32R, offset=at_ring + 4 * (SLOT * i + 4096))
               for i in range(2)]
        ident = sb("ident", [128, 128])
        ones = sb("ones", [128, 128])
        headones = sb("headones", [128, 128])
        causal = sb("causal", [128, 128])
        causal_s = sb("causal_s", [128, NS])
        before = sb("before", [128, 128])
        slots_iota = sb("slots_iota", [128, CAP])
        sels = sb("sels", [128, H, NS])
        g_pool = sb("g_pool", [128, KC]); p_scale = sb("p_scale", [128, KC]); g_kv = sb("g_kv", [128, KC])
        g_attn = sb("g_attn", [128, KC]); g_ffn = sb("g_ffn", [128, 2, KC])
        gk = sb("gk", [128, 1]); gq = sb("gq", [128, 1]); gq8 = sb("gq8", [128, 1]); bf = sb("bf", [H, 1])
        eps = sb("eps", [128, 1]); one = sb("one", [128, 1])
        stat = sb("stat", [128, 64])
        silu_scratch = stat[:, 40:41]
        counts = stat[:, 48:64]; inv_cnt = sb("inv_cnt", [128, 16])
        wf = sb("wf", [128, KC, H]); wr = sb("wr", [128, KC, NE])
        rms = sb("rms", [128, 2, TOK]); rstd = sb("rstd", [128, 2, TOK])
        QS = sb("QS", [128, KC, 128])
        negs = sb("negs", [128, PAST + NS]); negp = sb("negp", [128, NP])
        lt = sb("lt", [128, 4, H])
        lo = sb("lo", [128, 3, H])

        DE = lambda off, n: (regD[:, off:off + n] if off + n <= 3 * D else regE[:, off - 3 * D:off - 3 * D + n])
        xtok = regD[:, :].rearrange("p (t n) -> p t n", t=3)
        UW = NP + NS + 2 * HIST
        U = regE[:, 0:KC * UW].rearrange("p (c n) -> p c n", c=KC)
        winA = regD[:, 0:KC * UW].rearrange("p (c n) -> p c n", c=KC)
        winB = regC[:, 0:6 * UW].rearrange("p (c n) -> p c n", c=6)
        diff = regB[:, :].rearrange("p (c n) -> p c n", c=KC)
        u32 = regD[:, 0:KC * TOK].rearrange("p (c n) -> p c n", c=KC)
        sq = regC[:, :].rearrange("p (c n) -> p c n", c=KC)
        hmA = regD[:, 0:10 * TOK].rearrange("p (c n) -> p c n", c=10)
        hmB = regE[:, 0:12 * TOK].rearrange("p (c n) -> p c n", c=12)
        kT = regC[:, :].rearrange("p (c n) -> p c n", c=KC)
        vtok = regD[:, :].rearrange("p (t n) -> p t n", t=3)
        qz = regE[:, :].rearrange("p (h n) -> p h n", h=H)
        oT = regB[:, :].rearrange("p (c n) -> p c n", c=KC)
        htok = regD[:, :].rearrange("p (t n) -> p t n", t=3)
        acc = regE[:, 0:3 * D].rearrange("p (t n) -> p t n", t=3)
        kout = [regE[:, D * t:D * t + D] for t in range(3)]
        tail4, tail5 = ring[:, 2, 4096:SLOT], ring[:, 3, 4096:SLOT]
        st_out = tail4[0:HIST, 0:2 * D].rearrange("p (s n) -> p s n", s=2)
        Pp = tail4[:, 0:3 * NP].rearrange("p (i n) -> p i n", i=3)
        PTp = tail4[:, 3 * NP:5 * NP].rearrange("p (i n) -> p i n", i=2)
        t32 = tail4[:, 0:2 * TOK].rearrange("p (i n) -> p i n", i=2)
        r2 = tail4[:, 2 * TOK:3 * TOK]
        sg = regE[:, 14 * TOK:16 * TOK].rearrange("p (i n) -> p i n", i=2)
        raw = tail5[:, 0:2 * TOK].rearrange("p (i n) -> p i n", i=2)
        sqh = tail5[:, 2 * TOK:4 * TOK].rearrange("p (i n) -> p i n", i=2)
        zf, lf = tail5[0:H, 4 * TOK:5 * TOK], tail5[0:H, 5 * TOK:6 * TOK]
        af = tail5[0:H, 6 * TOK:7 * TOK]
        cat = tail4[0:H, 5 * NP:5 * NP + PAST + NS]
        Ps = [tail5[:, 0:640], tail5[:, 640:1280]]
        PTs = tail5[:, 1280:1920].rearrange("p (t n) -> p t n", t=5)
        kc = ring[:, U_KC % SLOTS, 0:4096].rearrange("p (t n) -> p t n", t=4)
        vc = ring[:, U_VC % SLOTS, 0:4096].rearrange("p (t n) -> p t n", t=4)
        ytok = regC[0:CAP, 8 * CAP:8 * CAP + D]
        hflat = hT[:, :, :].rearrange("p c n -> p (c n)")
        Dx = hflat[:, 0:3 * CAP].rearrange("p (t n) -> p t n", t=3)
        Dg = hflat[:, 3 * CAP:6 * CAP].rearrange("p (t n) -> p t n", t=3)
        DgT = hflat[0:CAP, 6 * CAP:6 * CAP + 3 * 128]
        sl = hflat[:, 1152:1664].rearrange("p (i n) -> p i n", i=2)
        hm = hflat[:, 1664:2176].rearrange("p (i n) -> p i n", i=2)
        qflat = QS[:, :, :].rearrange("p c n -> p (c n)")
        lg, m1, m2, key, l2 = (qflat[:, 24 * i:24 * i + 24].rearrange("p (t e) -> p t e", t=3) for i in range(5))
        tv = qflat[:, 120:144].rearrange("p (i t) -> p i t", i=8)
        rank = qflat[:, 144:171].rearrange("p (e t) -> p e t", t=3)
        cur = qflat[:, 198:204]
        gate = qflat[:, 171:198].rearrange("p (e t) -> p e t", t=3)
        wrg = qflat[:, 204:268].rearrange("p (k e) -> p k e", k=KC)
        desc = sb("desc", [128, 3, NE]); rs_tok = sb("rs_tok", [128, 3]); valid = sb("valid", [128, 3])
        most = sb("most", [128, 1]); most_i = sb("most_i", [128, 1], I32)

        P = [ctx.enter_context(nc.psum_tensor(f"P{i}", [128, 512], F32)) for i in range(8)]

        def slot(n):
            return ring[:, n % SLOTS, :]

        def through(n):
            return sum(32 if U_GU <= x < U_DN else 16 for x in range(n % SLOTS, n + 1, SLOTS))

        def arrived(eng, n):
            eng.wait_ge(S(f"arrived{n % SLOTS}"), through(n))

        def exp_arrived(eng, e, uu):
            s = EXP_SLOT[uu]
            base = through(max(n for n in range(U_MOE) if n % SLOTS == s))
            per = [v for v in range(BLK) if EXP_SLOT[v] == s]
            eng.wait_ge(S(f"arrived{s}"), e * (48 * len(per)) + (base + 48 * (per.index(uu) + 1)))

        def used(eng, n):
            if n == U_POOL:
                eng.wait_ge(S("pool_mm"), KC)
            elif n < U_DN:
                eng.wait_ge(S("ffn_wl"), 2 * (n - U_GU + 1))
            elif n < U_Q:
                eng.wait_ge(S("ffn_wl"), FC + 3 * (n - U_DN + 1))
            elif n < U_KC:
                eng.wait_ge(S("p_wl"), 2 * (n - U_Q + 1))
            elif n < U_O:
                eng.wait_ge(S("pvs_mm"), 4)
            else:
                eng.wait_ge(S("wo_mm"), 4 * (n - U_O + 1))

        exp_gu = [ring[:, s, 0:4096].rearrange("p (k h n) -> p k h n", k=KC, h=2) for s in range(SLOTS)]
        exp_dn = [ring[:, s, 4096:6144].rearrange("p (c n) -> p c n", c=2) for s in range(SLOTS)]

        E_GA, E_GB, E_T, E_DN, E_SILU, E_HM, E_HTH, E_HTL = 1, 1, 2, 2, 1, 2, 1, 2
        E_HI, E_LO, E_XH, E_XL, E_Y, E_D, E_AUXP, E_AUXV = 1, 8, 1, 1, 2, 1, 1, 1
        ITS = 9
        ITV = 7

        def buf(q, uu):
            return ((0 if uu == 0 else 2), (1 if uu == 0 else 0), (2 if uu == BLK - 1 else 1))[q]

        def ffn_raw(f):
            w = slot(U_GU + f // 2)[:, 0:4096].rearrange("p (h n) -> p h n", h=2 * KC)
            return w[:, :, 128 * (f % 2):128 * (f % 2) + 128]

        def ffn_part(part, f):
            return part[:, f % 3, :].rearrange("p (h n) -> p h n", h=2 * KC)

        def dn_chunks(i):
            a, b = DN_PARTS[i % 3]
            at = BLK * (i // 3 % 2)
            return i // 6, range(at + a, at + b)

        def dn_raw(i):
            a, b = DN_PARTS[i % 3]
            return slot(U_DN + i // 3)[:, 512 * a:512 * b]

        def dn_part(part, i):
            a, b = DN_PARTS[i % 3]
            return part[:, (FC + i) % 3, 0:512 * (b - a)]

        SWEEP = FC - 3

        def chunk_done(eng, v):
            if v % FC >= SWEEP:
                eng.wait_ge(S("ffn_sum"), 4 * (v // FC + 1))
            else:
                eng.wait_ge(S("ffn_dn"), SWEEP * (v // FC) + v % FC + 1)

        def dn_buffer_free(eng, i):
            if i < 3:
                eng.wait_ge(S("ffn_gu"), FC - 2 + i)
            else:
                sweep, chunks = dn_chunks(i - 3)
                chunk_done(eng, FC * sweep + chunks[-1])

        def sweeps(first, weights, rows, sums):
            ends = {FC * dn_chunks(i - 3)[0] + dn_chunks(i - 3)[1][-1] + 8: i for i in range(3, 12)}
            for v in range(2 * FC):
                if v in ends:
                    weights(ends[v])
                if v == FC + 5:
                    sums(0)
                rows(v)
                if v == 3:
                    weights(first)
            sums(1)

        def hidden(f):
            return hmA[:, f, :] if f < 10 else hmB[:, f - 10, :]

        def p_raw(g):
            w = slot(U_Q + g // 2)[:, 0:4096].rearrange("p (k n) -> p k n", k=KC)
            return w[:, :, 256 * (g % 2):256 * (g % 2) + 256]

        def p_part(part, g):
            return part[:, (FC + 12 + g) % 3, :].rearrange("p (k n) -> p k n", k=KC)

        def kv_chunks(i):
            return range(2) if i == 0 else range(i + 1, min(i + 2, KC))

        DN_BANKS = (7, 0, 3, 4, 5, 6, 2, 7)
        sq2 = [regE[:, (12 + c) * TOK:(13 + c) * TOK] if c < 4 else sq[:, c, :] for c in range(KC)]

        CONSTS = 23

        block = ctx.enter_context(nc.Block())

        @block.sync
        def _(sp):
            def load(n, dst, src, **kw):
                if n >= SLOTS:
                    used(sp, n - SLOTS)
                sp.dma_start(dst, src, **kw).then_inc(S(f"arrived{n % SLOTS}"), 16)

            sp.dma_start(xtok[:, 0:2, :], ins["x_prompt"][0].rearrange("(t p) n -> p t n", p=128))\
              .then_inc(S("x_in"), 16)
            sp.wait_ge(S("xtok_zero"), 1)
            sp.dma_start(xtok[0:NS, 2, :], ins["x_sample"][0]).then_inc(S("x_in"), 16)
            sp.dma_start(xtok[NS:NS + HIST, 2, :], ins["state_pool"][0, 0]).then_inc(S("x_in"), 16)
            load(U_POOL, slot(U_POOL)[:, 0:2048].rearrange("p (g k n) -> p (g k) n", g=4, k=2),
                 ins["w_pool"][0].rearrange("g (k p) n -> p (g k) n", p=128))
            for b in range(BLK):
                n = U_GU + b
                if n >= SLOTS:
                    used(sp, n - SLOTS)
                gu = ins["w_ffn_gu"][0].rearrange("(k p) (h n) -> h p k n", p=128, h=2)
                dst = slot(n)[:, 0:4096].rearrange("p (h k n) -> p h k n", h=2, k=KC)
                for half in range(2):
                    sp.dma_start(dst[:, half], gu[half, :, :, 256 * b:256 * b + 256])\
                      .then_inc(S(f"arrived{n % SLOTS}"), 16)
            for b in range(4):
                if (U_DN + b) % SLOTS == 2:
                    sp.wait_ge(S("stored"), 32)
                half, fh = b // 2, b % 2
                load(U_DN + b, slot(U_DN + b)[:, 0:BLK * 512].rearrange("p (k n) -> p k n", k=BLK),
                     ins["w_ffn_down"][0].rearrange("(k p) n -> p k n", p=128)
                     [:, BLK * fh:BLK * fh + BLK, 512 * half:512 * half + 512])
            for n0, cnt, w in ((U_Q, 2, ins["w_q"][0]), (U_KV, 4, ins["w_kvf"]), (U_KC, 1, None), (U_VC, 1, None),
                               (U_O, 2, ins["w_o"][0])):
                for b in range(cnt):
                    n = n0 + b
                    if w is None:
                        c = ins["cache_k" if n == U_KC else "cache_v"][0].rearrange("(t p) h d -> p t (h d)", p=128)
                        load(n, slot(n)[:, 0:4096].rearrange("p (t n) -> p t n", t=4), c)
                    else:
                        load(n, slot(n)[:, 0:4096].rearrange("p (k n) -> p k n", k=KC),
                             w.rearrange("(k p) n -> p k n", p=128)[:, :, 512 * b:512 * b + 512])

            def load_expert(e, it):
                for uu in range(BLK):
                    if isinstance(it, int) and earlier_user(uu) < 0:
                        used(sp, U_MOE + uu - SLOTS)
                    else:
                        v = earlier_user(uu)
                        sp.wait_ge(S("w_lo"), it * SPLITS + (E_LO + split_no(2, v % BLK) - (SPLITS if v < 0 else 0)))
                        if v == 0:
                            sp.wait_ge(S("first_lo"), it * 2 + 2)
                    s = EXP_SLOT[uu]
                    wgu = ins["w_moe_gu"][0, bass.ds(e, 1)].rearrange("e (k p) n -> p (e k) n", p=128)
                    wdn = ins["w_moe_down"][0, bass.ds(e, 1)].rearrange("e (k p) n -> p (e k) n", p=128)
                    sp.dma_start(exp_gu[s][:, :, 0], wgu[:, :, 256 * uu:256 * uu + 256]).then_inc(S(f"arrived{s}"), 16)
                    sp.dma_start(exp_gu[s][:, :, 1], wgu[:, :, FF + 256 * uu:FF + 256 * uu + 256])\
                      .then_inc(S(f"arrived{s}"), 16)
                    sp.dma_start(exp_dn[s], wdn[:, 2 * uu:2 * uu + 2, :]).then_inc(S(f"arrived{s}"), 16)

            load_expert(0, 0)
            with sp.Fori(1, NE) as e:
                load_expert(e, e)
            sp.wait_ge(S("most_ready"), 1)
            n = sp.value_load(most_i[0:1, 0:1], min_val=0, max_val=TOK)
            for p in range(1, PASSES):
                with sp.If(n > p * CAP):
                    with sp.Fori(0, NE) as e:
                        load_expert(e, e + p * NE)

        @block.gpsimd
        def _(pool):
            pool.memset(xtok[:, 2, :], 0.0).then_inc(S("xtok_zero"), 1)
            made = 0

            def const(ins):
                nonlocal made
                made += 1
                ins.then_inc(S("const"), 1)
                pool.wait_ge(S("const"), made)

            const(pool.memset(ident[:, :], 0.0))
            const(pool.memset(causal[:, :], 0.0))
            const(pool.memset(causal_s[:, :], 0.0))
            const(pool.memset(before[:, :], 0.0))
            const(pool.memset(ones[:, :], 1.0))
            const(pool.memset(headones[:, :], 0.0))
            const(pool.iota(slots_iota[:, :], [[1, CAP]], base=0, channel_multiplier=0,
                            allow_small_or_imprecise_dtypes=True))
            const(pool.iota(counts[:, :], [[1, 16]], base=1, channel_multiplier=0,
                            allow_small_or_imprecise_dtypes=True))
            const(pool.iota(desc[:, :, :], [[0, 3], [-1, NE]], base=NE, channel_multiplier=0,
                            allow_small_or_imprecise_dtypes=True))
            const(pool.memset(eps[:, :], EPS))
            const(pool.memset(one[:, :], 1.0))
            const(pool.memset(valid[:, :], 1.0))
            const(pool.affine_select(out=ident[:, :], in_=ident[:, :], compare_op=ALU.not_equal, fill=1.0, base=0,
                                     pattern=[[-1, 128]], channel_multiplier=1))
            const(pool.affine_select(out=causal[:, :], in_=causal[:, :], compare_op=ALU.is_ge, fill=NEG, base=0,
                                     pattern=[[-1, 128]], channel_multiplier=1))
            const(pool.affine_select(out=before[:, :], in_=before[:, :], compare_op=ALU.is_ge, fill=1.0, base=0,
                                     pattern=[[-1, 128]], channel_multiplier=1))
            for q in range(4):
                const(pool.affine_select(out=causal_s[32 * q:32 * q + 32, :], in_=causal_s[32 * q:32 * q + 32, :],
                                         compare_op=ALU.is_ge, fill=NEG, base=0, pattern=[[-1, NS]],
                                         channel_multiplier=1))
            for q in range(2):
                const(pool.memset(headones[64 * q:64 * q + 64, 64 * q:64 * q + 64], 1.0))
            const(pool.memset(valid[32:64, 2:3], 0.0))
            const(pool.memset(valid[64:128, 2:3], 0.0))
            assert made == CONSTS
            for dst, src in ((g_kv, ins["g_kv_norm"]), (g_attn, ins["g_attn_norm"][0]), (g_ffn[:, 1], ins["g_ffn_norm"][1])):
                with nc.allow_non_contiguous_dma(reason="a gain for each feature, 4 KB"):
                    pool.dma_start(dst[:, :], src.rearrange("(c p) -> p c", p=128)).then_inc(S("gains_in"), 16)
            for half in range(2):
                pool.dma_start(gk[64 * half:64 * half + 64, :], ins["g_k"].rearrange("(d a) -> d a", a=1))\
                    .then_inc(S("gains_in"), 16)
                pool.dma_start(gq[64 * half:64 * half + 64, :], ins["g_q"][0].rearrange("(d a) -> d a", a=1))\
                    .then_inc(S("gains_in"), 16)
            pool.dma_start(bf[:, :], ins["b_f"].rearrange("(d a) -> d a", a=1)).then_inc(S("gains_in"), 16)
            pool.dma_start(wf[:, :, :], ins["w_kvf"].rearrange("(k p) n -> p k n", p=128)[:, :, 2 * D:2 * D + H])\
                .then_inc(S("gains_in"), 16)
            pool.dma_start(wr[:, :, :], ins["w_router"][0].rearrange("(k p) n -> p k n", p=128))\
                .then_inc(S("gains_in"), 16)
            pool.dma_start(lt[:, :, :], ins["cache_logf"][0].rearrange("(t p) h -> p t h", p=128))\
                .then_inc(S("gains_in"), 16)
            for tile in (QS[:, :, :], negs[:, :], negp[:, :]):
                pool.memset(tile, 0.0).then_inc(S("zeros"), 1)
            pool.wait_ge(S("U"), 4)
            pool.wait_ge(S("U_hist"), 1)
            for i, (dst, src, c) in enumerate(((winA, U, 6), (winB, winA, 4), (winA, winB, 6), (winB, winA, 4))):
                w = 1 << i
                a = src[:, 6:8] if src is not winB else src[:, 4:6]
                pool.tensor_tensor(dst[:, c:c + 2, 2 * w - 1:UW], a[:, :, 2 * w - 1:UW], a[:, :, w - 1:UW - w], ALU.add)\
                    .then_inc(S("win3"), 1)
                pool.wait_ge(S("win3"), i + 1)
            pool.wait_ge(S("state_out"), 4)
            pool.dma_start(outs["state_prompt"][0, 0], st_out[:, 0, :]).then_inc(S("stored"), 16)
            pool.dma_start(outs["state_sample"][0, 0], st_out[:, 1, :]).then_inc(S("stored"), 16)
            pool.wait_ge(S("stored"), 32)

            def p_low(g):
                pool.wait_ge(S("p_wh"), g + 1)
                pool.tensor_tensor(p_part(w_lo, g), p_raw(g), p_part(w_hi, g).bitcast(F32), ALU.subtract)\
                    .then_inc(S("p_wl"), 1)

            for g in range(3):
                p_low(g)
            pool.wait_ge(S("ffn_out"), KC)
            pool.wait_ge(S("p_wl"), 3)
            pool.memset(qz[0:64, 1:H:2, :], 0.0).then_inc(S("qz_zero"), 1)
            pool.memset(qz[64:128, 0:H:2, :], 0.0).then_inc(S("qz_zero"), 1)
            pool.wait_ge(S("qz_zero"), 2)
            for g in range(3, 8):
                p_low(g)
            pool.wait_ge(S("proj_mm"), KC)
            pool.wait_ge(S("f_mm"), 1)
            pool.memset(vtok[:, 2, :], 0.0).then_inc(S("v_zero"), 1)
            for g in range(8, 12):
                p_low(g)
            pool.wait_ge(S("logf_tok"), 3)
            pool.dma_start(outs["logf_prompt"][0].rearrange("(t p) h -> p t h", p=128), lo[:, 0:2, :])\
                .then_inc(S("stored"), 16)
            pool.dma_start(outs["logf_sample"][0], lo[0:NS, 2, :]).then_inc(S("stored"), 16)
            pool.wait_ge(S("v_tok"), KC)
            pool.dma_start(outs["v_prompt"][0].rearrange("(t p) h d -> p t (h d)", p=128), vtok[:, 0:2, :])\
                .then_inc(S("v_stored"), 16)
            pool.dma_start(outs["v_sample"][0].rearrange("p h d -> p (h d)"), vtok[0:NS, 2, :])\
                .then_inc(S("v_stored"), 16)
            pool.wait_ge(S("v_stored"), 32)
            pool.wait_ge(S("pvs_mm"), 4)
            pool.memset(htok[:, 2, :], 0.0).then_inc(S("htok_zero"), 1)
            pool.wait_ge(S("k_tok"), 6)
            for t in range(2):
                pool.dma_start(outs["k_prompt"][0, 128 * t:128 * t + 128].rearrange("p h d -> p (h d)"), kout[t])\
                    .then_inc(S("k_stored"), 16)
            pool.dma_start(outs["k_sample"][0].rearrange("p h d -> p (h d)"), kout[2][0:NS, :])\
                .then_inc(S("k_stored"), 16)

            def expert(it):
                s = EXP_SLOT[0]
                for q in range(2):
                    if q == 0:
                        exp_arrived(pool, it, 0)
                        pool.wait_ge(S("e_gb"), it * BLK + E_GB)
                    else:
                        pool.wait_ge(S("e_dn"), it * BLK + (E_DN - 1))
                    w = ring[:, s, 2048 * q:2048 * q + 2048]
                    pool.tensor_tensor(w_hi[:, buf(q, 0), :], w, ones[:, 0:1].to_broadcast([128, 2048]), ALU.mult).then_inc(S("first_hi"), 1)
                    pool.wait_ge(S("first_hi"), it * 2 + (q + 1))
                    pool.tensor_tensor(w_lo[:, buf(q, 0), :], w, w_hi[:, buf(q, 0), :].bitcast(F32), ALU.subtract)\
                        .then_inc(S("first_lo"), 1)

            expert(0)
            pool.wait_ge(S("h_tok"), 6)
            pool.wait_ge(S("k_stored"), 48)
            for t in range(3):
                pool.tensor_copy(acc[:, t, :], htok[:, t, :]).then_inc(S("acc_init"), 1)
            with pool.Fori(1, NE) as e:
                expert(e)
            pool.wait_ge(S("most_ready"), 1)
            n = pool.value_load(most_i[0:1, 0:1], min_val=0, max_val=TOK)
            for p in range(1, PASSES):
                with pool.If(n > p * CAP):
                    with pool.Fori(0, NE) as e:
                        expert(e + p * NE)
            pool.wait_ge(S("acc_done"), 1)
            pool.dma_start(outs["y_prompt"][0].rearrange("(t p) n -> p t n", p=128), acc[:, 0:2, :])\
                .then_inc(S("stored"), 16)
            pool.dma_start(outs["y_sample"][0], acc[0:NS, 2, :]).then_inc(S("stored"), 16)
            pool.wait_ge(S("stored"), 96)
            pool.wait_ge(S("k_stored"), 48)

        @block.tensor
        def _(pe):
            def mm(out, lhsT, rhs, start, stop, **kw):
                return pe.matmul(out, lhsT, rhs, start=start, stop=stop, **kw)

            def products(bank, pairs, first, last):
                for i, (a, w) in enumerate(pairs):
                    m = mm(bank, a, w, first and i == 0, last and i == len(pairs) - 1, skip_group_check=True)
                return m

            def three(ah, al, wh, wl):
                return [(ah, wh), (ah, wl), (al, wh)]

            pe.wait_ge(S("const"), CONSTS)
            pe.wait_ge(S("x_in"), 48)
            for c in range(KC):
                if c >= 4:
                    pe.wait_ge(S("xT"), c - 3)
                for t in range(3):
                    m = pe.transpose(P[c % 4][:, 128 * t:128 * t + 128], xtok[:, t, 128 * c:128 * c + 128], ident[:, :])
                m.then_inc(S("xT_mm"), 1)

            def sum_squares(bank, stage, c):
                pe.wait_ge(S(stage + "_sq"), c + 1)
                m = mm(P[bank][:, 0:TOK], ones[:, :], sq2[c] if stage == "n2" else sq[:, c, :], c == 0, c == KC - 1,
                       skip_group_check=True)
                if c == KC - 1:
                    m.then_inc(S(stage + "_ss"), 1)

            for c in range(KC):
                sum_squares(4, "n0", c)

            arrived(pe, U_POOL)
            wp = slot(U_POOL)[:, 0:2048].rearrange("p (g k n) -> p (g k) n", g=4, k=2)
            for c in range(KC):
                g = c // 2
                pe.wait_ge(S("diff"), g + 1)
                if c >= 4:
                    pe.wait_ge(S("pooled"), c - 3)
                for k in range(2):
                    m = mm(P[c % 4][:, 0:TOK], wp[:, 2 * g + k, 128 * (c % 2):128 * (c % 2) + 128],
                           diff[:, 2 * g + k, :], k == 0, k == 1)
                m.then_inc(S("pool_mm"), 1)
            for c in range(KC):
                if c == 0:
                    pe.wait_ge(S("pooled"), 5)
                sum_squares(0, "n1", c)
            for s, at in ((0, HIST + NP - HIST), (1, HIST + NP + HIST + NS - HIST)):
                for half in range(2):
                    bank = [5, 6, 7, 4][2 * s + half]
                    for c in range(4):
                        m = pe.transpose(P[bank][0:HIST, 128 * c:128 * c + 128],
                                         U[:, 4 * half + c, at:at + HIST], ident[:, :])
                    m.then_inc(S("state_mm"), 1)


            for f in range(FC):
                if f == 1:
                    pe.wait_ge(S("state_out"), 4)
                if f >= 3:
                    pe.wait_ge(S("ffn_hm"), f - 2)
                pe.wait_ge(S("ffn_wl"), f + 1)
                wh, wl = ffn_part(w_hi, f), ffn_part(w_lo, f)
                for half in range(2):
                    for k in range(KC):
                        if f == 0 and half == 0:
                            pe.wait_ge(S("u_ffn"), k + 1)
                        h, l = wh[:, KC * half + k, :], wl[:, KC * half + k, :]
                        m = products(P[1 + 2 * (f % 3) + half][:, 0:TOK],
                                     [(h, uh[:, k, :]), (h, ul[:, k, :]), (l, uh[:, k, :])], k == 0, k == KC - 1)
                m.then_inc(S("ffn_gu"), 1)
            for i in range(12):
                sweep, chunks = dn_chunks(i)
                pe.wait_ge(S("ffn_wl"), FC + i + 1)
                if i == 6:
                    pe.wait_ge(S("ffn_out"), 1)
                w_h, w_l = dn_part(w_hi, i), dn_part(w_lo, i)

                def product(f, d):
                    at, v = 512 * (f - chunks[0]) + 128 * d, (FC * sweep + f) % 8
                    h, l = w_h[:, at:at + 128], w_l[:, at:at + 128]
                    return products(P[DN_BANKS[4 * sweep + d]][:, 0:TOK],
                                    [(h, uh[:, v, :]), (h, ul[:, v, :]), (l, uh[:, v, :])], f == 0, f == FC - 1)

                if i % 6 < 5:
                    for f in chunks:
                        pe.wait_ge(S("hid_low"), FC * sweep + f + 1)
                        for d in range(4):
                            m = product(f, d)
                        m.then_inc(S("ffn_dn"), 1)
                else:
                    pe.wait_ge(S("hid_low"), FC * sweep + FC)
                    for d in range(4):
                        for f in chunks:
                            m = product(f, d)
                        m.then_inc(S("ffn_sum"), 1)
                if i == 7:
                    for c in range(4):
                        sum_squares(1, "n2", c)
            for c in range(4, KC):
                sum_squares(1, "n2", c)

            def proj(i, high, low, first_wait):
                if i % 2 == 0:
                    pe.wait_ge(S("p_wl"), i // 2 + 1)
                if i >= 2:
                    pe.wait_ge(S("raw"), i - 1)
                w_h, w_l = p_part(w_hi, i // 2), p_part(w_lo, i // 2)
                for k in range(KC):
                    if first_wait is not None:
                        pe.wait_ge(S(first_wait), k + 1)
                    h, l = (a[:, k, 128 * (i % 2):128 * (i % 2) + 128] for a in (w_h, w_l))
                    m = products(P[2 + i % 2][:, 0:TOK], [(h, high[:, k, :]), (h, low(k)), (l, high[:, k, :])],
                                 k == 0, k == KC - 1)
                m.then_inc(S("proj_mm"), 1)
                return m

            def q_low(k):
                return ul[:, k, :]

            def kv_low(k):
                return kvl[k // 4][:, k % 4, :]

            def head_sums(i):
                pe.wait_ge(S("head_sq"), i + 1)
                if i >= 2:
                    pe.wait_ge(S("head_rms"), i - 1)
                mm(P[4 + i % 2][:, 0:TOK], headones[:, :], sqh[:, i % 2, :], True, True).then_inc(S("head_ss"), 1)

            pe.wait_ge(S("gains_in"), 176)
            for t in range(4):
                m = pe.transpose(P[6][0:H, 128 * t:128 * t + 128], lt[:, t, :], ident[:, :])
            m.then_inc(S("cache_f"), 1)
            for i in range(2 * KC):
                if i < KC:
                    proj(i, uqh, q_low, "u_q" if i == 0 else None)
                else:
                    proj(i, uh, kv_low, "u_kv" if i == KC else None)
                if i == KC:
                    pe.wait_ge(S("wf_split"), 1)
                    for k in range(KC):
                        m = products(P[7][0:H, 0:TOK], [(wfh[:, k, :], uh[:, k, :]), (wfh[:, k, :], kv_low(k)),
                                                        (wfl[:, k, :], uh[:, k, :])], k == 0, k == KC - 1)
                    m.then_inc(S("f_mm"), 1)
                if i >= 1:
                    head_sums(i - 1)

            def v_transposes(c):
                i = 2 * KC + c
                pe.wait_ge(S("raw"), i + 1)
                if c >= 2:
                    pe.wait_ge(S("v_tok"), c - 1)
                if c == 0:
                    pe.wait_ge(S("cat_ready"), 1)
                if c == 1:
                    pe.wait_ge(S("z_ready"), 1)
                for t in range(3):
                    r = 128 if t < 2 else NS
                    m = pe.transpose(P[6 + c % 2][0:r, 128 * t:128 * t + 128], raw[:, i % 2, 128 * t:128 * t + r], ident[:, :])
                m.then_inc(S("vt_mm"), 1)

            for c in range(KC):
                i = 2 * KC + c
                proj(i, uh, kv_low, None)
                if c == 0:
                    head_sums(2 * KC - 1)
                if c == 2:
                    pe.wait_ge(S("lf_ready"), 1)
                    for t in range(3):
                        r = 128 if t < 2 else NS
                        m = pe.transpose(P[1][0:r, H * t:H * t + H], lf[:, 128 * t:128 * t + r], ident[0:H, 0:H])
                    m.then_inc(S("lf_mm"), 1)
                if c >= 1:
                    v_transposes(c - 1)
            v_transposes(KC - 1)

            arrived(pe, U_KC)
            for j in range(8):
                if j >= 2:
                    pe.wait_ge(S("kc_out"), j - 1)
                if j == 1:
                    pe.wait_ge(S("logf_tok"), 3)
                for c in range(4):
                    m = pe.transpose(P[j % 2][:, 128 * c:128 * c + 128],
                                     kc[:, j // 2, 512 * (j % 2) + 128 * c:512 * (j % 2) + 128 * c + 128], ident[:, :])
                m.then_inc(S("kc_mm"), 1)

            def scores(n):
                h, qt = n // 2, n % 2
                nk = 128 * (qt + 1)
                if n == 0:
                    pe.wait_ge(S("k_ready"), KC)
                    pe.wait_ge(S("q_ready"), KC)
                    pe.wait_ge(S("neg_ready"), 2)
                    pe.wait_ge(S("kc_out"), 8)
                if n >= 3:
                    pe.wait_ge(S("p_exp"), n - 2)
                b = P[n % 3]
                mm(b[:, 0:nk], qz[:, h, 128 * qt:128 * qt + 128], kT[:, h // 2, 0:nk], True, False)
                mm(b[:, 0:nk], ident[:, h:h + 1].to_broadcast([128, 128]), negp[:, 0:nk], False, False)
                mm(b[:, nk - 128:nk], ident[:, :], causal[:, :], False, True).then_inc(S("s_mm"), 1)

            def probs_T(n):
                pe.wait_ge(S("p_norm"), n + 1)
                if n >= 2:
                    pe.wait_ge(S("pt_out"), n - 1)
                for t in range(n % 2 + 1):
                    m = pe.transpose(P[3 + n % 2][:, 128 * t:128 * t + 128], Pp[:, n % 3, 128 * t:128 * t + 128], ident[:, :])
                m.then_inc(S("pt_mm"), 1)

            def values(n):
                h, qt = n // 2, n % 2
                c = h // 2
                pe.wait_ge(S("pt_out"), n + 1)
                if n % 4 == 0 and c >= 2:
                    pe.wait_ge(S("o_out"), c - 1)
                at = NP * (h % 2) + 128 * qt
                for t in range(qt + 1):
                    m = mm(P[5 + c % 2][:, at:at + 128], vtok[:, t, 128 * c:128 * c + 128],
                           PTp[:, n % 2, 128 * t:128 * t + 128], t == 0, t == qt)
                m.then_inc(S("pv_mm"), 1)

            NA = 2 * H
            pe.wait_ge(S("v_tok"), KC)
            for n in range(NA + 3):
                if n < NA:
                    scores(n)
                if 2 <= n < NA + 2:
                    probs_T(n - 2)
                if n >= 3:
                    values(n - 3)

            arrived(pe, U_VC)
            SB = [(0, 1), (2, 7)]

            def s_scores(j):
                if j >= 2:
                    pe.wait_ge(S("ps_exp"), j - 1)
                if j == 0:
                    pe.wait_ge(S("p_exp"), NA)
                b0, b1 = P[SB[j % 2][0]], P[SB[j % 2][1]]
                for a in range(2):
                    c = 2 * j + a
                    mm(b0[:, :].rearrange("p (t n) -> p t n", t=4), QS[:, c, :], kc[:, :, 128 * c:128 * c + 128], a == 0, False)
                    mm(b1[:, 0:NS], QS[:, c, :], kT[:, c, NP:TOK], a == 0, False)
                sel = sels[:, 4 * j:4 * j + 4, :].rearrange("p h n -> p (h n)")
                mm(b0[:, :], sel, negs[:, 0:PAST], False, True)
                mm(b1[:, 0:NS], sel, negs[:, PAST:PAST + NS], False, False)
                mm(b1[:, 0:NS], ident[:, :], causal_s[:, :], False, True).then_inc(S("ss_mm"), 1)

            def keys_out(i):
                t, half = i // 2, i % 2
                r = 128 if t < 2 else NS
                if i == 0:
                    pe.wait_ge(S("o_out"), KC)
                else:
                    pe.wait_ge(S("k_tok"), i)
                for c in range(4):
                    m = pe.transpose(P[6][0:r, 128 * c:128 * c + 128], kT[:, 4 * half + c, 128 * t:128 * t + r], ident[:, :])
                m.then_inc(S("kt_mm"), 1)

            def s_turn(j):
                pe.wait_ge(S("ps_norm"), j + 1)
                if j >= 1:
                    pe.wait_ge(S("pts_out"), j)
                for t in range(5):
                    m = pe.transpose(P[3 + t // 4][:, 128 * (t % 4):128 * (t % 4) + 128], Ps[j % 2][:, 128 * t:128 * t + 128], ident[:, :])
                m.then_inc(S("pts_mm"), 1)
                if j < 3:
                    keys_out(2 * j)

            def s_values(j):
                pe.wait_ge(S("pts_out"), j + 1)
                if j == 0:
                    pe.wait_ge(S("o_out"), KC)
                if j >= 1:
                    pe.wait_ge(S("os_out"), j)
                for a in range(2):
                    c = 2 * j + a
                    for t in range(5):
                        v = vc[:, t, 128 * c:128 * c + 128] if t < 4 else vtok[:, 2, 128 * c:128 * c + 128]
                        m = mm(P[5][:, 64 * a:64 * a + 64], v, PTs[:, t, 64 * a:64 * a + 64], t == 0, t == 4)
                m.then_inc(S("pvs_mm"), 1)
                if j < 3:
                    keys_out(2 * j + 1)

            s_scores(0)
            s_scores(1)
            for j in range(4):
                s_turn(j)
                if j < 2:
                    s_scores(j + 2)
                s_values(j)

            def logits(k):
                pe.wait_ge(S("h2"), k + 1)
                if k == 0:
                    pe.wait_ge(S("wrg_ready"), 1)
                for t in range(3):
                    r = 128 if t < 2 else NS
                    mm(P[4][0:r, NE * t:NE * t + NE], hT[:, k, 128 * t:128 * t + r], wrg[:, k, :],
                       k == 0 and t == 0, k == KC - 1, skip_group_check=True)

            def rows_out(half):
                pe.wait_ge(S("h2"), 4 * half + 4)
                for t in range(3):
                    r, j = (128 if t < 2 else NS), 3 * half + t
                    if j >= 2:
                        pe.wait_ge(S("h_tok"), j - 1)
                    for c in range(4):
                        m = pe.transpose(P[2 + j % 2][0:r, 128 * c:128 * c + 128], hT[:, 4 * half + c, 128 * t:128 * t + r], ident[:, :])
                    m.then_inc(S("ht_mm"), 1)

            for d in range(KC):
                n = U_O + d // 4
                if d % 4 == 0:
                    arrived(pe, n)
                w = slot(n)[:, 0:4096].rearrange("p (k n) -> p k n", k=KC)
                if d == 0:
                    pe.wait_ge(S("os_out"), 4)
                if d >= 2:
                    pe.wait_ge(S("h2"), d - 1)
                for k in range(KC):
                    m = mm(P[d % 2][:, 0:TOK], w[:, k, 128 * (d % 4):128 * (d % 4) + 128], oT[:, k, :], k == 0, k == KC - 1)
                m.then_inc(S("wo_mm"), 1)
                if d >= 1:
                    logits(d - 1)
                if d == 5:
                    rows_out(0)
            logits(KC - 1)
            pe.wait_ge(S("row_sq"), KC)
            for t in range(3):
                r = 128 if t < 2 else NS
                m = mm(P[4][0:r, 32 + t:33 + t], sq[:, 0, 128 * t:128 * t + r], ones[:, 0:1], False, True,
                       skip_group_check=True)
            m.then_inc(S("lg_mm"), 1)
            rows_out(1)
            pe.wait_ge(S("mask_ready"), 1)
            for t in range(3):
                for s in range(t + 1):
                    mm(P[7][:, NE * t:NE * t + NE], before[:, :] if s == t else ones[:, :], key[:, s, :], s == 0, s == t)
            for s in range(3):
                m = mm(P[7][:, 32:32 + NE], ones[:, :], key[:, s, :], s == 0, s == 2)
            m.then_inc(S("rank_mm"), 1)

            def gather(first, want_d, want_v):
                pe.wait_ge(S("dispatch"), want_d)
                pe.wait_ge(S("aux_dve"), want_v)
                b = P[5 + first // 4]
                for j in range(4):
                    c = first + j
                    for t in range(3):
                        m = mm(b[:, CAP * j:CAP * j + CAP], htok[:, t, 128 * c:128 * c + 128], Dx[:, t, :], t == 0, t == 2)
                m.then_inc(S("aux_pe"), 1)

            def expert(it, p):
                V = it * ITV + E_AUXV
                X = it * 2 + (E_XL + 2 * (p + 1))

                def gate_up(uu, q):
                    if uu == 0:
                        pe.wait_ge(S("first_lo"), it * 2 + (q + 1))
                    else:
                        pe.wait_ge(S("w_lo"), it * SPLITS + (E_LO + split_no(q, uu)))
                    if q == 0:
                        pe.wait_ge(S("e_hm"), it * BLK + (E_HM + uu - 1))
                    for k in range(4):
                        c = 4 * q + k
                        wh, wl = w_hi[:, buf(q, uu), 512 * k:512 * k + 512], w_lo[:, buf(q, uu), 512 * k:512 * k + 512]
                        m = products(P[uu % 2][:, :], three(xh[:, c, :], xl[:, c, :], wh, wl), c == 0, c == KC - 1)
                    m.then_inc(S("e_gb" if q else "e_ga"), 1)

                def turn(uu):
                    pe.wait_ge(S("e_hm"), it * BLK + (E_HM + uu + 1))
                    pe.wait_ge(S("e_htl"), it * BLK + (E_HTL + uu))
                    if uu == 0:
                        pe.wait_ge(S("aux_dve"), V)
                    for f in range(2):
                        m = pe.transpose(P[2][:, 128 * f:128 * f + 128], hm[:, uu % 2, 128 * f:128 * f + 128], ident[:, :])
                    m.then_inc(S("e_t"), 1)

                def down(uu):
                    pe.wait_ge(S("e_htl"), it * BLK + (E_HTL + uu + 1))
                    pe.wait_ge(S("w_lo"), it * SPLITS + (E_LO + split_no(2, uu)))
                    if uu == 0:
                        pe.wait_ge(S("e_y"), it * 2 + E_Y)
                    for f in range(2):
                        for half in range(2):
                            at = 1024 * f + 512 * half
                            wh, wl = w_hi[:, buf(2, uu), at:at + 512], w_lo[:, buf(2, uu), at:at + 512]
                            m = products(P[3 + half][:, :], three(hTh[:, uu % 2, f, :], hTl[:, uu % 2, f, :], wh, wl),
                                         uu == 0 and f == 0, uu == BLK - 1 and f == 1)
                    m.then_inc(S("e_dn"), 1)

                for uu in range(BLK):
                    if uu == 0:
                        pe.wait_ge(S("e_xl"), X)
                    gate_up(uu, 0)
                    if uu == 0:
                        pe.wait_ge(S("aux_dve"), V)
                        for t in range(3):
                            m = pe.transpose(P[7][0:CAP, 128 * t:128 * t + 128], Dg[:, t, :], ident[:, :])
                        m.then_inc(S("aux_pe"), 1)
                    else:
                        turn(uu - 1)
                    gate_up(uu, 1)
                    if uu >= 1:
                        down(uu - 1)
                turn(BLK - 1)
                gather(0, it + (E_D + 2 + p), V + 1)
                down(BLK - 1)
                gather(4, it + (E_D + 2 + p), V + 1)
                for i, (bank, emptied) in enumerate(((7, 1), (2, 1), (5, 1), (6, 1), (7, 2), (2, 3))):
                    half, t = i // 3, i % 3
                    r = 128 if t < 2 else NS
                    pe.wait_ge(S("aux_dve"), V + emptied)
                    pe.wait_ge(S("e_y"), it * 2 + (E_Y + 1 + half))
                    if bank == 2:
                        pe.wait_ge(S("e_htl"), it * BLK + (E_HTL + BLK))
                    elif bank in (5, 6):
                        pe.wait_ge(S("e_xl"), X + (bank - 4))
                    mm(P[bank][0:r, :], DgT[:, 128 * t:128 * t + r], ytok[:, 512 * half:512 * half + 512], True, True)\
                        .then_inc(S("aux_pe"), 1)

            def first_gather(p):
                for first in (0, 4):
                    gather(first, NE * p + (E_D + 1 + p), NE * p * ITV + E_AUXV)

            first_gather(0)
            with pe.Fori(0, NE) as e:
                expert(e, 0)
            pe.wait_ge(S("most_ready"), 1)
            n = pe.value_load(most_i[0:1, 0:1], min_val=0, max_val=TOK)
            for p in range(1, PASSES):
                with pe.If(n > p * CAP):
                    first_gather(p)
                    with pe.Fori(0, NE) as e:
                        expert(e + p * NE, p)

        @block.scalar
        def _(act):
            def squares(stage, src_sem):
                for c in range(KC):
                    act.wait_ge(S(src_sem), c + 1)
                    act.activation(sq[:, c, :], hT[:, c, :], ACT.Square).then_inc(S(stage + "_sq"), 1)

            def root(stage, bank, i):
                act.wait_ge(S(stage + "_ss"), 1)
                act.activation(rms[:, i, :], P[bank][:, 0:TOK], ACT.Sqrt, bias=eps[:, :], scale=1.0 / D)\
                    .then_inc(S(stage + "_rms"), 1)

            for dst, src in ((g_pool, ins["g_pool_norm"][0]), (p_scale, ins["pool_scale"][0]),
                             (g_ffn[:, 0], ins["g_ffn_norm"][0])):
                with nc.allow_non_contiguous_dma(reason="a gain for each feature, 4 KB"):
                    act.dma_start(dst[:, :], src.rearrange("(c p) -> p c", p=128)).then_inc(S("first_gains"), 16)
            act.wait_ge(S("const"), CONSTS)
            squares("n0", "xT")
            root("n0", 4, 0)

            def ffn_high(f):
                if f % 2 == 0:
                    arrived(act, U_GU + f // 2)
                if f >= 3:
                    act.wait_ge(S("ffn_gu"), f - 2)
                act.activation(ffn_part(w_hi, f), ffn_raw(f), ACT.Copy).then_inc(S("ffn_wh"), 1)

            for f in range(3):
                ffn_high(f)
            squares("n1", "pooled")
            root("n1", 0, 1)
            for c in range(KC):
                act.wait_ge(S("u32"), c + 1)
                act.activation(uh[:, c, :], u32[:, c, :], ACT.Copy).then_inc(S("u_high"), 1)
            for s in range(2):
                for half in range(2):
                    act.wait_ge(S("state_mm"), 2 * s + half + 1)
                    act.activation(st_out[:, s, 512 * half:512 * half + 512], P[[5, 6, 7, 4][2 * s + half]][0:HIST, :],
                                   ACT.Copy).then_inc(S("state_out"), 1)
            def dn_high(i):
                if i % 3 == 0:
                    arrived(act, U_DN + i // 3)
                dn_buffer_free(act, i)
                act.activation(dn_part(w_hi, i), dn_raw(i), ACT.Copy).then_inc(S("ffn_wh"), 1)

            def hid_high(v):
                act.wait_ge(S("ffn_hm"), v % FC + 1)
                if v < 8:
                    act.wait_ge(S("ffn_gu"), FC)
                else:
                    chunk_done(act, v - 8)
                act.activation(uh[:, v % 8, :], hidden(v % FC), ACT.Copy).then_inc(S("hid_high"), 1)

            def ffn_squares(sweep):
                for c in range(4 * sweep, 4 * sweep + 4):
                    act.wait_ge(S("ffn_out"), c + 1)
                    act.activation(sq2[c], hT[:, c, :], ACT.Square).then_inc(S("n2_sq"), 1)

            for f in range(FC):
                if 3 <= f + 2 < FC:
                    ffn_high(f + 2)
                elif f + 2 >= FC:
                    dn_high(f + 2 - FC)
                act.wait_ge(S("ffn_gu"), f + 1)
                if f >= 2:
                    act.wait_ge(S("ffn_hm"), f - 1)
                act.activation(sg[:, f % 2, :], P[1 + 2 * (f % 3)][:, 0:TOK], ACT.Silu).then_inc(S("ffn_sg"), 1)
            def p_high(g):
                if g % 2 == 0:
                    arrived(act, U_Q + g // 2)
                if g < 3:
                    dn_buffer_free(act, 12 + g)
                else:
                    act.wait_ge(S("proj_mm"), 2 * g - 4)
                act.activation(p_part(w_hi, g), p_raw(g), ACT.Copy).then_inc(S("p_wh"), 1)

            def last_squares(sweep):
                if sweep == 1:
                    p_high(0)
                    p_high(1)
                ffn_squares(sweep)

            sweeps(2, dn_high, hid_high, last_squares)
            root("n2", 1, 0)
            p_high(2)
            for c in range(KC):
                act.wait_ge(S("q32"), c + 1)
                act.activation(uqh[:, c, :], t32[:, c % 2, :], ACT.Copy).then_inc(S("q_high"), 1)
            act.wait_ge(S("gains_in"), 176)
            act.activation(wfh[:, :, :], wf[:, :, :], ACT.Copy).then_inc(S("wf_high"), 1)
            act.wait_ge(S("cache_f"), 1)
            act.wait_ge(S("stored"), 32)
            act.activation(cat[:, 0:PAST], P[6][0:H, :], ACT.Copy).then_inc(S("cat_ready"), 1)

            def head_root(i):
                act.wait_ge(S("head_ss"), i + 1)
                if i >= 2:
                    act.wait_ge(S("head_rstd"), i - 1)
                act.activation(rms[:, i % 2, :], P[4 + i % 2][:, 0:TOK], ACT.Sqrt, bias=eps[:, :], scale=1.0 / HD)\
                    .then_inc(S("head_rms"), 1)

            act.wait_ge(S("n2_rstd"), 1)
            for i in range(3 * KC):
                act.wait_ge(S("proj_mm"), i + 1)
                if i < 2 * KC:
                    if i >= 2:
                        act.wait_ge(S("head_ss"), i - 1)
                    act.activation(sqh[:, i % 2, :], P[2 + i % 2][:, 0:TOK], ACT.Square).then_inc(S("head_sq"), 1)
                if 1 <= i <= 2 * KC:
                    head_root(i - 1)
                if 2 <= i < KC + 2:
                    act.wait_ge(S("q_ready"), i - 1)
                elif KC + 2 <= i < 2 * KC + 2:
                    act.wait_ge(S("k_ready"), i - KC - 1)
                elif i >= 2 * KC + 2:
                    act.wait_ge(S("vt_mm"), i - 2 * KC - 1)
                act.activation(raw[:, i % 2, :], P[2 + i % 2][:, 0:TOK], ACT.Copy).then_inc(S("raw"), 1)
                for c in kv_chunks(i):
                    act.wait_ge(S("kv32"), c + 1)
                    act.activation(uh[:, c, :], t32[:, c % 2, :], ACT.Copy).then_inc(S("kv_high"), 1)
                if i % 2 == 1 and i < 2 * KC + 2:
                    p_high((i + 1) // 2 + 2)
                if i == 2 * KC:
                    act.wait_ge(S("z_ready"), 2)
                    act.activation(af, af, ACT.Exp, scale=-1.0).then_inc(S("f_exp"), 1)
                    act.wait_ge(S("f_exp"), 1)
                    act.activation(af, af, ACT.Ln, bias=one[0:H, :]).then_inc(S("f_ln"), 1)
            for j in range(8):
                act.wait_ge(S("kc_mm"), j + 1)
                act.activation(kc[:, j // 2, 512 * (j % 2):512 * (j % 2) + 512], P[j % 2][:, :], ACT.Copy)\
                    .then_inc(S("kc_out"), 1)
            for n in range(2 * H):
                act.wait_ge(S("p_max"), n + 1)
                if n >= 3:
                    act.wait_ge(S("pt_mm"), n - 2)
                nk = 128 * (n % 2 + 1)
                act.activation(Pp[:, n % 3, 0:nk], P[n % 3][:, 0:nk], ACT.Exp, bias=stat[:, n % 3:n % 3 + 1],
                               accum_out=stat[:, 4 + n % 3:5 + n % 3]).then_inc(S("p_exp"), 1)
            def s_exp(j):
                act.wait_ge(S("ps_max"), j + 1)
                if j >= 2:
                    act.wait_ge(S("pts_mm"), j - 1)
                b0, b1 = [(0, 1), (2, 7)][j % 2]
                nm = stat[:, 16 + 8 * (j % 2):17 + 8 * (j % 2)]
                act.activation(Ps[j % 2][:, 0:PAST], P[b0][:, :], ACT.Exp, bias=nm,
                               accum_out=stat[:, 17 + 8 * (j % 2):18 + 8 * (j % 2)]).then_inc(S("ps_exp_a"), 1)
                act.activation(Ps[j % 2][:, PAST:PAST + NS], P[b1][:, 0:NS], ACT.Exp, bias=nm,
                               accum_out=stat[:, 18 + 8 * (j % 2):19 + 8 * (j % 2)]).then_inc(S("ps_exp"), 1)

            def keys(*which):
                for j in which:
                    t, half = j // 2, j % 2
                    r = 128 if t < 2 else NS
                    act.wait_ge(S("kt_mm"), j + 1)
                    act.activation(kout[t][0:r, 512 * half:512 * half + 512], P[6][0:r, :], ACT.Copy)\
                        .then_inc(S("k_tok"), 1)

            s_exp(0)
            s_exp(1)
            keys(0)
            s_exp(2)
            keys(1, 2)
            s_exp(3)
            keys(3, 4, 5)

            act.wait_ge(S("htok_zero"), 1)
            act.wait_ge(S("kt_mm"), 6)

            def rows(half):
                for t in range(3):
                    r, j = (128 if t < 2 else NS), 3 * half + t
                    act.wait_ge(S("ht_mm"), j + 1)
                    act.activation(htok[0:r, t, 512 * half:512 * half + 512], P[2 + j % 2][0:r, :], ACT.Copy)\
                        .then_inc(S("h_tok"), 1)

            for d in range(KC):
                act.wait_ge(S("h2"), d + 1)
                act.activation(sq[:, d, :], hT[:, d, :], ACT.Square).then_inc(S("h2_sq"), 1)
                if d == 5:
                    rows(0)
            act.wait_ge(S("lg_mm"), 1)
            act.activation(tv[:, 1, 0:2], P[4][:, 32:34], ACT.Sqrt, bias=eps[:, :], scale=1.0 / D).then_inc(S("row_rms"), 1)
            act.activation(tv[0:NS, 1, 2:3], P[4][0:NS, 34:35], ACT.Sqrt, bias=eps[0:NS, :], scale=1.0 / D)\
                .then_inc(S("row_rms"), 1)
            rows(1)
            act.wait_ge(S("top2"), 1)
            act.activation(tv[:, 4, :], tv[:, 3, :], ACT.Exp).then_inc(S("e2_ready"), 1)

            def rows_high(first, want_p):
                act.wait_ge(S("aux_pe"), want_p)
                for c in range(first, first + 4):
                    m = act.activation(xh[:, c, :], P[5 + first // 4][:, CAP * (c % 4):CAP * (c % 4) + CAP], ACT.Copy,
                                       scale=g_ffn[:, 1, c:c + 1])
                m.then_inc(S("e_xh"), 1)

            def expert(it, p):
                A = it * ITS + (E_AUXP + 2 * (p + 1))

                def high(q, uu):
                    if q == 0 or (q == 2 and uu == 0):
                        exp_arrived(act, it, uu)
                    if (q, uu) == (0, 1):
                        act.wait_ge(S("e_dn"), it * BLK + E_DN)
                    elif (q == 0 and uu >= 2) or (q, uu) in ((1, 1), (2, BLK - 1)):
                        act.wait_ge(S("e_ga"), it * BLK + (E_GA + (uu + 1 if q == 2 else uu)))
                    elif q == 1:
                        act.wait_ge(S("e_gb"), it * BLK + (E_GB + uu))
                    elif uu == 0:
                        act.wait_ge(S("e_gb"), it * BLK + (E_GB + 1))
                    else:
                        act.wait_ge(S("e_dn"), it * BLK + (E_DN + uu))
                    s, w = EXP_SLOT[uu], 2048 * q
                    act.activation(w_hi[:, buf(q, uu), :], ring[:, s, w:w + 2048], ACT.Copy).then_inc(S("w_hi"), 1)

                def hidden_high(uu):
                    act.wait_ge(S("e_t"), it * BLK + (E_T + uu + 1))
                    act.wait_ge(S("e_dn"), it * BLK + (E_DN + uu - 1 if uu >= 1 else E_DN))
                    act.activation(hTh[:, uu % 2].rearrange("p f n -> p (f n)"), P[2][:, 0:256], ACT.Copy)\
                        .then_inc(S("e_hth"), 1)

                act.activation(silu_scratch[:, :], one[:, :], ACT.Silu)
                for uu in range(BLK):
                    if uu >= 1:
                        hidden_high(uu - 1)
                    if uu < BLK - 1:
                        high(0, uu + 1)
                    if uu == 0:
                        high(1, 1)
                    act.wait_ge(S("e_gb"), it * BLK + (E_GB + uu + 1))
                    act.wait_ge(S("e_hm"), it * BLK + (E_HM + uu - 1))
                    act.activation(sl[:, uu % 2, :], P[uu % 2][:, 0:256], ACT.Silu).then_inc(S("e_silu"), 1)
                    if 1 <= uu < BLK - 1:
                        high(1, uu + 1)
                    high(2, uu)
                hidden_high(BLK - 1)
                rows_high(0, A + 2)
                act.wait_ge(S("e_dn"), it * BLK + (E_DN + BLK))
                act.wait_ge(S("aux_pe"), A)
                for half in range(2):
                    act.activation(ytok[:, 512 * half:512 * half + 512], P[3 + half][:, :], ACT.Copy)\
                        .then_inc(S("e_y"), 1)
                rows_high(4, A + 3)

            def first_rows(p):
                for i in range(2):
                    rows_high(4 * i, NE * p * ITS + (E_AUXP + 2 * p + i + 1))

            first_rows(0)
            with act.Fori(0, NE) as e:
                expert(e, 0)
            act.wait_ge(S("most_ready"), 1)
            n = act.value_load(most_i[0:1, 0:1], min_val=0, max_val=TOK)
            for p in range(1, PASSES):
                with act.If(n > p * CAP):
                    first_rows(p)
                    with act.Fori(0, NE) as e:
                        expert(e + p * NE, p)

        @block.vector
        def _(dve):
            def then(ins, name):
                chain[name] = chain.get(name, 0) + 1
                ins.then_inc(S(name), 1)
                dve.wait_ge(S(name), chain[name])

            chain = {}
            dve.wait_ge(S("const"), CONSTS)
            then(dve.reciprocal(inv_cnt[:, :], counts[:, :]), "dve_setup")
            then(dve.tensor_copy(sels[:, :, :], ident[:, 0:H].unsqueeze(2).to_broadcast([128, H, NS])), "dve_setup")
            for name, v in (("e_ga", E_GA), ("e_gb", E_GB), ("e_t", E_T), ("e_dn", E_DN), ("e_silu", E_SILU), ("e_hm", E_HM),
                            ("e_hth", E_HTH), ("e_htl", E_HTL), ("w_hi", E_HI), ("w_lo", E_LO), ("e_xh", E_XH), ("e_xl", E_XL),
                            ("e_y", E_Y), ("dispatch", E_D), ("aux_pe", E_AUXP), ("aux_dve", E_AUXV)):
                dve.sem_inc(S(name), v)
            for c in range(KC):
                dve.wait_ge(S("xT_mm"), c + 1)
                dve.tensor_copy(hT[:, c, :], P[c % 4][:, 0:TOK]).then_inc(S("xT_a"), 1)
                dve.tensor_copy(U[:, c, HIST + NP:2 * HIST + NP], P[c % 4][:, TOK:TOK + HIST]).then_inc(S("xT"), 1)
            dve.memset(U[:, :, 0:HIST], 0.0).then_inc(S("U_hist"), 1)
            dve.wait_ge(S("U_hist"), 1)

            def inverse(stage, i):
                dve.wait_ge(S(stage + "_rms"), 1)
                dve.reciprocal(rstd[:, i, :], rms[:, i, :]).then_inc(S(stage + "_rstd"), 1)
                dve.wait_ge(S(stage + "_rstd"), 1)

            dve.wait_ge(S("first_gains"), 48)
            inverse("n0", 0)
            for c in (6, 7, 0, 1, 2, 3, 4, 5):
                dve.scalar_tensor_tensor(U[:, c, HIST:HIST + NP], hT[:, c, 0:NP], g_pool[:, c:c + 1],
                                         rstd[:, 0, 0:NP], ALU.mult, ALU.mult).then_inc(S("U"), 1)
                dve.scalar_tensor_tensor(U[:, c, 2 * HIST + NP:UW], hT[:, c, NP:TOK], g_pool[:, c:c + 1],
                                         rstd[:, 0, NP:TOK], ALU.mult, ALU.mult).then_inc(S("U"), 1)
            dve.wait_ge(S("U"), 2 * KC)

            def differences(g, win, w):
                cs = slice(2 * g, 2 * g + 2)
                dve.scalar_tensor_tensor(diff[:, cs, 0:NP], win[:, :, HIST:HIST + NP], 1.0 / w, U[:, cs, HIST:HIST + NP],
                                         ALU.mult, ALU.subtract).then_inc(S("diff_a"), 1)
                dve.scalar_tensor_tensor(diff[:, cs, NP:TOK], win[:, :, 2 * HIST + NP:UW], 1.0 / w,
                                         U[:, cs, 2 * HIST + NP:UW], ALU.mult, ALU.subtract).then_inc(S("diff_a"), 1)
                dve.wait_ge(S("diff_a"), 3 * g + 2)
                dve.tensor_tensor(diff[:, cs, 0:w - 1], win[:, :, HIST:HIST + w - 1],
                                  inv_cnt[:, 0:w - 1].unsqueeze(1).to_broadcast([128, 2, w - 1]), ALU.mult)\
                    .then_inc(S("diff_a"), 1)
                dve.wait_ge(S("diff_a"), 3 * g + 3)
                dve.tensor_tensor(diff[:, cs, 0:w - 1], diff[:, cs, 0:w - 1], U[:, cs, HIST:HIST + w - 1],
                                  ALU.subtract).then_inc(S("diff"), 1)

            then(dve.tensor_tensor(winA[:, 0:6, 1:UW], U[:, 0:6, 1:UW], U[:, 0:6, 0:UW - 1], ALU.add), "win")
            differences(0, winA[:, 0:2], 2)
            then(dve.tensor_tensor(winB[:, 0:4, 3:UW], winA[:, 2:6, 3:UW], winA[:, 2:6, 1:UW - 2], ALU.add), "win")
            differences(1, winB[:, 0:2], 4)
            then(dve.tensor_tensor(winA[:, 4:6, 7:UW], winB[:, 2:4, 7:UW], winB[:, 2:4, 3:UW - 4], ALU.add), "win")
            differences(2, winA[:, 4:6], 8)
            dve.wait_ge(S("win3"), 4)
            differences(3, winB[:, 4:6], 16)

            def ffn_low(f):
                dve.wait_ge(S("ffn_wh"), f + 1)
                dve.tensor_tensor(ffn_part(w_lo, f), ffn_raw(f), ffn_part(w_hi, f).bitcast(F32), ALU.subtract)\
                    .then_inc(S("ffn_wl"), 1)

            for c in range(KC):
                dve.wait_ge(S("pool_mm"), c + 1)
                dve.scalar_tensor_tensor(hT[:, c, :], P[c % 4][:, 0:TOK], p_scale[:, c:c + 1], hT[:, c, :],
                                         ALU.mult, ALU.add).then_inc(S("pooled"), 1)
                if c == 1:
                    ffn_low(0)
            dve.wait_ge(S("pooled"), KC)

            inverse("n1", 1)
            for c in range(KC + 1):
                if c < KC:
                    dve.scalar_tensor_tensor(u32[:, c, :], hT[:, c, :], g_ffn[:, 0, c:c + 1], rstd[:, 1, :],
                                             ALU.mult, ALU.mult).then_inc(S("u32"), 1)
                if c >= 1:
                    dve.wait_ge(S("u_high"), c)
                    dve.tensor_tensor(ul[:, c - 1, :], u32[:, c - 1, :], uh[:, c - 1, :].bitcast(F32), ALU.subtract)\
                        .then_inc(S("u_ffn"), 1)
            dve.wait_ge(S("u_ffn"), KC)
            ffn_low(1)
            ffn_low(2)
            dve.wait_ge(S("state_mm"), 4)

            def dn_low(i):
                dve.wait_ge(S("ffn_wh"), FC + i + 1)
                dve.tensor_tensor(dn_part(w_lo, i), dn_raw(i), dn_part(w_hi, i).bitcast(F32), ALU.subtract)\
                    .then_inc(S("ffn_wl"), 1)

            def hid_low(v):
                dve.wait_ge(S("hid_high"), v + 1)
                dve.tensor_tensor(ul[:, v % 8, :], hidden(v % FC), uh[:, v % 8, :].bitcast(F32), ALU.subtract)\
                    .then_inc(S("hid_low"), 1)

            def ffn_sums(sweep):
                for c in range(4 * sweep, 4 * sweep + 4):
                    dve.wait_ge(S("ffn_sum"), c + 1)
                    dve.tensor_tensor(hT[:, c, :], hT[:, c, :], P[DN_BANKS[c]][:, 0:TOK], ALU.add)\
                        .then_inc(S("ffn_out"), 1)

            for f in range(FC):
                if 3 <= f + 2 < FC:
                    ffn_low(f + 2)
                elif f + 2 >= FC:
                    dn_low(f + 2 - FC)
                dve.wait_ge(S("ffn_sg"), f + 1)
                dve.tensor_tensor(hidden(f), sg[:, f % 2, :], P[2 + 2 * (f % 3)][:, 0:TOK], ALU.mult)\
                    .then_inc(S("ffn_hm"), 1)
            sweeps(2, dn_low, hid_low, ffn_sums)
            dve.wait_ge(S("ffn_out"), KC)
            dve.wait_ge(S("gains_in"), 176)
            then(dve.tensor_scalar(gq8[:, :], gq[:, :], HD ** -0.5, None, ALU.mult), "dve_setup")
            dve.wait_ge(S("n2_rms"), 1)
            dve.reciprocal(r2, rms[:, 0, :]).then_inc(S("n2_rstd"), 1)
            dve.wait_ge(S("n2_rstd"), 1)
            for c in range(KC + 1):
                if c < KC:
                    if c >= 2:
                        dve.wait_ge(S("u_q"), c - 1)
                    dve.scalar_tensor_tensor(t32[:, c % 2, :], hT[:, c, :], g_attn[:, c:c + 1], r2, ALU.mult, ALU.mult)\
                        .then_inc(S("q32"), 1)
                if c >= 1:
                    dve.wait_ge(S("q_high"), c)
                    dve.tensor_tensor(ul[:, c - 1, :], t32[:, (c - 1) % 2, :], uqh[:, c - 1, :].bitcast(F32), ALU.subtract)\
                        .then_inc(S("u_q"), 1)
            dve.wait_ge(S("wf_high"), 1)
            dve.tensor_tensor(wfl[:, :, :], wf[:, :, :], wfh[:, :, :].bitcast(F32), ALU.subtract).then_inc(S("wf_split"), 1)
            dve.wait_ge(S("qz_zero"), 2)
            dve.wait_ge(S("zeros"), 3)

            def head_norm(i):
                c = i % KC
                dve.wait_ge(S("head_rms"), i + 1)
                dve.reciprocal(rstd[:, i % 2, :], rms[:, i % 2, :]).then_inc(S("head_rstd"), 1)
                dve.wait_ge(S("head_rstd"), i + 1)
                r = raw[:, i % 2, :]
                if i < KC:
                    for a in range(2):
                        ps = slice(64 * a, 64 * a + 64)
                        q4 = 32 * (2 * (c % 2) + a)
                        dve.scalar_tensor_tensor(qz[ps, 2 * c + a, :], r[ps, :], gq8[ps, :], rstd[ps, i % 2, :],
                                                 ALU.mult, ALU.mult).then_inc(S("q_a"), 1)
                        m = dve.scalar_tensor_tensor(QS[ps, c, q4:q4 + NS], r[ps, NP:TOK], gq8[ps, :],
                                                     rstd[ps, i % 2, NP:TOK], ALU.mult, ALU.mult)
                    m.then_inc(S("q_ready"), 1)
                    dve.wait_ge(S("q_ready"), c + 1)
                else:
                    dve.scalar_tensor_tensor(kT[:, c, :], r, gk[:, :], rstd[:, i % 2, :], ALU.mult, ALU.mult)\
                        .then_inc(S("k_ready"), 1)
                    dve.wait_ge(S("k_ready"), c + 1)

            def v_rows(c):
                dve.wait_ge(S("vt_mm"), c + 1)
                b = P[6 + c % 2]
                dve.tensor_copy(vtok[:, 0:2, 128 * c:128 * c + 128], b[:, 0:256].rearrange("p (t n) -> p t n", t=2))
                dve.tensor_copy(vtok[0:NS, 2, 128 * c:128 * c + 128], b[0:NS, 256:384]).then_inc(S("v_tok"), 1)

            for i in range(3 * KC):
                for c in kv_chunks(i):
                    if c < 2:
                        dve.wait_ge(S("u_q"), KC)
                    else:
                        dve.wait_ge(S("u_kv"), c - 1)
                    dve.scalar_tensor_tensor(t32[:, c % 2, :], hT[:, c, :], g_kv[:, c:c + 1], r2, ALU.mult, ALU.mult)\
                        .then_inc(S("kv32"), 1)
                if 1 <= i <= 2 * KC:
                    dve.wait_ge(S("raw"), i)
                    head_norm(i - 1)
                for c in kv_chunks(i):
                    dve.wait_ge(S("kv_high"), c + 1)
                    dve.tensor_tensor(kvl[c // 4][:, c % 4, :], t32[:, c % 2, :], uh[:, c, :].bitcast(F32), ALU.subtract)\
                        .then_inc(S("u_kv"), 1)
                if i == KC:
                    dve.wait_ge(S("f_mm"), 1)
                    dve.tensor_scalar(zf, P[7][0:H, 0:TOK], bf[:, :], None, ALU.add).then_inc(S("z_ready"), 1)
                    dve.wait_ge(S("z_ready"), 1)
                    dve.scalar_tensor_tensor(af, zf, -1.0, zf, ALU.mult, ALU.max).then_inc(S("z_ready"), 1)
                if i == 2 * KC + 1:
                    dve.wait_ge(S("f_ln"), 1)
                    dve.scalar_tensor_tensor(lf, zf, 0.0, af, ALU.min, ALU.subtract).then_inc(S("lf_ready"), 1)
                    dve.wait_ge(S("lf_ready"), 1)
                    dve.wait_ge(S("cat_ready"), 1)
                    then(dve.tensor_copy(cat[:, PAST:PAST + NS], lf[:, NP:TOK]), "cum")
                    zero = lambda n: ones[0:H, 0:1].to_broadcast([H, n])
                    then(dve.tensor_tensor_scan(negp[0:H, :], zero(NP), lf[:, 0:NP], 0.0, ALU.mult, ALU.add), "cum")
                    then(dve.tensor_tensor_scan(negs[0:H, :], zero(PAST + NS), cat, 0.0, ALU.mult, ALU.add), "cum")
                    dve.tensor_scalar(negp[0:H, :], negp[0:H, :], -1.0, None, ALU.mult).then_inc(S("neg_ready"), 1)
                    dve.tensor_scalar(negs[0:H, :], negs[0:H, :], -1.0, None, ALU.mult).then_inc(S("neg_ready"), 1)
                if i == 2 * KC + 3:
                    dve.wait_ge(S("lf_mm"), 1)
                    for t in range(3):
                        r = 128 if t < 2 else NS
                        dve.tensor_copy(lo[0:r, t, :], P[1][0:r, H * t:H * t + H]).then_inc(S("logf_tok"), 1)
                if i == 2 * KC + 1:
                    dve.wait_ge(S("v_zero"), 1)
                if i >= 2 * KC + 1:
                    v_rows(i - 2 * KC - 1)
            v_rows(KC - 1)

            def negmax(n):
                nk = 128 * (n % 2 + 1)
                dve.wait_ge(S("s_mm"), n + 1)
                if n >= 3:
                    dve.wait_ge(S("p_exp"), n - 2)
                then(dve.reduce_max(stat[:, 8 + n % 3:9 + n % 3], P[n % 3][:, 0:nk], AX.X), "max_a")
                dve.tensor_scalar(stat[:, n % 3:n % 3 + 1], stat[:, 8 + n % 3:9 + n % 3], -1.0, None, ALU.mult)\
                    .then_inc(S("p_max"), 1)

            def norm_p(n):
                nk = 128 * (n % 2 + 1)
                dve.wait_ge(S("p_exp"), n + 1)
                then(dve.reciprocal(stat[:, 12 + n % 3:13 + n % 3], stat[:, 4 + n % 3:5 + n % 3]), "max_a")
                dve.tensor_scalar(Pp[:, n % 3, 0:nk], Pp[:, n % 3, 0:nk], stat[:, 12 + n % 3:13 + n % 3], None, ALU.mult)\
                    .then_inc(S("p_norm"), 1)

            def copy_pt(n):
                nk = 128 * (n % 2 + 1)
                dve.wait_ge(S("pt_mm"), n + 1)
                if n >= 2:
                    dve.wait_ge(S("pv_mm"), n - 1)
                dve.tensor_copy(PTp[:, n % 2, 0:nk], P[3 + n % 2][:, 0:nk]).then_inc(S("pt_out"), 1)

            def copy_o(c):
                dve.wait_ge(S("pv_mm"), 4 * c + 4)
                for a in range(2):
                    m = dve.tensor_copy(oT[64 * a:64 * a + 64, c, 0:NP], P[5 + c % 2][64 * a:64 * a + 64, NP * a:NP * a + NP])
                m.then_inc(S("o_out"), 1)

            NA = 2 * H
            for n in range(NA + 3):
                if n < NA:
                    negmax(n)
                if 1 <= n <= NA:
                    norm_p(n - 1)
                if 2 <= n < NA + 2:
                    copy_pt(n - 2)
                if n >= 3 and (n - 3) % 4 == 3:
                    copy_o((n - 3) // 4)
            for i in range(2):
                then(dve.memset(Ps[i][:, PAST + NS:640], 0.0), "max_a")

            def s_negmax(j):
                st = 16 + 8 * (j % 2)
                b0, b1 = [(0, 1), (2, 7)][j % 2]
                dve.wait_ge(S("ss_mm"), j + 1)
                if j >= 2:
                    dve.wait_ge(S("ps_exp"), j - 1)
                then(dve.reduce_max(stat[:, st + 3:st + 4], P[b0][:, :], AX.X), "max_a")
                then(dve.reduce_max(stat[:, st + 4:st + 5], P[b1][:, 0:NS], AX.X), "max_a")
                then(dve.tensor_tensor(stat[:, st + 5:st + 6], stat[:, st + 3:st + 4], stat[:, st + 4:st + 5], ALU.max), "max_a")
                dve.tensor_scalar(stat[:, st:st + 1], stat[:, st + 5:st + 6], -1.0, None, ALU.mult).then_inc(S("ps_max"), 1)

            def s_norm(j):
                st = 16 + 8 * (j % 2)
                dve.wait_ge(S("ps_exp"), j + 1)
                then(dve.tensor_tensor(stat[:, st + 6:st + 7], stat[:, st + 1:st + 2], stat[:, st + 2:st + 3], ALU.add), "max_a")
                then(dve.reciprocal(stat[:, st + 7:st + 8], stat[:, st + 6:st + 7]), "max_a")
                dve.tensor_scalar(Ps[j % 2][:, 0:PAST + NS], Ps[j % 2][:, 0:PAST + NS], stat[:, st + 7:st + 8], None, ALU.mult)\
                    .then_inc(S("ps_norm"), 1)

            def s_copy(j):
                dve.wait_ge(S("pts_mm"), j + 1)
                if j >= 1:
                    dve.wait_ge(S("pvs_mm"), j)
                dve.tensor_copy(PTs[:, 0:4, :].rearrange("p t n -> p (t n)"), P[3][:, :])
                dve.tensor_copy(PTs[:, 4, :], P[4][:, 0:128]).then_inc(S("pts_out"), 1)

            def s_out(j):
                dve.wait_ge(S("pvs_mm"), j + 1)
                for a in range(2):
                    c = 2 * j + a
                    for b in range(2):
                        m = dve.tensor_copy(oT[64 * b:64 * b + 64, c, NP:TOK],
                                            P[5][64 * b:64 * b + 64, 64 * a + 32 * b:64 * a + 32 * b + 32])
                m.then_inc(S("os_out"), 1)

            s_negmax(0)
            s_negmax(1)
            s_norm(0)
            for j in range(4):
                s_copy(j)
                if j < 3:
                    s_norm(j + 1)
                if j < 2:
                    s_negmax(j + 2)
                s_out(j)
            then(dve.memset(tv[:, 1, :], 1.0), "route")
            for k in range(KC):
                m = dve.tensor_scalar(wrg[:, k, :], wr[:, k, :], g_ffn[:, 1, k:k + 1], None, ALU.mult)
            m.then_inc(S("wrg_ready"), 1)

            def add_squares(c):
                dve.wait_ge(S("h2_sq"), c + 1)
                if c == 0:
                    dve.sem_inc(S("row_sq"), 1)
                else:
                    dve.wait_ge(S("row_sq"), c)
                    dve.tensor_tensor(sq[:, 0, :], sq[:, 0, :], sq[:, c, :], ALU.add).then_inc(S("row_sq"), 1)

            for d in range(KC):
                dve.wait_ge(S("wo_mm"), d + 1)
                dve.tensor_tensor(hT[:, d, :], hT[:, d, :], P[d % 2][:, 0:TOK], ALU.add).then_inc(S("h2"), 1)
                if d >= 1:
                    add_squares(d - 1)
            add_squares(KC - 1)

            R = "route"
            then(dve.memset(lg[:, :, :], 0.0), R)
            dve.wait_ge(S("row_rms"), 2)
            then(dve.reciprocal(rs_tok[:, :], tv[:, 1, :]), R)
            dve.wait_ge(S("lg_mm"), 1)
            for t in range(3):
                r = 128 if t < 2 else NS
                then(dve.tensor_scalar(lg[0:r, t, :], P[4][0:r, NE * t:NE * t + NE], rs_tok[0:r, t:t + 1], None, ALU.mult), R)
            bc = lambda a: a.unsqueeze(2).to_broadcast([128, 3, NE])

            def largest(src, mask, i):
                then(dve.tensor_reduce(tv[:, i, :], src, AX.X, ALU.max), R)
                then(dve.tensor_tensor(key[:, :, :], src, bc(tv[:, i, :]), ALU.is_equal), R)
                then(dve.tensor_tensor(key[:, :, :], key[:, :, :], desc[:, :, :], ALU.mult), R)
                then(dve.tensor_reduce(tv[:, 7, :], key[:, :, :], AX.X, ALU.max), R)
                then(dve.tensor_tensor(mask, key[:, :, :], bc(tv[:, 7, :]), ALU.is_equal), R)

            largest(lg[:, :, :], m1[:, :, :], 5)
            then(dve.scalar_tensor_tensor(l2[:, :, :], m1[:, :, :], NEG, lg[:, :, :], ALU.mult, ALU.add), R)
            largest(l2[:, :, :], m2[:, :, :], 6)
            then(dve.tensor_tensor(tv[:, 3, :], tv[:, 6, :], tv[:, 5, :], ALU.subtract), R)
            dve.sem_inc(S("top2"), 1)
            bv = bc(valid[:, :])
            then(dve.tensor_tensor(m1[:, :, :], m1[:, :, :], bv, ALU.mult), R)
            then(dve.tensor_tensor(m2[:, :, :], m2[:, :, :], bv, ALU.mult), R)
            dve.tensor_tensor(key[:, :, :], m1[:, :, :], m2[:, :, :], ALU.add).then_inc(S("mask_ready"), 1)
            dve.wait_ge(S("mask_ready"), 1)
            dve.wait_ge(S("e2_ready"), 1)
            then(dve.tensor_scalar(tv[:, 2, :], tv[:, 4, :], 1.0, None, ALU.add), R)
            then(dve.reciprocal(tv[:, 5, :], tv[:, 2, :]), R)
            then(dve.tensor_tensor(tv[:, 6, :], tv[:, 4, :], tv[:, 5, :], ALU.mult), R)
            then(dve.tensor_tensor(m1[:, :, :], m1[:, :, :], bc(tv[:, 5, :]), ALU.mult), R)
            then(dve.tensor_tensor(m2[:, :, :], m2[:, :, :], bc(tv[:, 6, :]), ALU.mult), R)
            ge = gate[:, 0:NE, :].rearrange("p e t -> p t e")
            rk = rank[:, 0:NE, :].rearrange("p e t -> p t e")
            then(dve.memset(rank[:, NE, :], -1.0), R)
            then(dve.memset(gate[:, NE, :], 0.0), R)
            then(dve.tensor_tensor(ge, m1[:, :, :], m2[:, :, :], ALU.add), R)
            dve.wait_ge(S("rank_mm"), 1)
            then(dve.scalar_tensor_tensor(l2[:, :, :], P[7][:, 0:3 * NE].rearrange("p (t e) -> p t e", t=3), 1.0,
                                          key[:, :, :], ALU.add, ALU.mult), R)
            then(dve.tensor_scalar(rk, l2[:, :, :], -1.0, None, ALU.add), R)
            then(dve.reduce_max(most[:, :], P[7][:, 32:32 + NE], AX.X), R)
            dve.tensor_copy(most_i[:, :], most[:, :]).then_inc(S("most_ready"), 1)

            def rows_low(first, want_h):
                dve.wait_ge(S("e_xh"), want_h)
                for c in range(first, first + 4):
                    m = dve.scalar_tensor_tensor(xl[:, c, :], P[5 + first // 4][:, CAP * (c % 4):CAP * (c % 4) + CAP],
                                                 g_ffn[:, 1, c:c + 1], xh[:, c, :].bitcast(F32), ALU.mult, ALU.subtract)
                m.then_inc(S("e_xl"), 1)

            def expert(e, it, p):
                A, XH = it * ITS + (E_AUXP + 2 * (p + 1)), it * 2 + (E_XH + 2 * (p + 1))

                def low(q, uu):
                    dve.wait_ge(S("w_hi"), it * SPLITS + (E_HI + split_no(q, uu)))
                    s, w = EXP_SLOT[uu], 2048 * q
                    dve.tensor_tensor(w_lo[:, buf(q, uu), :], ring[:, s, w:w + 2048], w_hi[:, buf(q, uu), :].bitcast(F32), ALU.subtract)\
                        .then_inc(S("w_lo"), 1)

                def hidden_low(uu):
                    dve.wait_ge(S("e_hth"), it * BLK + (E_HTH + uu + 1))
                    dve.tensor_tensor(hTl[:, uu % 2].rearrange("p f n -> p (f n)"), P[2][:, 0:256],
                                      hTh[:, uu % 2].rearrange("p f n -> p (f n)").bitcast(F32), ALU.subtract)\
                        .then_inc(S("e_htl"), 1)

                for uu in range(BLK):
                    if uu >= 1:
                        hidden_low(uu - 1)
                    if uu == BLK - 1:
                        dispatch_next(e, it, p)
                    if uu < BLK - 1:
                        low(0, uu + 1)
                    if uu == 0:
                        low(1, 1)
                        dve.wait_ge(S("aux_pe"), A + 1)
                        dve.tensor_copy(DgT[:, :], P[7][0:CAP, 0:384]).then_inc(S("aux_dve"), 1)
                    dve.wait_ge(S("e_silu"), it * BLK + (E_SILU + uu + 1))
                    dve.wait_ge(S("e_t"), it * BLK + (E_T + uu - 1))
                    dve.tensor_tensor(hm[:, uu % 2, :], sl[:, uu % 2, :], P[uu % 2][:, 256:512], ALU.mult)\
                        .then_inc(S("e_hm"), 1)
                    if 1 <= uu < BLK - 1:
                        low(1, uu + 1)
                    low(2, uu)
                hidden_low(BLK - 1)
                for i in range(2):
                    rows_low(4 * i, XH + (i + 1))
                for i, bank in enumerate((7, 2, 5, 6, 7, 2)):
                    half, t = i // 3, i % 3
                    r = 128 if t < 2 else NS
                    dve.wait_ge(S("aux_pe"), A + (i + 4))
                    a = acc[0:r, t, 512 * half:512 * half + 512]
                    dve.tensor_tensor(a, a, P[bank][0:r, :], ALU.add).then_inc(S("aux_dve"), 1)

            def first_rows(p):
                for i in range(2):
                    rows_low(4 * i, NE * p * 2 + (E_XH + 2 * p + i + 1))

            def make(e, want_aux, want_cur, wait_read):
                dve.wait_ge(S("aux_pe"), want_aux)
                dve.wait_ge(S("dispatch"), wait_read)
                dve.tensor_copy(cur[:, 0:3], rank[:, bass.ds(e, 1), :].rearrange("p a t -> p (a t)")).then_inc(S("cur"), 1)
                dve.tensor_copy(cur[:, 3:6], gate[:, bass.ds(e, 1), :].rearrange("p a t -> p (a t)")).then_inc(S("cur"), 1)
                dve.wait_ge(S("cur"), want_cur)
                for t in range(3):
                    dve.tensor_scalar(Dg[:, t, :], slots_iota[:, :], cur[:, t:t + 1], cur[:, 3 + t:4 + t],
                                      ALU.is_equal, ALU.mult)
                for t in range(3):
                    m = dve.tensor_scalar(Dx[:, t, :], slots_iota[:, :], cur[:, t:t + 1], rs_tok[:, t:t + 1],
                                          ALU.is_equal, ALU.mult)
                m.then_inc(S("dispatch"), 1)

            def dispatch_next(e, it, p):
                make(e + 1, it * ITS + (E_AUXP + 2 * (p + 1) + 1), it * 2 + (4 + 2 * p), it + (E_D + 1 + p))

            dve.wait_ge(S("ht_mm"), 6)
            make(0, E_AUXP, 2, E_D)
            first_rows(0)
            dve.wait_ge(S("acc_init"), 3)
            with dve.Fori(0, NE) as e:
                expert(e, e, 0)
            n = dve.value_load(most_i[0:1, 0:1], min_val=0, max_val=TOK)
            for p in range(1, PASSES):
                with dve.If(n > p * CAP):
                    dve.wait_ge(S("cur"), 18 * p)
                    dve.tensor_scalar(rank[:, :, :], rank[:, :, :], -float(CAP), None, ALU.add).then_inc(S("pass"), 1)
                    dve.wait_ge(S("pass"), p)
                    make(0, NE * p * ITS + (E_AUXP + 2 * p), 18 * p + 2, NE * p + (E_D + p))
                    first_rows(p)
                    with dve.Fori(0, NE) as e:
                        expert(e, e + p * NE, p)
            dve.drain().then_inc(S("acc_done"), 1)

        assert len(sems) < 200, len(sems)


_INS = ["x_prompt", "x_sample", "state_pool", "cache_k", "cache_v", "cache_logf", "g_pool_norm", "w_pool",
        "pool_scale", "g_kv_norm", "w_kvf", "b_f", "g_k", "g_attn_norm", "w_q", "g_q", "w_o", "g_ffn_norm",
        "w_ffn_gu", "w_ffn_down", "w_router", "w_moe_gu", "w_moe_down"]
_OUTS = [("y_prompt", (1, 256, 1024)), ("y_sample", (1, 32, 1024)), ("state_prompt", (1, 1, 15, 1024)),
         ("k_prompt", (1, 256, 16, 64)), ("v_prompt", (1, 256, 16, 64)), ("logf_prompt", (1, 256, 16)),
         ("state_sample", (1, 1, 15, 1024)), ("k_sample", (1, 32, 16, 64)), ("v_sample", (1, 32, 16, 64)),
         ("logf_sample", (1, 32, 16))]


def kernel(**inputs):
    import numpy as _np
    import concourse.bacc as _bacc
    from concourse import mybir as _mybir
    from concourse.bass_utils import run_bass_kernel_spmd as _run

    nc = _bacc.Bacc("TRN2", target_bir_lowering=False, num_devices=1, dynamic_dma_scratch_size=4096)
    arrays, ins, outs = {}, {}, {}
    for name in _INS:
        a = _np.ascontiguousarray(inputs[name])
        arrays[f"in_{name}"] = a
        ins[name] = nc.dram_tensor(f"in_{name}", a.shape, _mybir.dt.from_np(a.dtype), kind="ExternalInput").ap()
    for name, shape in _OUTS:
        outs[name] = nc.dram_tensor(f"out_{name}", shape, _mybir.dt.float32, kind="ExternalOutput").ap()
    build_program(nc, ins, outs)
    r = _run(nc, [arrays], core_ids=[0])
    return tuple(r.results[0][f"out_{name}"] for name, _ in _OUTS)
```
